# Optimizing a Trainium2 kernel written in Bass

```python
import math
import jax, jax.numpy as jnp
from jax import lax
import numpy as np

D_MODEL = 1024
BATCH = 1
SEQ = 256
DEPTH = 2

CHUNK = 64
N_MIXERS = 2
N_LAYERS_A = (DEPTH + 1) // 2
N_LAYERS_B = DEPTH // 2

A_HEADS = 8
A_HEAD_DIM = 64
A_V_DIM = 2 * A_HEAD_DIM
Q_BLOCK = 128
T5_BUCKETS = 32
T5_MAX_DIST = 1024

B_HEADS = 16
B_HEAD_DIM = D_MODEL // B_HEADS
LEFT_CHUNKS = 8
BAND = (LEFT_CHUNKS + 1) * CHUNK
MAX_REL = 256

N_EXPERTS = 16
N_GROUPS = 4
E_PER_GROUP = N_EXPERTS // N_GROUPS
TOPK_GROUPS = 1
TOP_K = 2
D_FF_EXPERT = 512

NORM_EPS = 1e-6
NEG_INF = -1e30


def rms_norm(x, g):
    xf = x.astype(jnp.float32)
    y = xf * lax.rsqrt(jnp.mean(xf * xf, axis=-1, keepdims=True) + NORM_EPS)
    return (y * g.astype(jnp.float32)).astype(x.dtype)

def t5_bucket(rel):
    nb = T5_BUCKETS // 2
    ret = jnp.where(rel > 0, nb, 0)
    n = jnp.abs(rel)
    max_exact = nb // 2
    nf = jnp.maximum(n, 1).astype(jnp.float32)
    large = max_exact + (jnp.log(nf / max_exact) / math.log(T5_MAX_DIST / max_exact)
                         * (nb - max_exact)).astype(jnp.int32)
    large = jnp.minimum(large, nb - 1)
    return ret + jnp.where(n < max_exact, n, large)

def diff_attention(h, w_qkv, q_gain, k_gain, lam, subln_g, w_o, t5_bias, lambda_init):
    B, S, D = h.shape
    qkv = h @ w_qkv
    q, k, v = jnp.split(qkv, 3, axis=-1)
    q = q.reshape(B, S, A_HEADS, 2, A_HEAD_DIM)
    k = k.reshape(B, S, A_HEADS, 2, A_HEAD_DIM)
    v = v.reshape(B, S, A_HEADS, A_V_DIM)
    q = rms_norm(q, q_gain) * (A_HEAD_DIM ** -0.5)
    k = rms_norm(k, k_gain)
    lamf = lam.astype(jnp.float32)
    lam_full = (jnp.exp(jnp.sum(lamf[0] * lamf[1])) - jnp.exp(jnp.sum(lamf[2] * lamf[3]))
                + lambda_init)
    n_blocks = S // Q_BLOCK
    q_blocks = q.reshape(B, n_blocks, Q_BLOCK, A_HEADS, 2, A_HEAD_DIM).transpose(1, 0, 2, 3, 4, 5)
    k_pos = jnp.arange(S, dtype=jnp.int32)

    def one_block(args):
        qb, blk = args
        q_pos = blk * Q_BLOCK + jnp.arange(Q_BLOCK, dtype=jnp.int32)
        rel = k_pos[None, :] - q_pos[:, None]
        bias = t5_bias.astype(jnp.float32)[t5_bucket(rel)].transpose(2, 0, 1)
        allowed = (k_pos[None, :] // CHUNK) <= (q_pos[:, None] // CHUNK)
        s = jnp.einsum('bqhmd,bkhmd->bmhqk', qb, k).astype(jnp.float32) + bias[None, None]
        s = jnp.where(allowed[None, None, None], s, NEG_INF)
        p = jax.nn.softmax(s, axis=-1)
        a = p[:, 0] - lam_full * p[:, 1]
        return jnp.einsum('bhqk,bkhe->bqhe', a.astype(v.dtype), v)

    o = lax.map(one_block, (q_blocks, jnp.arange(n_blocks, dtype=jnp.int32)))
    o = o.transpose(1, 0, 2, 3, 4).reshape(B, S, A_HEADS, A_V_DIM)
    o = rms_norm(o, subln_g) * (1.0 - lambda_init)
    return o.reshape(B, S, D) @ w_o

def chunked_attention(h, w_qkv, q_gain, k_gain, rel_bias, w_o):
    B, S, D = h.shape
    NC = S // CHUNK
    qkv = h @ w_qkv
    q, k, v = jnp.split(qkv, 3, axis=-1)
    q = rms_norm(q.reshape(B, S, B_HEADS, B_HEAD_DIM), q_gain) * (B_HEAD_DIM ** -0.5)
    k = rms_norm(k.reshape(B, S, B_HEADS, B_HEAD_DIM), k_gain)
    v = v.reshape(B, S, B_HEADS, B_HEAD_DIM)
    pad = ((0, 0), (LEFT_CHUNKS * CHUNK, 0), (0, 0), (0, 0))
    kp = jnp.pad(k, pad)
    vp = jnp.pad(v, pad)
    qi = jnp.arange(CHUNK, dtype=jnp.int32)
    kb = jnp.arange(BAND, dtype=jnp.int32)
    rel = kb[None, :] - LEFT_CHUNKS * CHUNK - qi[:, None]
    idx = jnp.clip(rel, -MAX_REL, MAX_REL) + MAX_REL
    bias = rel_bias.astype(jnp.float32)[:, idx]
    band_chunk = kb // CHUNK
    q_chunks = q.reshape(B, NC, CHUNK, B_HEADS, B_HEAD_DIM).transpose(1, 0, 2, 3, 4)

    def one_chunk(args):
        qc, ci = args
        kband = lax.dynamic_slice_in_dim(kp, ci * CHUNK, BAND, axis=1)
        vband = lax.dynamic_slice_in_dim(vp, ci * CHUNK, BAND, axis=1)
        valid = (ci - LEFT_CHUNKS + band_chunk) >= 0
        s = jnp.einsum('bqhd,bkhd->bhqk', qc, kband).astype(jnp.float32) + bias[None]
        s = jnp.where(valid[None, None, None, :], s, NEG_INF)
        p = jax.nn.softmax(s, axis=-1)
        return jnp.einsum('bhqk,bkhd->bqhd', p.astype(vband.dtype), vband)

    o = lax.map(one_chunk, (q_chunks, jnp.arange(NC, dtype=jnp.int32)))
    o = o.transpose(1, 0, 2, 3, 4).reshape(B, S, D)
    return o @ w_o

def grouped_moe(h, router_w, router_bias, w_gate, w_up, w_down):
    B, S, D = h.shape
    t = h.reshape(B * S, D)
    scores = jax.nn.sigmoid((t @ router_w).astype(jnp.float32))
    sel = scores + router_bias.astype(jnp.float32)
    grp = sel.reshape(-1, N_GROUPS, E_PER_GROUP)
    group_score = lax.top_k(grp, TOP_K)[0].sum(-1)
    _, g_idx = lax.top_k(group_score, TOPK_GROUPS)
    group_mask = jax.nn.one_hot(g_idx, N_GROUPS, dtype=jnp.float32).sum(1) > 0
    expert_mask = jnp.repeat(group_mask, E_PER_GROUP, axis=1)
    masked = jnp.where(expert_mask, sel, NEG_INF)
    _, e_idx = lax.top_k(masked, TOP_K)
    w = jnp.take_along_axis(scores, e_idx, axis=1)
    w = w / jnp.sum(w, axis=-1, keepdims=True)
    gates = jnp.sum(jax.nn.one_hot(e_idx, N_EXPERTS, dtype=jnp.float32) * w[..., None], axis=1)
    gates = gates.astype(t.dtype)
    out = jnp.zeros_like(t)
    for e in range(N_EXPERTS):
        he = jax.nn.silu(t @ w_gate[e]) * (t @ w_up[e])
        out = out + gates[:, e:e + 1] * (he @ w_down[e])
    return out.reshape(B, S, D)

def first_inputs(seed: int = 0) -> dict:
    key = jax.random.key(seed)
    ks = jax.random.split(key, 24)
    D, F, E = D_MODEL, D_FF_EXPERT, N_EXPERTS
    nrm = lambda k, shape, s: jax.random.normal(k, shape, jnp.float32) * s
    gain = lambda k, shape: 1.0 + 0.02 * jax.random.normal(k, shape, jnp.float32)
    return {
        "x": nrm(ks[0], (BATCH, SEQ, D), 1.0),
        "c": nrm(ks[1], (BATCH, D), 1.0),
        "ada_w": nrm(ks[2], (DEPTH, D, 6 * D), 0.5 * D ** -0.5),
        "ada_b": nrm(ks[3], (DEPTH, 6 * D), 0.01),
        "norm_mix_g": gain(ks[4], (DEPTH, D)),
        "norm_ffn_g": gain(ks[5], (DEPTH, D)),
        "t5_bias": nrm(ks[6], (T5_BUCKETS, A_HEADS), 0.2),
        "a_w_qkv": nrm(ks[7], (N_LAYERS_A, D, 3 * D), D ** -0.5),
        "a_q_gain": gain(ks[8], (N_LAYERS_A, A_HEAD_DIM)),
        "a_k_gain": gain(ks[9], (N_LAYERS_A, A_HEAD_DIM)),
        "a_lambda": nrm(ks[10], (N_LAYERS_A, 4, A_HEAD_DIM), 0.1),
        "a_subln_g": gain(ks[11], (N_LAYERS_A, A_V_DIM)),
        "a_w_o": nrm(ks[12], (N_LAYERS_A, D, D), D ** -0.5),
        "b_w_qkv": nrm(ks[13], (N_LAYERS_B, D, 3 * D), D ** -0.5),
        "b_q_gain": gain(ks[14], (N_LAYERS_B, B_HEAD_DIM)),
        "b_k_gain": gain(ks[15], (N_LAYERS_B, B_HEAD_DIM)),
        "b_rel_bias": nrm(ks[16], (N_LAYERS_B, B_HEADS, 2 * MAX_REL + 1), 0.2),
        "b_w_o": nrm(ks[17], (N_LAYERS_B, D, D), D ** -0.5),
        "router_w": nrm(ks[18], (D, E), D ** -0.5),
        "router_bias": nrm(ks[19], (E,), 0.01),
        "moe_w_gate": nrm(ks[20], (DEPTH, E, D, F), D ** -0.5),
        "moe_w_up": nrm(ks[21], (DEPTH, E, D, F), D ** -0.5),
        "moe_w_down": nrm(ks[22], (DEPTH, E, F, D), F ** -0.5),
    }

def first_block(x, c, ada_w, ada_b, norm_mix_g, norm_ffn_g, t5_bias,
              a_w_qkv, a_q_gain, a_k_gain, a_lambda, a_subln_g, a_w_o,
              b_w_qkv, b_q_gain, b_k_gain, b_rel_bias, b_w_o,
              router_w, router_bias, moe_w_gate, moe_w_up, moe_w_down):
    silu_c = jax.nn.silu(c)
    for i in range(DEPTH):
        mod = silu_c @ ada_w[i] + ada_b[i]
        sh1, sc1, g1, sh2, sc2, g2 = [m[:, None, :] for m in jnp.split(mod, 6, axis=-1)]
        h = rms_norm(x, norm_mix_g[i]) * (1.0 + sc1) + sh1
        if i % N_MIXERS == 0:
            j = i // N_MIXERS
            lambda_init = 0.8 - 0.6 * math.exp(-0.3 * i)
            y = diff_attention(h, a_w_qkv[j], a_q_gain[j], a_k_gain[j], a_lambda[j],
                               a_subln_g[j], a_w_o[j], t5_bias, lambda_init)
        else:
            j = i // N_MIXERS
            y = chunked_attention(h, b_w_qkv[j], b_q_gain[j], b_k_gain[j], b_rel_bias[j], b_w_o[j])
        x = x + g1 * y
        h = rms_norm(x, norm_ffn_g[i]) * (1.0 + sc2) + sh2
        x = x + g2 * grouped_moe(h, router_w, router_bias, moe_w_gate[i], moe_w_up[i], moe_w_down[i])
    return x


DEPTH_2 = 1

GRID_W = 64
CTX_LEN = 256
HEAD_DIM = 64
EPS = 1e-6
A_WIDTH = D_MODEL // 4
A_HEADS_2 = A_WIDTH // HEAD_DIM
A_CHUNK = 128
B_WIDTH = D_MODEL // 2
B_HEADS_2 = B_WIDTH // HEAD_DIM
B_KV_HEADS = 2
B_GROUP = B_HEADS_2 // B_KV_HEADS
B_KV_WIDTH = B_KV_HEADS * HEAD_DIM
ROPE_AXIS_DIM = HEAD_DIM // 2
ROPE_BASE = 10000.0
C_WIDTH = D_MODEL // 4
C_HEADS = C_WIDTH // HEAD_DIM
C_CHUNK = 64
MIX_WIDTH = A_WIDTH + B_WIDTH + C_WIDTH
OFF_B = 2 * A_WIDTH
OFF_KV = OFF_B + B_WIDTH
OFF_C = OFF_KV + 2 * B_KV_WIDTH
OFF_G = OFF_C + 4 * C_WIDTH
IN_WIDTH = OFF_G + C_WIDTH
EXPERTS_PER_GROUP = 8
N_EXPERTS_2 = N_GROUPS * EXPERTS_PER_GROUP
D_FF_EXPERT_2 = D_MODEL // 2
MOE_BLOCK = 128


def _rms(x):
    xf = x.astype(jnp.float32)
    return (xf * lax.rsqrt(jnp.mean(xf * xf, axis=-1, keepdims=True) + EPS)).astype(x.dtype)

def axial_rope_tables(rows):
    row = jnp.repeat(jnp.arange(rows), GRID_W).astype(jnp.float32)
    col = jnp.tile(jnp.arange(GRID_W), rows).astype(jnp.float32)
    inv_freq = 1.0 / (ROPE_BASE ** (jnp.arange(0, ROPE_AXIS_DIM, 2, dtype=jnp.float32) / ROPE_AXIS_DIM))
    ang = jnp.stack([row[:, None] * inv_freq, col[:, None] * inv_freq], axis=1)
    return jnp.cos(ang)[:, None, :, None, :], jnp.sin(ang)[:, None, :, None, :]

def apply_rope(x, cos, sin):
    b, t, h, _ = x.shape
    xr = x.astype(jnp.float32).reshape(b, t, h, 2, 2, ROPE_AXIS_DIM // 2)
    rot = jnp.stack([-xr[..., 1, :], xr[..., 0, :]], axis=-2)
    return (xr * cos + rot * sin).reshape(b, t, h, HEAD_DIM).astype(x.dtype)

def chunk_mlp(z, w_s, b_s):
    b, t, _ = z.shape
    u, v = jnp.split(jax.nn.gelu(z), 2, axis=-1)
    v = _rms(v.reshape(b, t // A_CHUNK, A_CHUNK, A_HEADS_2, HEAD_DIM))
    mixed = jnp.einsum('hts,bnshd->bnthd', w_s, v) + b_s.T[:, :, None]
    return u * mixed.reshape(b, t, A_WIDTH)

def _gqa(q, k, v):
    s = jnp.einsum('bqkgd,bskd->bkgqs', q, k).astype(jnp.float32) * (HEAD_DIM ** -0.5)
    p = jax.nn.softmax(s, axis=-1).astype(v.dtype)
    return jnp.einsum('bkgqs,bskd->bqkgd', p, v)

def latent_attention(q, k, v, kc, vc):
    b, t, _, _ = q.shape
    keys = jnp.concatenate([k, kc], axis=1)
    vals = jnp.concatenate([v, vc], axis=1)
    qb = q.reshape(b, t // Q_BLOCK, Q_BLOCK, B_KV_HEADS, B_GROUP, HEAD_DIM).transpose(1, 0, 2, 3, 4, 5)
    out = lax.map(lambda qblk: _gqa(qblk, keys, vals), qb)
    return out.transpose(1, 0, 2, 3, 4, 5).reshape(b, t, B_WIDTH)

def forget_gate(zf, lb):
    zf32 = zf.astype(jnp.float32)
    lbh = lb.reshape(C_HEADS, HEAD_DIM)
    pos = lbh > 0.0
    log_lb = jnp.log(jnp.where(pos, lbh, 1.0))
    log_rest = jnp.log1p(-lbh) + jax.nn.log_sigmoid(zf32)
    log_f = jnp.where(pos, jnp.logaddexp(log_lb, log_rest), log_rest)
    k = (1.0 - lbh) * jax.nn.sigmoid(-zf32)
    return k, log_f

def hgrn_inputs(z, lb):
    b, t, _ = z.shape
    q, zf, zb, v = [a.reshape(b, t, C_HEADS, HEAD_DIM) for a in jnp.split(z, 4, axis=-1)]
    kf, logf_f = forget_gate(zf, lb[0])
    kb, logf_b = forget_gate(zb, lb[1])
    return jax.nn.silu(q), v, kf, logf_f, kb, logf_b

def hgrn_scan(q, k, v, log_f, s0, with_output):
    b, t, h, _ = q.shape
    nc = t // C_CHUNK

    def chunks(a):
        return a.astype(jnp.float32).reshape(b, nc, C_CHUNK, h, a.shape[-1]).transpose(1, 0, 3, 2, 4)

    qc, kc, vc = chunks(q), chunks(k), chunks(v)
    bc = jnp.cumsum(chunks(log_f), axis=3)
    tri = jnp.tril(jnp.ones((C_CHUNK, C_CHUNK), bool))[:, :, None]

    def step(s, inp):
        qi, ki, vi, bi = inp
        b_last = bi[:, :, -1:, :]
        s_new = jnp.exp(b_last[:, :, 0, :, None]) * s + jnp.einsum('bhsk,bhsv->bhkv', ki * jnp.exp(b_last - bi), vi)
        if not with_output:
            return s_new, None
        diff = bi[:, :, :, None, :] - bi[:, :, None, :, :]
        decay = jnp.where(tri, jnp.exp(jnp.where(tri, diff, 0.0)), 0.0)
        scores = jnp.einsum('bhtk,bhsk,bhtsk->bhts', qi, ki, decay)
        o = jnp.einsum('bhts,bhsv->bhtv', scores, vi) + jnp.einsum('bhtk,bhkv->bhtv', qi * jnp.exp(bi), s)
        return s_new, o

    s_fin, o = lax.scan(step, s0, (qc, kc, vc, bc))
    if with_output:
        o = o.transpose(1, 0, 3, 2, 4).reshape(b, t, h, v.shape[-1])
    return s_fin, o

def hgrn_bidir(z, zc, lb, ctx_out):
    q, v, kf, lf, kb, lbw = hgrn_inputs(z, lb)
    qc, vc, kfc, lfc, kbc, lbc = hgrn_inputs(zc, lb)
    s0 = jnp.zeros((z.shape[0], C_HEADS, HEAD_DIM, HEAD_DIM), jnp.float32)
    rev = lambda a: a[:, ::-1]
    sf, of_c = hgrn_scan(qc, kfc, vc, lfc, s0, ctx_out)
    _, of = hgrn_scan(q, kf, v, lf, sf, True)
    sb, ob_c = hgrn_scan(rev(qc), rev(kbc), rev(vc), rev(lbc), s0, ctx_out)
    _, ob = hgrn_scan(rev(q), rev(kb), rev(v), rev(lbw), sb, True)
    o = of + rev(ob)
    o_c = of_c + rev(ob_c) if ctx_out else None
    return o, o_c

def hgrn_out(o, g, w):
    b, t = g.shape[:2]
    return (_rms(o) * w).reshape(b, t, C_WIDTH).astype(g.dtype) * jax.nn.silu(g)

def hier_moe(h, w_grp, b_grp, w_exp, b_exp, w1, w3, w2):
    n_tok, d = h.shape
    g_logits = (h @ w_grp + b_grp).astype(jnp.float32)
    grp = jnp.argmax(g_logits, axis=-1)
    p_grp = jnp.take_along_axis(jax.nn.softmax(g_logits, axis=-1), grp[:, None], axis=-1)
    e_logits = (h @ w_exp + b_exp).astype(jnp.float32).reshape(n_tok, N_GROUPS, EXPERTS_PER_GROUP)
    e_in = jnp.take_along_axis(e_logits, grp[:, None, None], axis=1)[:, 0]
    top_val, top_idx = lax.top_k(e_in, TOP_K)
    gate = (jax.nn.softmax(top_val, axis=-1) * p_grp).reshape(-1)
    expert = (grp[:, None] * EXPERTS_PER_GROUP + top_idx).reshape(-1)
    tok = jnp.repeat(jnp.arange(n_tok), TOP_K)
    n_asg = n_tok * TOP_K
    order = jnp.argsort(expert)
    e_sorted, tok_sorted, gate_sorted = expert[order], tok[order], gate[order]
    counts = jax.ops.segment_sum(jnp.ones_like(expert), expert, num_segments=N_EXPERTS_2)
    padded = (counts + MOE_BLOCK - 1) // MOE_BLOCK * MOE_BLOCK
    starts = jnp.cumsum(counts) - counts
    pad_ends = jnp.cumsum(padded)
    pad_starts = pad_ends - padded
    dest = pad_starts[e_sorted] + jnp.arange(n_asg) - starts[e_sorted]
    n_blocks = -(-n_asg // MOE_BLOCK) + N_EXPERTS_2
    buf = jnp.zeros((n_blocks * MOE_BLOCK, d), h.dtype).at[dest].set(h[tok_sorted])
    blk_expert = jnp.minimum(jnp.searchsorted(pad_ends, jnp.arange(n_blocks) * MOE_BLOCK, side='right'), N_EXPERTS_2 - 1)

    def expert_block(args):
        xb, e = args
        return (jax.nn.silu(xb @ w1[e]) * (xb @ w3[e])) @ w2[e]

    out = lax.map(expert_block, (buf.reshape(n_blocks, MOE_BLOCK, d), blk_expert)).reshape(-1, d)
    y = jax.ops.segment_sum(out[dest] * gate_sorted[:, None], tok_sorted, num_segments=n_tok)
    return y.astype(h.dtype)

def hybrid_layer(x, xc, c, c_ctx, cos, sin, lb, w_mod, b_mod, norm1_w, w_in, w_s, b_s, q_norm_w, k_norm_w,
                 hgrn_norm_w, w_out, norm2_w, w_grp, b_grp, w_exp, b_exp, w1, w3, w2, ctx_out):
    b, t, d = x.shape
    lc = xc.shape[1]
    sh1, sc1, g1, sh2, sc2, g2 = jnp.split((jax.nn.silu(c) @ w_mod + b_mod)[:, None, :], 6, axis=-1)
    n_mod = 6 if ctx_out else 2
    mod_c = jnp.split(jax.nn.silu(c_ctx) @ w_mod[:, :n_mod * d] + b_mod[:n_mod * d], n_mod)
    h = _rms(x) * norm1_w * (1.0 + sc1) + sh1
    hc = _rms(xc) * norm1_w * (1.0 + mod_c[1]) + mod_c[0]
    p = h @ w_in
    pc = hc @ w_in[:, OFF_KV:OFF_G]
    ya = chunk_mlp(p[..., :OFF_B], w_s, b_s)
    q = apply_rope(_rms(p[..., OFF_B:OFF_KV].reshape(b, t, B_HEADS_2, HEAD_DIM)) * q_norm_w, cos, sin)
    k, v = jnp.split(p[..., OFF_KV:OFF_C].reshape(b, t, 2 * B_KV_HEADS, HEAD_DIM), 2, axis=2)
    k = apply_rope(_rms(k) * k_norm_w, cos, sin)
    kc, vc = jnp.split(pc[..., :2 * B_KV_WIDTH].reshape(b, lc, 2 * B_KV_HEADS, HEAD_DIM), 2, axis=2)
    kc = _rms(kc) * k_norm_w
    yb = latent_attention(q, k, v, kc, vc)
    o, o_c = hgrn_bidir(p[..., OFF_C:OFF_G], pc[..., 2 * B_KV_WIDTH:], lb, ctx_out)
    yc = hgrn_out(o, p[..., OFF_G:], hgrn_norm_w)
    x = x + g1 * (jnp.concatenate([ya, yb, yc], axis=-1) @ w_out)
    h2 = _rms(x) * norm2_w * (1.0 + sc2) + sh2
    if ctx_out:
        pc_rest = hc @ w_in[:, :OFF_KV]
        pc_g = hc @ w_in[:, OFF_G:]
        ya_c = chunk_mlp(pc_rest[..., :OFF_B], w_s, b_s)
        qc = _rms(pc_rest[..., OFF_B:].reshape(b, lc, B_HEADS_2, HEAD_DIM)) * q_norm_w
        yb_c = _gqa(qc.reshape(b, lc, B_KV_HEADS, B_GROUP, HEAD_DIM), kc, vc).reshape(b, lc, B_WIDTH)
        yc_c = hgrn_out(o_c, pc_g, hgrn_norm_w)
        xc = xc + mod_c[2] * (jnp.concatenate([ya_c, yb_c, yc_c], axis=-1) @ w_out)
        h2c = _rms(xc) * norm2_w * (1.0 + mod_c[4]) + mod_c[3]
        tokens = jnp.concatenate([h2.reshape(-1, d), h2c.reshape(-1, d)], axis=0)
        m = hier_moe(tokens, w_grp, b_grp, w_exp, b_exp, w1, w3, w2)
        x = x + g2 * m[:b * t].reshape(b, t, d)
        xc = xc + mod_c[5] * m[b * t:].reshape(b, lc, d)
    else:
        x = x + g2 * hier_moe(h2.reshape(-1, d), w_grp, b_grp, w_exp, b_exp, w1, w3, w2).reshape(b, t, d)
    return x, xc

def second_inputs(seed: int = 0) -> dict:
    key = jax.random.key(seed)
    ks = jax.random.split(key, 24)
    nrm = lambda k, shape, scale: jax.random.normal(k, shape, jnp.float32) * scale
    return {
        'x': nrm(ks[0], (BATCH, SEQ, D_MODEL), 1.0),
        'c': nrm(ks[1], (BATCH, D_MODEL), 1.0),
        'ctx': nrm(ks[2], (BATCH, CTX_LEN, D_MODEL), 1.0),
        'c_ctx': nrm(ks[3], (D_MODEL,), 1.0),
        'w_mod': nrm(ks[4], (DEPTH_2, D_MODEL, 6 * D_MODEL), 0.5 * D_MODEL ** -0.5),
        'b_mod': nrm(ks[5], (DEPTH_2, 6 * D_MODEL), 0.02),
        'norm1_w': 1.0 + nrm(ks[6], (DEPTH_2, D_MODEL), 0.02),
        'w_in': nrm(ks[7], (DEPTH_2, D_MODEL, IN_WIDTH), D_MODEL ** -0.5),
        'w_s': nrm(ks[8], (DEPTH_2, A_HEADS_2, A_CHUNK, A_CHUNK), A_CHUNK ** -0.5),
        'b_s': 1.0 + nrm(ks[9], (DEPTH_2, A_HEADS_2, A_CHUNK), 0.02),
        'q_norm_w': 1.0 + nrm(ks[10], (DEPTH_2, HEAD_DIM), 0.02),
        'k_norm_w': 1.0 + nrm(ks[11], (DEPTH_2, HEAD_DIM), 0.02),
        'hgrn_lb_logits': nrm(ks[12], (DEPTH_2, 2, C_WIDTH), 1.0),
        'hgrn_norm_w': 1.0 + nrm(ks[13], (DEPTH_2, HEAD_DIM), 0.02),
        'w_out': nrm(ks[14], (DEPTH_2, MIX_WIDTH, D_MODEL), MIX_WIDTH ** -0.5),
        'norm2_w': 1.0 + nrm(ks[15], (DEPTH_2, D_MODEL), 0.02),
        'w_grp': nrm(ks[16], (DEPTH_2, D_MODEL, N_GROUPS), D_MODEL ** -0.5),
        'b_grp': nrm(ks[17], (DEPTH_2, N_GROUPS), 0.01),
        'w_exp': nrm(ks[18], (DEPTH_2, D_MODEL, N_EXPERTS_2), D_MODEL ** -0.5),
        'b_exp': nrm(ks[19], (DEPTH_2, N_EXPERTS_2), 0.01),
        'w1': nrm(ks[20], (DEPTH_2, N_EXPERTS_2, D_MODEL, D_FF_EXPERT_2), D_MODEL ** -0.5),
        'w3': nrm(ks[21], (DEPTH_2, N_EXPERTS_2, D_MODEL, D_FF_EXPERT_2), D_MODEL ** -0.5),
        'w2': nrm(ks[22], (DEPTH_2, N_EXPERTS_2, D_FF_EXPERT_2, D_MODEL), D_FF_EXPERT_2 ** -0.5),
    }

def second_block(x, c, ctx, c_ctx, w_mod, b_mod, norm1_w, w_in, w_s, b_s, q_norm_w, k_norm_w, hgrn_lb_logits,
              hgrn_norm_w, w_out, norm2_w, w_grp, b_grp, w_exp, b_exp, w1, w3, w2):
    ROWS = x.shape[1] // GRID_W
    cos, sin = axial_rope_tables(ROWS)
    lb_sm = jax.nn.softmax(hgrn_lb_logits.astype(jnp.float32), axis=0)
    lb = jnp.cumsum(lb_sm, axis=0) - lb_sm[0]
    xc = ctx
    for l in range(DEPTH_2):
        x, xc = hybrid_layer(x, xc, c, c_ctx, cos, sin, lb[l], w_mod[l], b_mod[l], norm1_w[l], w_in[l], w_s[l],
                             b_s[l], q_norm_w[l], k_norm_w[l], hgrn_norm_w[l], w_out[l], norm2_w[l], w_grp[l],
                             b_grp[l], w_exp[l], b_exp[l], w1[l], w3[l], w2[l], ctx_out=(l < DEPTH_2 - 1))
    return x


def setup_inputs(seed=0):
    out = dict(first_inputs(seed))
    for name, value in second_inputs(seed + 1).items():
        if name != "x":
            out[name + "_2"] = value
    return out


def reference(
    x, c, ada_w, ada_b, norm_mix_g, norm_ffn_g, t5_bias, a_w_qkv, a_q_gain, a_k_gain, a_lambda,
    a_subln_g, a_w_o, b_w_qkv, b_q_gain, b_k_gain, b_rel_bias, b_w_o, router_w, router_bias,
    moe_w_gate, moe_w_up, moe_w_down, c_2, ctx_2, c_ctx_2, w_mod_2, b_mod_2, norm1_w_2, w_in_2,
    w_s_2, b_s_2, q_norm_w_2, k_norm_w_2, hgrn_lb_logits_2, hgrn_norm_w_2, w_out_2, norm2_w_2,
    w_grp_2, b_grp_2, w_exp_2, b_exp_2, w1_2, w3_2, w2_2,
):
    x = first_block(
        x, c, ada_w, ada_b, norm_mix_g, norm_ffn_g, t5_bias, a_w_qkv, a_q_gain, a_k_gain,
        a_lambda, a_subln_g, a_w_o, b_w_qkv, b_q_gain, b_k_gain, b_rel_bias, b_w_o, router_w,
        router_bias, moe_w_gate, moe_w_up, moe_w_down,
    )
    return second_block(
        x, c_2, ctx_2, c_ctx_2, w_mod_2, b_mod_2, norm1_w_2, w_in_2, w_s_2, b_s_2, q_norm_w_2,
        k_norm_w_2, hgrn_lb_logits_2, hgrn_norm_w_2, w_out_2, norm2_w_2, w_grp_2, b_grp_2,
        w_exp_2, b_exp_2, w1_2, w3_2, w2_2,
    )


_drawn_inputs = setup_inputs


def setup_inputs(seed=0):
    import zlib

    import numpy as np

    out = dict(_drawn_inputs(seed))
    spreads = {}
    factors = {'norm_mix_g': 4.008,
     'a_q_gain': 5.161,
     'a_k_gain': 3.963,
     'a_subln_g': 2.673,
     'b_q_gain': 8.0,
     'b_k_gain': 8.0,
     'b_rel_bias': 4.716,
     'ctx_2': 4.488,
     'b_mod_2': 3.204,
     'norm1_w_2': 8.0,
     'b_s_2': 8.0,
     'q_norm_w_2': 8.0,
     'k_norm_w_2': 8.0,
     'hgrn_norm_w_2': 8.0,
     'norm2_w_2': 4.99,
     'b_grp_2': 7.396,
     'b_exp_2': 45.439}
    for name, (base, spread) in spreads.items():
        noise = np.random.default_rng([zlib.crc32(name.encode()), seed]).standard_normal(out[name].shape)
        drawn = base * np.exp(spread * noise) if base else spread * noise
        out[name] = __import__('jax').numpy.asarray(drawn.astype(out[name].dtype))
    for name, factor in factors.items():
        out[name] = (out[name] * factor).astype(out[name].dtype)
    return out
```

```python
from contextlib import ExitStack
import math

import numpy as np
import concourse.bass as bass
from concourse import mybir

F32 = mybir.dt.float32
I32 = mybir.dt.int32
U32 = mybir.dt.uint32
ALU = mybir.AluOpType
ACT = mybir.ActivationFunctionType
AX = mybir.AxisListType

P = 128
D = 1024
KT = D // P
S = 256
TT = S // P
FF = 512
FT = FF // P
CHUNK = 512
NSLOT = 6
SLOTS = 64
ROUNDS = S // SLOTS
HEAD = 64
EPS = 1e-6
NEG = -1e30
FAR = -3e38
LAMBDA_INIT = 0.8 - 0.6 * math.exp(-0.3 * 0)
SUB = 16
NSUB = S // SUB
N_MOD = 6 * KT
SH1, SC1, G1, SH2, SC2, G2 = (KT * n for n in range(6))
EXPERTS = (16, 16, 32)
GROUPS = 4

V_ADA = (0, 48, 128)
V_C, V_NORM1 = 96, 120
V_MIX, V_FFN = (176, 184, V_NORM1), (192, 200, 208)
V_GAIN = 216
GAIN_AQ, GAIN_AK, GAIN_BQ, GAIN_BK, GAIN_Q2, GAIN_K2, GAIN_O2, GAIN_SUB = range(V_GAIN, V_GAIN + 8)
N_VEC = V_GAIN + 8

C_ID, C_FLIP, C_TRI, C_ONE = 0, 128, 256, 384
C_SEL = 512
C_SEL8 = C_SEL + 512
C_IOTA = C_SEL8 + 64
C_COS, C_SIN = C_IOTA + 64, C_IOTA + 64 + 256
C_ROT = C_SIN + 256
C_DIAG = C_ROT + 128
C_DUP = C_DIAG + 256
N_CST = C_DUP + 256
C2_SPREAD, C2_SPREAD8 = 0, 2048
N_CST2 = 2048 + 1024


def constants():
    c = np.zeros((P, N_CST), np.float32)
    p = np.arange(P)
    c[:, C_ID:C_ID + P] = np.eye(P)
    c[:, C_FLIP:C_FLIP + P] = np.eye(P)[::-1]
    c[:, C_TRI:C_TRI + P] = p[:, None] < p[None, :]
    c[:, C_ONE:C_ONE + P] = 1.0
    c2 = np.zeros((32, N_CST2), np.float32)
    for sl in range(16):
        c[p, C_SEL + 32 * sl + 2 * sl + p // HEAD] = 1.0
        c2[2 * sl + p // HEAD, C2_SPREAD + P * sl + p] = 1.0
    for h in range(8):
        c[:, C_SEL8 + 8 * h + h] = 1.0
        c2[h, C2_SPREAD8 + P * h:C2_SPREAD8 + P * h + P] = 1.0
    c[:, C_IOTA:C_IOTA + 64] = np.arange(64)
    t = np.arange(S)
    inv = (1.0 / (np.float32(10000.0) ** (np.arange(0, 32, 2, dtype=np.float32) / np.float32(32)))).astype(np.float32)
    ang = np.stack([(t // 64).astype(np.float32)[:, None] * inv, (t % 64).astype(np.float32)[:, None] * inv], 1)
    d = p % HEAD
    c[:, C_COS:C_COS + S] = np.cos(ang)[:, d // 32, d % 16].T
    c[:, C_SIN:C_SIN + S] = np.sin(ang)[:, d // 32, d % 16].T
    for m in range(P):
        if (m % 32) < 16:
            c[m + 16, C_ROT + m] = -1.0
        else:
            c[m - 16, C_ROT + m] = 1.0
    same = p[:, None] // SUB == p[None, :] // SUB
    c[:, C_DIAG:C_DIAG + P] = same & (p[None, :] <= p[:, None])
    c[:, C_DIAG + P:C_DIAG + 2 * P] = same & (p[None, :] >= p[:, None])
    for g in range(2):
        c[g * HEAD + p % HEAD, C_DUP + P * g + p] = 1.0
    rel = np.arange(512) - 255
    n = np.abs(rel)
    far = 8 + (np.log(np.maximum(n, 1).astype(np.float32) / np.float32(8)) / np.float32(math.log(1024 / 8))
               * np.float32(8)).astype(np.int32)
    bucket = np.where(rel > 0, 16, 0) + np.where(n < 8, n, np.minimum(far, 15))
    onehot = (np.arange(32)[:, None] == bucket[None, :]).astype(np.float32)
    return c, c2, onehot


def make_turn():
    at = {}

    def turn(sem, n=1):
        at[sem.name] = at.get(sem.name, 0) + n
        return at[sem.name]

    return turn


def program(nc, x, c, ada_w, ada_b, norm_mix_g, norm_ffn_g, t5_bias, a_w_qkv, a_q_gain, a_k_gain, a_lambda,
            a_subln_g, a_w_o, b_w_qkv, b_q_gain, b_k_gain, b_rel_bias, b_w_o, router_w, router_bias,
            moe_w_gate, moe_w_up, moe_w_down, c_2, ctx_2, c_ctx_2, w_mod_2, b_mod_2, norm1_w_2, w_in_2,
            w_s_2, b_s_2, q_norm_w_2, k_norm_w_2, hgrn_lb_logits_2, hgrn_norm_w_2, w_out_2, norm2_w_2,
            w_grp_2, b_grp_2, w_exp_2, b_exp_2, w1_2, w3_2, w2_2, cst_d, cst2_d, bucket_d, out):
    with ExitStack() as ctx:
        def sb(name, shape, dt=F32):
            return ctx.enter_context(nc.sbuf_tensor(name, shape, dt))

        def sem(name):
            return ctx.enter_context(nc.semaphore(name))

        ring = [sb(f"ring{s}", [P, KT * CHUNK]) for s in range(NSLOT)]
        xT = sb("xT", [P, KT, S])
        hh = sb("hh", [P, KT, 2 * S])
        sq = sb("sq", [P, KT * S])
        cst, cst2 = sb("cst", [P, N_CST]), sb("cst2", [32, N_CST2])
        vec = sb("vec", [P, N_VEC])
        csil = sb("csil", [P, 3, KT])
        mod = sb("mod", [P, 3, N_MOD])
        modc = sb("modc", [P, 2 * KT])
        gain1, gain2 = sb("gain1", [P, 3, KT]), sb("gain2", [P, 3, KT])
        gainc = sb("gainc", [P, KT])
        qscale = sb("qscale", [P, 4])
        rt, rstd = sb("rt", [P, S]), sb("rstd", [P, S])
        rw, rb = sb("rw", [P, KT, 16]), sb("rb", [P, 16])
        rw2, rb2 = sb("rw2", [P, KT, 36]), sb("rb2", [P, 36])
        eps = sb("eps", [P, 1])
        nlam = sb("nlam", [P, 1])
        stat = sb("stat", [P, 2, 8])
        nit = sb("nit", [P, 2], I32)
        arena = sb("arena", [P, 13448])

        def view(at, *shape):
            n = int(np.prod(shape))
            v = arena[:, at:at + n]
            if len(shape) == 2:
                v = v.rearrange("p (a b) -> p a b", a=shape[0])
            elif len(shape) == 3:
                v = v.rearrange("p (a b c) -> p a b c", a=shape[0], b=shape[1])
            elif len(shape) == 4:
                v = v.rearrange("p (a b c d) -> p a b c d", a=shape[0], b=shape[1], c=shape[2])
            return v

        vecrow = view(0, 2, P)
        t5row = arena[0:8, 256:768]
        lamrow = arena[0:1, 768:1024]
        lamtmp = arena[0:1, 1024:1160]
        bucket = arena[0:32, 1160:1672]
        t5b = arena[0:32, 1672:1680]
        raw = view(0, 16, S)
        v_tok = view(4096, TT, D)
        bias = view(6144, 16, S)
        s_sb = view(10240, 2, 2, S)
        prob = view(11264, 2, 2, S)
        probT = view(12288, 2, 2, S)
        h_tok = view(0, TT, D)
        x_sel = view(2048, KT, 2 * SLOTS)
        hid = view(3072, 2, FT * SLOTS)
        gate_act = view(3584, 2, FT * SLOTS)
        y_sel = view(4096, D)
        pick = view(5120, TT, 2 * SLOTS)
        pick_g = view(5376, TT, 2 * SLOTS)
        spread_g = view(5632, S)
        slot_of, gate_of = view(5888, TT, 130), view(6148, TT, 130)
        r0 = 6408
        ctx_tok = view(7300, TT, D)
        ws = view(9348, 4, P)
        bs = arena[0:1, 9860:10372]
        cT = view(10372, KT, S)
        uT, vm = view(0, 2, S), view(512, TT, S)
        q2, k2, vb = view(1024, 4, S), view(2048, 512), view(2560, 4, P)
        wsT = view(3072, 4, P)
        p2, pT2 = view(3584, 2, 512), view(4608, 4, S)
        qh, vh, gs = view(5632, 2, S), view(6144, 4, S), view(7168, 2, S)
        z = view(11400, 2, 2, 2 * S)
        bpad, epad = view(0, 2, 2, 257), view(1028, 2, 2, 257)
        bsub, lks, qq = view(2056, 2, 2, S), view(3080, 2, 2, S), view(4104, 2, 2, S)
        sc, dm = view(5128, 2, P), view(10752, 4, P)
        kk, sT = view(7680, 2, 512), view(8704, 2, 4, S)
        kd = view(7680, 2, 512)
        o2, osq = view(7680, 2, S), view(8192, 2, S)
        LK = z
        nlk = hh[:, :, S:2 * S]
        lnb = sq[:, :].rearrange("p (a b c) -> p a b c", a=2, b=2)
        oT = hh[:, :, S:2 * S]
        ymix = hh[:, :, 0:S]

        def K(at, n=P, rows=P):
            return cst[0:rows, at:at + n]

        ident, ones = K(C_ID), K(C_ONE)
        bank = [ctx.enter_context(nc.psum_tensor(f"bank{i}", [P, 512], F32)) for i in range(2)]
        pair = [ctx.enter_context(nc.psum_tensor(f"pair{i}", [P, 2, 512], F32)) for i in range(2)]
        b = [bank[0][:, :], bank[1][:, :], pair[0][:, 0, :], pair[0][:, 1, :], pair[1][:, 0, :], pair[1][:, 1, :]]
        bank6 = ctx.enter_context(nc.psum_tensor("bank6", [P, 512], F32))
        bank7 = ctx.enter_context(nc.psum_tensor("bank7", [P, 512], F32))
        b += [bank6[:, :], bank7[:, :]]
        t5_dram = nc.dram_tensor("t5_rows", (8, 512), F32, kind="Internal").ap()

        const_in, x_in = sem("const_in"), sem("x_in")
        t5_row, t5_out, bias_in = sem("t5_row"), sem("t5_out"), sem("bias_in")
        l2_in, out_done = sem("l2_in"), sem("out_done")
        full = [sem(f"slot_full{s}") for s in range(NSLOT)]
        dve_step, act_step = sem("dve_step"), sem("act_step")
        eps_ready, turned, vec_ready, csil_ready = sem("eps_ready"), sem("turned"), sem("vec_ready"), sem("csil_ready")
        x_ready, mod_cols, mod_ready = sem("x_ready"), sem("mod_cols"), sem("mod_ready")
        lam_sums, lam_exp, lam_diff, lam_bc, lam_ready = (sem(n) for n in ("lam_sums", "lam_exp", "lam_diff", "lam_bc", "lam_ready"))
        t5_ps = sem("t5_ps")
        sq_ready, ssq_ps, rt_ready, h_ready = sem("sq_ready"), sem("ssq_ps"), sem("rt_ready"), sem("h_ready")
        qk_proj, raw_ready, rs_ready, bc_ps, norm_ready = (sem(n) for n in ("qk_proj", "raw_ready", "rs_ready", "bc_ps", "norm_ready"))
        v_proj, v_ready, flip_ps, bias_ready = (sem(n) for n in ("v_proj", "v_ready", "flip_ps", "bias_ready"))
        scores_ps, s_added, max_ready, exp_ready, prob_ready = (sem(n) for n in ("scores_ps", "s_added", "max_ready", "exp_ready", "prob_ready"))
        turn_ps, probT_ready, pv_ps, o_ready = (sem(n) for n in ("turn_ps", "probT_ready", "pv_ps", "o_ready"))
        out_proj, x_attn = sem("out_proj"), sem("x_attn")
        logits_ps, h_turned, h_tok_ready = sem("logits_ps"), sem("h_turned"), sem("h_tok_ready")
        score_ready, mask_ready, rank_ps, n_ready = (sem(n) for n in ("score_ready", "mask_ready", "rank_ps", "n_ready"))
        in_proj, in_ready = sem("in_proj"), sem("in_ready")
        vm_ready, mix_ps, ymix_ready = sem("vm_ready"), sem("mix_ps"), sem("ymix_ready")
        prod_ready, sc_ps, sc_ready, dm_ready = (sem(n) for n in ("prod_ready", "sc_ps", "sc_ready", "dm_ready"))
        kk_zero, kk_ready, off_ps, sT_ready, sT_full = (sem(n) for n in ("kk_zero", "kk_ready", "off_ps", "sT_ready", "sT_full"))
        arg_ready, prod_exp = sem("arg_ready"), sem("prod_exp")
        gap_ready, gap_exp = sem("gap_ready"), sem("gap_exp")
        vec_ps, ws_ready, vm_sums, vm_rt = sem("vec_ps"), sem("ws_ready"), sem("vm_sums"), sem("vm_rt")
        dm_ps, ln_ready, log_ready, qdec_ready = sem("dm_ps"), sem("ln_ready"), sem("log_ready"), sem("qdec_ready")
        out_tok = sem("out_tok")
        MOE = []
        for l in range(3):
            MOE.append({n: sem(f"{n}_{l}") for n in (
                "pick_ready", "pickg_ready", "gather_ps", "sel_a", "sel_b", "gateup_ps", "silu_ready", "hid_ready",
                "gate_turned", "spread_ready", "down_ps", "y_a", "y_b", "comb_ps", "added")})
            MOE[l]["full"] = [sem(f"moe_full{s}_{l}") for s in range(NSLOT)]

        def columns(w, n):
            return w[:, n * CHUNK:(n + 1) * CHUNK].rearrange("(k p) n -> p k n", p=P)

        MOD_W = (ada_w[0], ada_w[1], w_mod_2[0])
        QKV, W_O = (a_w_qkv[0], b_w_qkv[0], w_in_2[0]), (a_w_o[0], b_w_o[0], w_out_2[0])
        GATE_W = (moe_w_gate[0], moe_w_gate[1], w1_2[0])
        UP_W = (moe_w_up[0], moe_w_up[1], w3_2[0])
        DOWN_W = (moe_w_down[0], moe_w_down[1], w2_2[0])
        IN_PARTS = [["u0", "u1", "vm0", "vm1"], ["q0", "q1", "q2", "q3"],
                    ["k", "vb0", "vb1", "vb2", "vb3", "qh0", "qh1"], ["zf0", "zf1", "zb0", "zb1"],
                    ["vh0", "vh1", "vh2", "vh3", "g0", "g1"]]
        chunks = []

        def add_mod(l):
            for n in range(12):
                chunks.append((columns(MOD_W[l], n), mod_cols, 12 * l + n + 1))

        def add_out(l):
            for n in range(2):
                chunks.append((columns(W_O[l], n), out_proj, 8 * l + 4 * (n + 1)))

        moe_at = []
        add_mod(0)
        for l in range(2):
            for n in range(6):
                chunks.append((columns(QKV[l], n),) + ((qk_proj, 16 * l + 4 * (n + 1)) if n < 4
                                                       else (v_proj, 4 * l + 2 * (n - 3))))
            add_mod(l + 1)
            add_out(l)
            moe_at.append(len(chunks))
        done = 0
        for n in range(5):
            done += len(IN_PARTS[n])
            chunks.append((columns(QKV[2], n), in_proj, done))
        add_out(2)
        moe_at.append(len(chunks))

        def slot_of_chunk(n):
            return n % NSLOT

        def moe_slot(l, a, m):
            return (moe_at[l] + 3 * a + m) % NSLOT

        const_loads = []

        def const(dst, src):
            const_loads.append((dst, src))

        const(cst[:, :], cst_d)
        const(cst2[:, :], cst2_d)
        const(bucket, bucket_d)
        const(t5b, t5_bias)
        rows = lambda r, n: arena[r % P:r % P + n, (r // P) * P:(r // P + 1) * P]
        as_rows = lambda a: a.rearrange("(r q) -> r q", q=P)
        for l in range(3):
            const(rows(V_ADA[l], 48), as_rows(b_mod_2[0] if l == 2 else ada_b[l]))
        const(rows(V_C, 8), as_rows(c[0]))
        const(rows(V_C + 8, 8), as_rows(c_2[0]))
        const(rows(V_C + 16, 8), as_rows(c_ctx_2))
        const(rows(V_NORM1, 8), as_rows(norm1_w_2[0]))
        for l in range(2):
            const(rows(V_MIX[l], 8), as_rows(norm_mix_g[l]))
            const(rows(V_FFN[l], 8), as_rows(norm_ffn_g[l]))
        const(rows(V_FFN[2], 8), as_rows(norm2_w_2[0]))
        for r, g in ((GAIN_AQ, a_q_gain), (GAIN_AK, a_k_gain), (GAIN_BQ, b_q_gain), (GAIN_BK, b_k_gain),
                     (GAIN_Q2, q_norm_w_2), (GAIN_K2, k_norm_w_2), (GAIN_O2, hgrn_norm_w_2)):
            for half in range(2):
                const(rows(r, 1)[:, half * HEAD:(half + 1) * HEAD], g)
        const(rows(GAIN_SUB, 1), a_subln_g)
        const(lamrow, a_lambda.rearrange("a n d -> a (n d)"))
        const(rw[:, :, :], router_w.rearrange("(k p) e -> p k e", p=P))
        const(rb[:, :], router_bias.partition_broadcast(P))
        const(rw2[:, :, 0:GROUPS], w_grp_2[0].rearrange("(k p) e -> p k e", p=P))
        const(rw2[:, :, GROUPS:36], w_exp_2[0].rearrange("(k p) e -> p k e", p=P))
        const(rb2[:, 0:GROUPS], b_grp_2[0].partition_broadcast(P))
        const(rb2[:, GROUPS:36], b_exp_2[0].partition_broadcast(P))

        block = ctx.enter_context(nc.Block())

        @block.sync
        def _(sp):
            turn = make_turn()
            for dst, src in const_loads:
                sp.dma_start(dst, src, allow_slow_non_contiguous=True).then_inc(const_in, 16)
            sp.dma_start(sq[:, :].rearrange("p (t d) -> p t d", t=TT),
                         x[0].rearrange("(t p) d -> p t d", p=P)).then_inc(x_in, 16)

            def load(n):
                src, _, _ = chunks[n]
                if n >= NSLOT and n - NSLOT not in fenced:
                    _, used, value = chunks[n - NSLOT]
                    sp.wait_ge(used, value)
                k = src.shape[1]
                s = slot_of_chunk(n)
                sp.dma_start(ring[s][:, :].rearrange("p (k n) -> p k n", k=k), src).then_inc(full[s], 16)

            fenced = set()
            more_rounds = [None] * 3

            def expert(l, a, m, e):
                s = moe_slot(l, a, m)
                w = (GATE_W, UP_W, DOWN_W)[m][l]
                src = w[bass.ds(e, 1)].rearrange("a (k p) n -> p (a k) n", p=P)
                sp.dma_start(ring[s][:, :].rearrange("p (k n) -> p k n", k=FT if m == 2 else KT),
                             src).then_inc(MOE[l]["full"][s], 16)

            def load_hybrid():
                sp.wait_ge(x_attn, 16)
                sp.dma_start(ctx_tok, ctx_2[0].rearrange("(t p) d -> p t d", p=P)).then_inc(l2_in, 16)
                sp.dma_start(ws, w_s_2[0].rearrange("h t s -> t h s")).then_inc(l2_in, 16)
                sp.dma_start(bs, b_s_2.rearrange("a h t -> a (h t)")).then_inc(l2_in, 16)

            def experts(l):
                E, M = EXPERTS[l], MOE[l]
                for a in range(2):
                    for m in range(3):
                        n = moe_at[l] + 3 * a + m - NSLOT
                        _, used, value = chunks[n]
                        sp.wait_ge(used, value)
                        expert(l, a, m, a)
                if l == 1:
                    load_hybrid()
                with sp.Fori(1, E // 2) as i:
                    for a in range(2):
                        for m in range(3):
                            sp.wait_ge(M["down_ps" if m == 2 else "gateup_ps"], 2 * i - 1 + a)
                            expert(l, a, m, 2 * i + a)
                sp.wait_ge(n_ready, turn(n_ready))
                more = sp.value_load(nit[0:1, 1:2], min_val=0, max_val=ROUNDS - 1)
                with sp.If(more > 0):
                    with sp.Fori(0, more) as r:
                        with sp.Fori(0, E // 2) as i:
                            for a in range(2):
                                for m in range(3):
                                    sp.wait_ge(M["down_ps" if m == 2 else "gateup_ps"],
                                               r * E + 2 * i + (E - 1 + a))
                                    expert(l, a, m, 2 * i + a)
                more_rounds[l] = more

            def after_experts(l, n):
                for k in range(NSLOT):
                    a, m = k // 3, k % 3
                    sp.wait_ge(MOE[l]["down_ps" if m == 2 else "gateup_ps"], more_rounds[l] * EXPERTS[l] + (EXPERTS[l] - 1 + a))
                    fenced.add(n + k - NSLOT)
                    load(n + k)

            for n in range(12):
                load(n)
                if n == 5:
                    sp.wait_ge(t5_row, turn(t5_row))
                    sp.dma_start(t5_dram, t5row).then_inc(t5_out, 16)
            sp.wait_ge(t5_out, 16)
            sp.dma_start(bias[:, 0:8, :], bass.AP(t5_dram.tensor, 0, [[1, P], [512, 8], [1, S]])).then_inc(bias_in, 16)
            for n in range(12, moe_at[0]):
                load(n)
            experts(0)
            after_experts(0, moe_at[0])
            sp.wait_ge(MOE[0]["added"], more_rounds[0] * (EXPERTS[0] // 2 * 4) + (EXPERTS[0] // 2 * 4 + 4))
            sp.dma_start(bias[:, :, :], bass.AP(b_rel_bias.tensor, 1, [[1, P], [513, 16], [1, S]])).then_inc(bias_in, 16)
            for n in range(moe_at[0] + NSLOT, moe_at[1]):
                load(n)
            experts(1)
            after_experts(1, moe_at[1])
            for n in range(moe_at[1] + NSLOT, moe_at[2]):
                load(n)
            experts(2)
            for t in range(TT):
                sp.wait_ge(out_tok, 2 * (t + 1))
                sp.dma_start(out[0, t * P:(t + 1) * P, :], sq[:, t * D:(t + 1) * D]).then_inc(out_done, 16)
            sp.wait_ge(out_done, 16 * TT)

        R8 = [ring[s][:, :].rearrange("p (k n) -> p k n", k=KT) for s in range(NSLOT)]
        R4 = [ring[s][:, :].rearrange("p (k n) -> p k n", k=FT) for s in range(NSLOT)]

        def cols(t):
            return slice(t * P, (t + 1) * P)

        def half(m):
            return slice(m * HEAD, (m + 1) * HEAD)

        def before(d, j):
            return slice(0, S + SUB * j) if d == 0 else slice(SUB * (j + 1), 2 * S)

        def ref_col(d, j):
            return SUB * j if d == 0 else SUB * (j + 1)

        def key_tiles(d, j):
            if d == 0:
                return (0, 1, 2) if j < NSUB // 2 else (0, 1, 2, 3)
            return (0, 1, 2, 3) if j < NSUB // 2 else (1, 2, 3)

        def seen_by(d, i):
            return slice(i, SUB) if d == 0 else slice(0, i + 1)

        def prod_of(q):
            d, i = divmod(q, SUB)
            buf = sq[:, q % 4 * 512:(q % 4 + 1) * 512]
            return buf.rearrange("p (n t) -> p n t", t=SUB)[:, :, seen_by(d, i)]

        vm_sq, vm_stat = view(3584, TT, S), arena[:, 4096:4120]

        def route_layout(E):
            at, r = r0, {}
            for name, shape in (("score", (TT, 16)), ("sel", (TT, 16)), ("sums", (TT * GROUPS, 6)), ("logits", (TT, 36)),
                                ("g8", (TT, 8)), ("best", (TT, 8)), ("number", (TT, 2)), ("gmask", (TT, GROUPS)),
                                ("masked", (TT, E)), ("fill", (TT, E)), ("hot0", (TT, E)), ("hot1", (TT, E)),
                                ("mask", (TT, E)), ("gate", (TT, E)), ("total", (TT,)), ("inv", (TT,)), ("inv1", (TT,)),
                                ("most", (1,)), ("steps", (ROUNDS - 1,)), ("gap", (TT, 5)), ("gap_exp", (TT, 5))):
                r[name] = view(at, *shape)
                at += int(np.prod(shape))
            r["index"] = arena[:, at:at + TT * 8].bitcast(U32).rearrange("p (t n) -> p t n", t=TT)
            r["hot"] = (r["hot0"], r["hot1"])
            assert at + TT * 8 <= 7300
            return r

        ROUTE = [route_layout(E) for E in EXPERTS]
        route_work = lambda l: ROUTE[l]
        route_mask = lambda l: ROUTE[l]["mask"]
        route_score = lambda l: ROUTE[l]["score"]
        route_gap, route_gap_exp = ROUTE[2]["gap"], ROUTE[2]["gap_exp"]
        UNITS = [(hp, d) for hp in range(2) for d in range(2)]
        PARTS = [(n, part) for n in range(5) for part in IN_PARTS[n]]

        @block.tensor
        def _(pe):
            turn = make_turn()
            mm = nc.tensor.matmul

            def chunk_in(n):
                s = slot_of_chunk(n)
                pe.wait_ge(full[s], turn(full[s], 16))
                return R8[s]

            def mod_chunk(l, n, at):
                w = chunk_in(at + n)
                width = 2 if l == 2 else 1
                for s4 in range(4):
                    col = (4 * n + s4) * width
                    for k in range(KT):
                        last = mm(b[0][:, col:col + width], w[:, k, cols(s4)],
                                  csil[:, 1:3, k] if l == 2 else csil[:, 0, k:k + 1],
                                  start=(k == 0), stop=(k == KT - 1))
                last.then_inc(mod_cols, 1)

            def square_sums():
                pe.wait_ge(sq_ready, turn(sq_ready))
                for k in range(KT):
                    last = mm(b[7][:, 0:S], ones, sq[:, k * S:(k + 1) * S], start=(k == 0), stop=(k == KT - 1))
                last.then_inc(ssq_ps, 1)

            def qkv(l, at):
                pe.wait_ge(h_ready, turn(h_ready))

                def project(sl):
                    if sl % 4 == 0:
                        project.w = chunk_in(at + sl // 4)
                    for k in range(KT):
                        last = mm(b[sl % 2][:, 0:S], project.w[:, k, cols(sl % 4)], hh[:, k, 0:S],
                                  start=(k == 0), stop=(k == KT - 1))
                    last.then_inc(qk_proj, 1)

                def sums(sl):
                    pe.wait_ge(raw_ready, turn(raw_ready))
                    last = mm(b[2][0:32, 0:S], K(C_SEL + 32 * sl, 32), sq[:, (sl % 8) * S:(sl % 8 + 1) * S],
                              start=(sl == 0), stop=(sl == 15))
                    if sl == 15:
                        last.then_inc(ssq_ps, 1)

                project(0)
                for sl in range(1, 16):
                    project(sl)
                    sums(sl - 1)
                sums(15)
                for n in range(2):
                    w = chunk_in(at + 4 + n)
                    for t in range(TT):
                        if n == 1:
                            pe.wait_ge(v_ready, turn(v_ready))
                        for k in range(KT):
                            last = mm(b[t], hh[:, k, cols(t)], w[:, k, :], start=(k == 0), stop=(k == KT - 1))
                        last.then_inc(v_proj, 1)
                pe.wait_ge(bias_in, turn(bias_in, 16))
                flips = 4 * (l + 1)
                for n in range(flips):
                    if n >= 2:
                        pe.wait_ge(bias_ready, turn(bias_ready))
                    mm(b[6 + n % 2], K(C_FLIP), bias[:, 2 * n:2 * n + 2, :], start=True, stop=True).then_inc(flip_ps, 1)
                pe.wait_ge(rs_ready, turn(rs_ready))
                for sl in range(16):
                    if sl >= 2:
                        pe.wait_ge(norm_ready, turn(norm_ready))
                    at2 = C2_SPREAD + P * sl
                    mm(b[4 + sl % 2][:, 0:S], cst2[0:32, at2:at2 + P], rstd[0:32, :],
                       start=True, stop=True).then_inc(bc_ps, 1)
                pe.wait_ge(norm_ready, turn(norm_ready, 2))
                pe.wait_ge(bias_ready, turn(bias_ready, 2))
                pe.wait_ge(v_ready, turn(v_ready, 2))

            def attention(l, mod_at):
                def scores(u):
                    h, qt = divmod(u, TT)
                    if u >= 2:
                        pe.wait_ge(s_added, turn(s_added))
                    for m in range(2):
                        last = mm(pair[u % 2][:, m, 0:P * (qt + 1)], raw[half(m), h, cols(qt)],
                                  raw[half(m), 8 + h, 0:P * (qt + 1)], start=True, stop=True)
                    last.then_inc(scores_ps, 1)

                maps = 1 if l == 0 else 2

                def transposes(u):
                    qt = u % TT
                    pe.wait_ge(prob_ready, turn(prob_ready))
                    if u >= 1:
                        pe.wait_ge(probT_ready, 16 * l + u)
                    for kt in range(qt + 1):
                        for m in range(maps):
                            last = nc.tensor.transpose(b[6][:, cols(kt * maps + m)], prob[:, u % 2, m, cols(kt)], ident)
                    last.then_inc(turn_ps, 1)

                def values(h):
                    pe.wait_ge(probT_ready, 16 * l + 2 * h + 2)
                    if h >= 1:
                        pe.wait_ge(o_ready, 8 * l + h)
                    wide = P // maps
                    for m in range(maps):
                        rows = slice(m * wide, (m + 1) * wide)
                        for kt in range(TT):
                            last = mm(b[7][rows, kt * P:S], v_tok[:, kt, h * P + m * wide:h * P + (m + 1) * wide],
                                      probT[:, kt, m, kt * P:S], start=(kt == 0), stop=(kt == TT - 1))
                    last.then_inc(pv_ps, 1)

                scores(0)
                n = 0
                for u in range(16):
                    if u < 15:
                        scores(u + 1)
                    if u % 4 != 3:
                        mod_chunk(l + 1, n, mod_at)
                        n += 1
                    transposes(u)
                    if u % TT == TT - 1:
                        values(u // TT)
                pe.wait_ge(o_ready, turn(o_ready, 8))
                if l == 0:
                    for h in range(8):
                        last = mm(b[6][0:8, 0:S], K(C_SEL8 + 8 * h, 8), sq[:, h * S:(h + 1) * S],
                                  start=(h == 0), stop=(h == 7))
                    last.then_inc(ssq_ps, 1)
                    pe.wait_ge(rs_ready, turn(rs_ready))
                    for h in range(8):
                        if h >= 2:
                            pe.wait_ge(norm_ready, turn(norm_ready))
                        at2 = C2_SPREAD8 + P * h
                        mm(b[4 + h % 2][:, 0:S], cst2[0:8, at2:at2 + P], rstd[0:8, :],
                           start=True, stop=True).then_inc(bc_ps, 1)
                    pe.wait_ge(norm_ready, turn(norm_ready, 2))

            def project_out(l, at, src):
                for n in range(2):
                    w = chunk_in(at + n)
                    for s4 in range(4):
                        c = 4 * n + s4
                        if c >= 4:
                            pe.wait_ge(x_attn, 8 * l + c - 3)
                        for k in range(KT):
                            last = mm(b[2 + c % 4][:, 0:S], w[:, k, cols(s4)], src[:, k, :],
                                      start=(k == 0), stop=(k == KT - 1))
                        last.then_inc(out_proj, 1)

            def route(l):
                E = EXPERTS[l]
                w, width = (rw2, 36) if l == 2 else (rw, 16)
                pe.wait_ge(h_ready, turn(h_ready))
                for t in range(TT):
                    for k in range(KT):
                        last = mm(b[6][:, t * width:(t + 1) * width], hh[:, k, cols(t)], w[:, k, :],
                                  start=(k == 0), stop=(k == KT - 1))
                last.then_inc(logits_ps, 1)
                if l < 2:
                    pe.wait_ge(mod_ready, l + 2)
                for t in range(TT):
                    for k in range(KT):
                        last = nc.tensor.transpose(b[2 * t + k // 4][:, cols(k % 4)], hh[:, k, cols(t)], ident)
                        if k % 4 == 3:
                            last.then_inc(h_turned, 1)
                pe.wait_ge(mask_ready, turn(mask_ready))
                mask = route_mask(l)
                mm(b[7][:, 0:E], K(C_TRI), mask[:, 0, :], start=True, stop=True)
                for n, first in ((1, K(C_TRI)), (2, ones)):
                    mm(b[7][:, n * E:(n + 1) * E], first, mask[:, 1, :], start=True, stop=False)
                    last = mm(b[7][:, n * E:(n + 1) * E], ones, mask[:, 0, :], start=False, stop=True)
                last.then_inc(rank_ps, 1)

            def experts(l):
                M = MOE[l]

                def gather():
                    for k in range(KT):
                        for t in range(TT):
                            last = mm(b[k // 4][:, cols(k % 4)], h_tok[:, t, cols(k)], pick[:, t, :],
                                      start=(t == 0), stop=(t == TT - 1))
                    last.then_inc(M["gather_ps"], 1)

                def gate_up(i, a):
                    pe.wait_ge(M["hid_ready"], 2 * i + 1 + a)
                    for m in range(2):
                        s = moe_slot(l, a, m)
                        pe.wait_ge(M["full"][s], 16 * i + 16)
                        for f in range(FT):
                            at = (m * FT + f) * SLOTS
                            for k in range(KT):
                                last = mm(b[2 + a][:, at:at + SLOTS], R8[s][:, k, cols(f)],
                                          x_sel[:, k, a * SLOTS:(a + 1) * SLOTS], start=(k == 0), stop=(k == KT - 1))
                    last.then_inc(M["gateup_ps"], 1)

                def down(i, a):
                    pe.wait_ge(M["hid_ready"], 2 * i + 3 + a)
                    s = moe_slot(l, a, 2)
                    pe.wait_ge(M["full"][s], 16 * i + 16)
                    for n in range(2):
                        for f in range(FT):
                            last = mm(b[4 + n][a * SLOTS:(a + 1) * SLOTS, :], hid[:, a, f * SLOTS:(f + 1) * SLOTS],
                                      R4[s][:, f, n * 512:(n + 1) * 512], start=(f == 0), stop=(f == FT - 1))
                    last.then_inc(M["down_ps"], 1)

                pe.wait_ge(n_ready, l + 1)
                n = pe.value_load(nit[0:1, 0:1], min_val=1, max_val=ROUNDS * EXPERTS[l] // 2)
                pe.wait_ge(h_tok_ready, turn(h_tok_ready, 4))
                pe.wait_ge(M["pick_ready"], 1)
                gather()
                with pe.Fori(0, n) as i:
                    pe.wait_ge(M["sel_a"], i + 1)
                    pe.wait_ge(M["sel_b"], i + 1)
                    gate_up(i, 0)
                    pe.wait_ge(M["pickg_ready"], i + 1)
                    pe.wait_ge(M["added"], 4 * i + 4)
                    for t in range(TT):
                        last = nc.tensor.transpose(b[7][:, cols(t)], pick_g[:, t, :], ident)
                    last.then_inc(M["gate_turned"], 1)
                    gate_up(i, 1)
                    pe.wait_ge(M["pick_ready"], i + 2)
                    gather()
                    pe.wait_ge(M["y_a"], i + 1)
                    pe.wait_ge(M["y_b"], i + 1)
                    down(i, 0)
                    down(i, 1)
                    pe.wait_ge(M["spread_ready"], i + 1)
                    pe.wait_ge(M["y_a"], i + 2)
                    pe.wait_ge(M["y_b"], i + 2)
                    for r in range(4):
                        if r >= 2:
                            pe.wait_ge(M["added"], 4 * i + 3 + r)
                        for k in range(2):
                            last = mm(b[6 + r % 2][:, k * S:(k + 1) * S], y_sel[:, cols(2 * r + k)], spread_g,
                                      start=True, stop=True)
                        last.then_inc(M["comb_ps"], 1)
                pe.wait_ge(M["sel_a"], n + 1)
                pe.wait_ge(M["sel_b"], n + 1)
                pe.wait_ge(M["added"], n * 4 + 4)

            def turn_tokens(src, last_sem):
                for k in range(KT):
                    for t in range(TT):
                        last = nc.tensor.transpose(b[1 + k // 2][:, cols(k % 2 * TT + t)], src(t, k), ident)
                    if k % 2 == 1:
                        last.then_inc(last_sem, 1)

            def hybrid(at):
                pe.wait_ge(l2_in, 48)
                turn_tokens(lambda t, k: ctx_tok[:, t, cols(k)], turned)
                square_sums()
                square_sums()
                pe.wait_ge(h_ready, turn(h_ready, 2))
                for idx, (n, part) in enumerate(PARTS):
                    if part == IN_PARTS[n][0]:
                        w = chunk_in(at + n)
                    if idx >= 4:
                        pe.wait_ge(in_ready, idx - 3)
                    name, num = part.rstrip("0123456789"), part[len(part.rstrip("0123456789")):]
                    num = int(num or 0)
                    o = b[idx % 4]
                    for k in range(KT):
                        f = dict(start=(k == 0), stop=(k == KT - 1))
                        if name == "u":
                            last = mm(o[:, 0:S], w[:, k, cols(num)], hh[:, k, 0:S], **f)
                        elif name == "vm":
                            last = mm(o[:, 0:S], hh[:, k, cols(num)], w[:, k, 256:512], **f)
                        elif name == "q":
                            last = mm(o[:, 0:S], w[:, k, cols(num)], hh[:, k, 0:S], **f)
                        elif name == "k":
                            last = mm(o, w[:, k, 0:P], hh[:, k, :], **f)
                        elif name == "vb":
                            last = mm(o[:, 0:P], hh[:, k, cols(num)], w[:, k, P:2 * P], **f)
                        elif name == "qh":
                            last = mm(o[:, 0:S], w[:, k, cols(2 + num)], hh[:, k, 0:S], **f)
                        elif name in ("zf", "zb"):
                            last = mm(o, w[:, k, cols(num + 2 * (name == "zb"))], hh[:, k, :], **f)
                        elif name == "vh":
                            last = mm(o[:, 0:S], hh[:, k, cols(num)], w[:, k, 0:256], **f)
                        else:
                            last = mm(o[:, 0:S], w[:, k, cols(2 + num)], hh[:, k, 0:S], **f)
                    last.then_inc(in_proj, 1)
                for h in range(4):
                    last = nc.tensor.transpose(b[4][:, cols(h)], ws[:, h, :], ident)
                last.then_inc(turned, 1)
                pe.wait_ge(ws_ready, 1)
                pe.wait_ge(vm_ready, 1)
                for h in range(4):
                    for t in range(TT):
                        o = b[5][half(h % 2), cols(h // 2 * TT + t)]
                        mm(o, vm[:, t, half(h)], wsT[:, h, :], start=True, stop=False)
                        last = mm(o, K(C_ONE, HEAD, 1), bs[:, cols(h)], start=False, stop=True)
                last.then_inc(mix_ps, 1)
                pe.wait_ge(in_ready, len(PARTS))
                pe.wait_ge(raw_ready, turn(raw_ready, 2))
                for j in range(4):
                    mm(b[6][0:32, 0:S], K(C_SEL + 32 * j, 32), sq[:, j * S:(j + 1) * S], start=(j == 0), stop=(j == 3))
                mm(b[7][0:32, :], K(C_SEL, 32), sq[:, 4 * S:6 * S], start=True, stop=True).then_inc(ssq_ps, 1)
                pe.wait_ge(rs_ready, turn(rs_ready))
                for j in range(4):
                    at2 = C2_SPREAD + P * j
                    last = mm(b[j // 2][:, j % 2 * S:(j % 2 + 1) * S], cst2[0:32, at2:at2 + P], rstd[0:32, :],
                              start=True, stop=True)
                    if j % 2 == 1:
                        last.then_inc(bc_ps, 1)
                mm(b[2], cst2[0:32, C2_SPREAD:C2_SPREAD + P], sq[0:32, 6 * S:8 * S], start=True, stop=True).then_inc(bc_ps, 1)
                for g in range(3):
                    pe.wait_ge(norm_ready, turn(norm_ready))
                    if g < 2:
                        last = mm(b[g], K(C_ROT), q2[:, 2 * g:2 * g + 2, :], start=True, stop=True)
                    else:
                        last = mm(b[2][:, 0:S], K(C_ROT), k2[:, 0:S], start=True, stop=True)
                    last.then_inc(bc_ps, 1)
                pe.wait_ge(norm_ready, turn(norm_ready, 3))
                for g in range(2):
                    mm(b[2 + g], K(C_DUP + P * g), k2, start=True, stop=True).then_inc(bc_ps, 1)
                pe.wait_ge(norm_ready, turn(norm_ready, 2))
                pe.wait_ge(ymix_ready, 1)

                def scores(u):
                    hd, qt = divmod(u, TT)
                    if u >= 2:
                        pe.wait_ge(exp_ready, 32 + u - 1)
                    mm(b[u % 2], q2[half(hd % 2), hd // 2, cols(qt)], kd[half(hd % 2), hd // 4, :],
                       start=True, stop=True).then_inc(scores_ps, 1)

                def transposes(u):
                    pe.wait_ge(prob_ready, turn(prob_ready))
                    if u >= 2:
                        pe.wait_ge(probT_ready, 32 + u - 1)
                    for kt in range(4):
                        last = nc.tensor.transpose(b[2 + u % 2][:, cols(kt)], p2[:, u % 2, cols(kt)], ident)
                    last.then_inc(turn_ps, 1)

                def values(hd):
                    pe.wait_ge(probT_ready, 32 + 2 * hd + 2)
                    if hd >= 2:
                        pe.wait_ge(o_ready, 16 + hd - 1)
                    for kt in range(4):
                        last = mm(b[4 + hd % 2][half(hd % 2), 0:S], vb[:, kt, half(hd // 4)], pT2[:, kt, :],
                                  start=(kt == 0), stop=(kt == 3))
                    last.then_inc(pv_ps, 1)

                scores(0)
                for u in range(16):
                    if u < 15:
                        scores(u + 1)
                    transposes(u)
                    if u % TT == TT - 1:
                        values(u // TT)
                pe.wait_ge(o_ready, 24)
                for q in range(2 * SUB):
                    d, i = divmod(q, SUB)
                    pe.wait_ge(prod_ready, q + 1)
                    prod = sq[:, q % 4 * 512:(q % 4 + 1) * 512]
                    for hp in range(2):
                        for t in range(TT):
                            at5 = ((d * 2 + hp) * TT + t) * 32 + i
                            last = mm(b[5][:, at5:at5 + 17:16], prod[:, hp * S + t * P:hp * S + (t + 1) * P],
                                      K(C_SEL, 2), start=True, stop=True)
                    last.then_inc(sc_ps, 1)
                for w, (hp, d) in enumerate(UNITS):
                    pe.wait_ge(dm_ready, w + 1)
                    for n in range(4):
                        last = nc.tensor.transpose(b[6][:, cols(n)], dm[:, n, :], ident)
                    last.then_inc(dm_ps, 1)
                    if w >= 1:
                        pe.wait_ge(sT_ready, w)
                    for jj in range(NSUB):
                        j = jj if d == 0 else NSUB - 1 - jj
                        pe.wait_ge(kk_ready, w * NSUB + jj + 1)
                        for m in range(2):
                            for kt in key_tiles(d, j):
                                o = b[2 * m + kt // 2][:, kt % 2 * S + j * SUB:kt % 2 * S + (j + 1) * SUB]
                                last = mm(o, kk[half(m), jj % 2, cols(kt)],
                                          qq[half(m), d, hp, j * SUB:(j + 1) * SUB], start=True, stop=True)
                        last.then_inc(off_ps, 1)
                    pe.wait_ge(sT_full, w + 1)
                    for m in range(2):
                        for n in range(4):
                            kt = n if d == 0 else (2, 3, 0, 1)[n]
                            tok = (2, 3, 0, 1)[kt] if d == 0 else kt
                            t0, t1 = (P, S) if (d, tok) == (0, 1) else (0, P) if (d, tok) == (1, 0) else (0, S)
                            last = mm(b[4][half(m), hp * S + t0:hp * S + t1], vh[:, tok, half(2 * hp + m)],
                                      sT[:, m, kt, t0:t1], start=(d == 0 and n == 0), stop=(d == 1 and n == 3))
                last.then_inc(pv_ps, 1)
                pe.wait_ge(o_ready, 25)
                for j in range(2):
                    last = mm(b[6][0:32, 0:S], K(C_SEL + 32 * j, 32), osq[:, j, :], start=(j == 0), stop=(j == 1))
                last.then_inc(ssq_ps, 1)
                pe.wait_ge(rs_ready, turn(rs_ready))
                for j in range(2):
                    at2 = C2_SPREAD + P * j
                    last = mm(b[5][:, j * S:(j + 1) * S], cst2[0:32, at2:at2 + P], rstd[0:32, :], start=True, stop=True)
                last.then_inc(bc_ps, 1)
                pe.wait_ge(ymix_ready, 2)

            pe.wait_ge(const_in, 16 * len(const_loads))
            nc.tensor.transpose(b[0][:, 0:P], vecrow[:, 0, :], ident)
            rest = N_VEC - P
            nc.tensor.transpose(b[0][:, P:N_VEC], vecrow[0:rest, 1, :], K(C_ID, rest, rest)).then_inc(vec_ps, 1)
            mm(b[5][0:8, :], t5b, bucket, start=True, stop=True).then_inc(t5_ps, 1)
            pe.wait_ge(x_in, 16)
            turn_tokens(lambda t, k: sq[:, t * D + k * P:t * D + (k + 1) * P], turned)
            pe.wait_ge(lam_diff, 1)
            mm(b[6][:, 0:1], K(C_ONE, P, 1), lamtmp[:, 132:133], start=True, stop=True).then_inc(lam_bc, 1)
            pe.wait_ge(csil_ready, 1)
            for n in range(12):
                mod_chunk(0, n, 0)
            at = 12
            for l in range(2):
                square_sums()
                qkv(l, at)
                attention(l, at + 6)
                project_out(l, at + 18, oT)
                square_sums()
                route(l)
                experts(l)
                at += 20
            hybrid(at)
            project_out(2, at + 5, ymix)
            square_sums()
            route(2)
            experts(2)
            for t in range(TT):
                for k in range(KT):
                    last = nc.tensor.transpose(b[2 * t + k // 4][:, cols(k % 4)], xT[:, k, cols(t)], ident)
                    if k % 4 == 3:
                        last.then_inc(turned, 1)

        @block.scalar
        def _(act):
            turn = make_turn()
            fn = nc.scalar.activation

            def squares(src):
                fn(sq[:, :].rearrange("p (k t) -> p k t", k=KT), src, ACT.Square).then_inc(sq_ready, 1)

            def root(src, dst, n, rows=P):
                fn(dst, src, ACT.Sqrt, bias=eps[0:rows, :], scale=1.0 / n).then_inc(rt_ready, 1)

            def norm(src):
                squares(src)
                act.wait_ge(ssq_ps, turn(ssq_ps))
                root(b[7][:, 0:S], rt[:, :], D)

            def qkv(l):
                for sl in range(16):
                    act.wait_ge(qk_proj, turn(qk_proj))
                    fn(raw[:, sl, :], b[sl % 2][:, 0:S], ACT.Copy)
                    fn(sq[:, (sl % 8) * S:(sl % 8 + 1) * S], b[sl % 2][:, 0:S], ACT.Square).then_inc(raw_ready, 1)
                act.wait_ge(ssq_ps, turn(ssq_ps))
                root(b[2][0:32, 0:S], rt[0:32, :], HEAD, 32)
                for n in range(2):
                    for t in range(TT):
                        act.wait_ge(v_proj, turn(v_proj))
                        fn(v_tok[:, t, n * 512:(n + 1) * 512], b[t], ACT.Copy).then_inc(v_ready, 1)

            def attention(l):
                maps = 1 if l == 0 else 2

                def exps(u):
                    act.wait_ge(max_ready, turn(max_ready))
                    wide = P * (u % TT + 1)
                    for m in range(2):
                        last = fn(prob[:, u % 2, m, 0:wide], s_sb[:, u % 2, m, 0:wide], ACT.Exp,
                                  bias=stat[:, u % 2, m:m + 1], accum_out=stat[:, u % 2, 2 + m:3 + m])
                    last.then_inc(exp_ready, 1)

                exps(0)
                for u in range(16):
                    h, qt = divmod(u, TT)
                    if u < 15:
                        exps(u + 1)
                    act.wait_ge(turn_ps, turn(turn_ps))
                    fn(probT[:, 0:qt + 1, 0:maps, cols(qt)],
                       b[6][:, 0:(qt + 1) * maps * P].rearrange("p (k m q) -> p k m q", k=qt + 1, m=maps),
                       ACT.Copy).then_inc(probT_ready, 1)
                    if qt == TT - 1:
                        act.wait_ge(pv_ps, turn(pv_ps))
                        last = fn(oT[:, h, :], b[7][:, 0:S], ACT.Copy)
                        if l == 0:
                            last = fn(sq[:, h * S:(h + 1) * S], b[7][:, 0:S], ACT.Square)
                        last.then_inc(o_ready, 1)
                if l == 0:
                    act.wait_ge(ssq_ps, turn(ssq_ps))
                    root(b[6][0:8, 0:S], rt[0:8, :], P, 8)

            def route(l):
                act.wait_ge(logits_ps, turn(logits_ps))
                if l < 2:
                    fn(route_score(l), b[6][:, 0:TT * 16].rearrange("p (t e) -> p t e", t=TT),
                       ACT.Sigmoid).then_inc(score_ready, 1)
                for n in range(4):
                    act.wait_ge(h_turned, turn(h_turned))
                    fn(h_tok[:, n // 2, n % 2 * 512:(n % 2 + 1) * 512], b[n], ACT.Copy).then_inc(h_tok_ready, 1)
                if l == 2:
                    act.wait_ge(gap_ready, 1)
                    fn(route_gap_exp, route_gap, ACT.Exp).then_inc(gap_exp, 1)

            def experts(l):
                M = MOE[l]
                act.wait_ge(n_ready, l + 1)
                n = act.value_load(nit[0:1, 0:1], min_val=1, max_val=ROUNDS * EXPERTS[l] // 2)
                act.wait_ge(M["gather_ps"], 1)
                fn(x_sel[:, 0:2, :], b[0][:, 0:2 * P].rearrange("p (k s) -> p k s", k=2),
                   ACT.Copy).then_inc(M["y_a"], 1)
                fn(x_sel[:, 2:4, :], b[0][:, 2 * P:4 * P].rearrange("p (k s) -> p k s", k=2),
                   ACT.Copy).then_inc(M["sel_a"], 1)
                with act.Fori(0, n) as i:
                    act.wait_ge(M["gateup_ps"], 2 * i + 1)
                    fn(gate_act[:, 0, :], b[2][:, 0:256], ACT.Silu).then_inc(M["silu_ready"], 1)
                    act.wait_ge(M["gate_turned"], i + 1)
                    fn(spread_g, b[7][:, 0:S], ACT.Copy).then_inc(M["spread_ready"], 1)
                    act.wait_ge(M["gateup_ps"], 2 * i + 2)
                    fn(gate_act[:, 1, :], b[3][:, 0:256], ACT.Silu).then_inc(M["silu_ready"], 1)
                    act.wait_ge(M["gather_ps"], i + 2)
                    fn(x_sel[:, 0:4, :], b[0].rearrange("p (k s) -> p k s", k=4), ACT.Copy).then_inc(M["sel_a"], 1)
                    act.wait_ge(M["down_ps"], 2 * i + 2)
                    fn(y_sel[:, 0:512], b[4], ACT.Copy).then_inc(M["y_a"], 1)
                act.wait_ge(M["added"], n * 4 + 4)

            def hybrid():
                for n in range(4):
                    act.wait_ge(turned, turn(turned))
                    fn(cT[:, 2 * n:2 * n + 2, :], b[1 + n].rearrange("p (k t) -> p k t", k=2), ACT.Copy).then_inc(act_step, 1)
                norm(xT[:, :, :])
                act.wait_ge(h_ready, 5)
                act.wait_ge(act_step, 4)
                norm(cT)
                for idx, (n, part) in enumerate(PARTS):
                    act.wait_ge(in_proj, idx + 1)
                    o = b[idx % 4]
                    num = int(part[-1]) if part[-1].isdigit() else 0
                    name = part[:-1] if part[-1].isdigit() else part
                    if name in ("u", "vm"):
                        last = fn((uT if name == "u" else vm)[:, num, :], o[:, 0:S], ACT.Gelu_apprx_tanh)
                    elif name in ("qh", "g"):
                        last = fn((qh if name == "qh" else gs)[:, num, :], o[:, 0:S], ACT.Silu)
                    elif name == "k":
                        last = fn(k2, o, ACT.Copy)
                    elif name in ("zf", "zb"):
                        last = fn(z[:, int(name == "zb"), num, :], o, ACT.Copy)
                    elif name == "vb":
                        last = fn(vb[:, num, :], o[:, 0:P], ACT.Copy)
                    else:
                        last = fn((q2 if name == "q" else vh)[:, num, :], o[:, 0:S], ACT.Copy)
                    last.then_inc(in_ready, 1)
                act.wait_ge(turned, turn(turned))
                fn(wsT, b[4].rearrange("p (h t) -> p h t", h=4), ACT.Copy).then_inc(ws_ready, 1)
                act.wait_ge(vm_sums, 1)
                fn(vm_stat[:, 8:16], vm_stat[:, 0:8], ACT.Sqrt, bias=eps[:, :], scale=1.0 / HEAD).then_inc(vm_rt, 1)
                act.wait_ge(in_ready, len(PARTS))
                fn(sq[:, 0:4 * S], q2.rearrange("p j t -> p (j t)"), ACT.Square).then_inc(raw_ready, 1)
                fn(sq[:, 4 * S:6 * S], k2, ACT.Square).then_inc(raw_ready, 1)
                act.wait_ge(ssq_ps, turn(ssq_ps))
                root(b[6][0:32, 0:S], rt[0:32, :], HEAD, 32)
                root(b[7][0:32, :], sq[0:32, 6 * S:8 * S], HEAD, 32)

                def exps(u):
                    act.wait_ge(max_ready, turn(max_ready))
                    fn(p2[:, u % 2, :], b[u % 2], ACT.Exp, bias=stat[:, u % 2, 0:1],
                       accum_out=stat[:, u % 2, 2:3]).then_inc(exp_ready, 1)

                exps(0)
                for u in range(16):
                    hd, qt = divmod(u, TT)
                    if u < 15:
                        exps(u + 1)
                    act.wait_ge(turn_ps, turn(turn_ps))
                    fn(pT2[:, :, cols(qt)], b[2 + u % 2].rearrange("p (k q) -> p k q", k=4), ACT.Copy).then_inc(probT_ready, 1)
                    if qt == TT - 1:
                        act.wait_ge(pv_ps, turn(pv_ps))
                        fn(ymix[half(hd % 2), 2 + hd // 2, :], b[4 + hd % 2][half(hd % 2), 0:S], ACT.Copy).then_inc(o_ready, 1)
                zz = z.rearrange("p a b t -> p (a b t)")
                act.wait_ge(norm_ready, 16 + 8 + 16 + 8)
                fn(sq[:, :], zz, ACT.Abs).then_inc(act_step, 1)
                act.wait_ge(act_step, 5)
                fn(sq[:, :], sq[:, :], ACT.Exp, scale=-1.0).then_inc(act_step, 1)
                act.wait_ge(act_step, 6)
                fn(sq[:, :], sq[:, :], ACT.Ln, bias=1.0).then_inc(ln_ready, 1)
                act.wait_ge(log_ready, 1)
                fn(qq.rearrange("p a b t -> p (a b t)"), bsub.rearrange("p a b t -> p (a b t)"), ACT.Exp).then_inc(qdec_ready, 1)
                for q in range(2 * SUB):
                    act.wait_ge(arg_ready, q + 1)
                    pr = prod_of(q)
                    fn(pr, pr, ACT.Exp).then_inc(prod_exp, 1)
                act.wait_ge(sc_ps, 2 * SUB)
                fn(sc.rearrange("p a b -> p (a b)"), b[5][:, 0:256], ACT.Copy).then_inc(sc_ready, 1)
                for w, (hp, d) in enumerate(UNITS):
                    act.wait_ge(kk_zero, w + 1)
                    for jj in range(NSUB):
                        j = jj if d == 0 else NSUB - 1 - jj
                        if jj >= 2:
                            act.wait_ge(off_ps, w * NSUB + jj - 1)
                        r = ref_col(d, j)
                        fn(kk[:, jj % 2, before(d, j)], LK[:, d, hp, before(d, j)], ACT.Exp,
                           bias=bpad[:, d, hp, r:r + 1]).then_inc(kk_ready, 1)
                    act.wait_ge(off_ps, (w + 1) * NSUB)
                    for n in range(4):
                        last = fn(sT[:, n // 2, n % 2 * 2:n % 2 * 2 + 2, :], b[n].rearrange("p (k t) -> p k t", k=2), ACT.Copy)
                    last.then_inc(sT_ready, 1)
                act.wait_ge(pv_ps, turn(pv_ps))
                fn(o2, b[4].rearrange("p (j t) -> p j t", j=2), ACT.Copy)
                fn(osq, b[4].rearrange("p (j t) -> p j t", j=2), ACT.Square).then_inc(o_ready, 1)
                act.wait_ge(ssq_ps, turn(ssq_ps))
                root(b[6][0:32, 0:S], rt[0:32, :], HEAD, 32)

            act.wait_ge(eps_ready, 1)
            act.wait_ge(t5_ps, 1)
            fn(t5row, b[5][0:8, :], ACT.Copy).then_inc(t5_row, 1)
            act.wait_ge(vec_ready, 1)
            fn(csil[:, :, :].rearrange("p a k -> p (a k)"), vec[:, V_C:V_C + 3 * KT], ACT.Silu).then_inc(csil_ready, 1)
            act.wait_ge(lam_sums, 1)
            fn(lamtmp[:, 130:132], lamtmp[:, 128:130], ACT.Exp).then_inc(lam_exp, 1)
            for n in range(4):
                act.wait_ge(turned, turn(turned))
                fn(xT[:, 2 * n:2 * n + 2, :], b[1 + n].rearrange("p (k t) -> p k t", k=2), ACT.Copy).then_inc(x_ready, 1)
            act.wait_ge(x_ready, 4)
            for l in range(2):
                norm(xT[:, :, :])
                qkv(l)
                attention(l)
                act.wait_ge(x_attn, 8 * (l + 1))
                norm(xT[:, :, :])
                route(l)
                experts(l)
            hybrid()
            act.wait_ge(x_attn, 24)
            norm(xT[:, :, :])
            route(2)
            experts(2)
            for n in range(4):
                act.wait_ge(turned, turn(turned))
                fn(sq[:, n * 512:(n + 1) * 512], b[n], ACT.Copy).then_inc(out_tok, 1)

        @block.gpsimd
        def _(pool):
            for w in range(len(UNITS)):
                if w == 0:
                    pool.wait_ge(log_ready, 1)
                else:
                    pool.wait_ge(off_ps, w * NSUB)
                nc.gpsimd.memset(kk, 0.0).then_inc(kk_zero, 1)

        @block.vector
        def _(dve):
            turn = make_turn()
            steps = [0]
            tt, ts, stt = nc.vector.tensor_tensor, nc.vector.tensor_scalar, nc.vector.scalar_tensor_tensor

            def then(ins):
                steps[0] += 1
                ins.then_inc(dve_step, 1)
                dve.wait_ge(dve_step, steps[0])

            def finish_mod(l):
                dve.wait_ge(mod_cols, 12 * (l + 1))
                v = V_ADA[l]
                if l < 2:
                    then(tt(mod[:, l, :], b[0][:, 0:N_MOD], vec[:, v:v + N_MOD], ALU.add))
                else:
                    m2 = b[0][:, 0:2 * N_MOD].rearrange("p (n w) -> p n w", w=2)
                    then(tt(modc[:, :], m2[:, 0:2 * KT, 1], vec[:, v:v + 2 * KT], ALU.add))
                    then(tt(mod[:, l, :], m2[:, :, 0], vec[:, v:v + N_MOD], ALU.add))
                    then(stt(gainc[:, :], modc[:, SC1:SC1 + KT], 1.0, vec[:, V_NORM1:V_NORM1 + KT], ALU.add, ALU.mult))
                then(stt(gain1[:, l, :], mod[:, l, SC1:SC1 + KT], 1.0, vec[:, V_MIX[l]:V_MIX[l] + KT], ALU.add, ALU.mult))
                stt(gain2[:, l, :], mod[:, l, SC2:SC2 + KT], 1.0, vec[:, V_FFN[l]:V_FFN[l] + KT],
                    ALU.add, ALU.mult).then_inc(mod_ready, 1)
                dve.wait_ge(mod_ready, l + 1)

            def norm(src, at, gain, shift):
                dve.wait_ge(rt_ready, turn(rt_ready))
                then(nc.vector.reciprocal(rstd[:, :], rt[:, :]))
                xn = sq[:, :].rearrange("p (k t) -> p k t", k=KT)
                then(tt(xn, src, rstd[:, :].unsqueeze(1).broadcast_to([P, KT, S]), ALU.mult))
                for k in range(KT):
                    last = ts(hh[:, k, at:at + S], xn[:, k, :], gain[:, k:k + 1], shift[:, k:k + 1], ALU.mult, ALU.add)
                last.then_inc(h_ready, 1)

            def head_norms(rows):
                dve.wait_ge(rt_ready, turn(rt_ready))
                nc.vector.reciprocal(rstd[0:rows, :], rt[0:rows, :]).then_inc(rs_ready, 1)

            def qkv(l):
                head_norms(32)
                flips = 4 * (l + 1)
                for n in range(flips):
                    dve.wait_ge(flip_ps, turn(flip_ps))
                    nc.vector.tensor_copy(bias[:, 2 * n:2 * n + 2, :],
                                          b[6 + n % 2].rearrange("p (h j) -> p h j", h=2)).then_inc(bias_ready, 1)
                dve.wait_ge(bias_ready, turn(bias_ready, flips))
                then(nc.vector.memset(bias[0:64, 0:2 * flips, P + 64:S], NEG))
                for sl in range(16):
                    dve.wait_ge(bc_ps, turn(bc_ps))
                    gain = qscale[:, l:l + 1] if sl < 8 else vec[:, GAIN_AK + 2 * l:GAIN_AK + 2 * l + 1]
                    stt(raw[:, sl, :], raw[:, sl, :], gain, b[4 + sl % 2][:, 0:S], ALU.mult, ALU.mult).then_inc(norm_ready, 1)

            def attention(l):
                def maxima(u):
                    h, qt = divmod(u, TT)
                    wide, n = P * (qt + 1), u % 2
                    dve.wait_ge(scores_ps, turn(scores_ps))
                    by_key = slice(P - qt * P, S)
                    if l == 0:
                        bb = bias[:, h, by_key].unsqueeze(1).broadcast_to([P, 2, wide])
                    else:
                        bb = bias[:, 2 * h:2 * h + 2, by_key]
                    tt(s_sb[:, n, :, 0:wide], pair[n][:, :, 0:wide], bb, ALU.add).then_inc(s_added, 1)
                    dve.wait_ge(s_added, turn(s_added))
                    then(nc.vector.tensor_reduce(stat[:, n, 4:6], s_sb[:, n, :, 0:wide], AX.X, ALU.max))
                    ts(stat[:, n, 0:2], stat[:, n, 4:6], -1.0, None, ALU.mult).then_inc(max_ready, 1)

                def weights(u):
                    wide, n = P * (u % TT + 1), u % 2
                    dve.wait_ge(exp_ready, turn(exp_ready))
                    then(nc.vector.reciprocal(stat[:, n, 6:8], stat[:, n, 2:4]))
                    p0, p1 = prob[:, n, 0, 0:wide], prob[:, n, 1, 0:wide]
                    if l == 0:
                        then(tt(stat[:, n, 7:8], stat[:, n, 7:8], nlam[:, :], ALU.mult))
                        then(ts(p0, p0, stat[:, n, 6:7], None, ALU.mult))
                        last = stt(p0, p1, stat[:, n, 7:8], p0, ALU.mult, ALU.add)
                    else:
                        ts(p0, p0, stat[:, n, 6:7], None, ALU.mult)
                        last = ts(p1, p1, stat[:, n, 7:8], None, ALU.mult)
                    last.then_inc(prob_ready, 1)

                maxima(0)
                for u in range(16):
                    if u < 15:
                        maxima(u + 1)
                    weights(u)
                finish_mod(l + 1)
                if l == 0:
                    head_norms(8)
                    for h in range(8):
                        dve.wait_ge(bc_ps, turn(bc_ps))
                        stt(oT[:, h, :], oT[:, h, :], qscale[:, 3:4], b[4 + h % 2][:, 0:S],
                            ALU.mult, ALU.mult).then_inc(norm_ready, 1)

            def add_out(l):
                for c in range(KT):
                    dve.wait_ge(out_proj, turn(out_proj))
                    stt(xT[:, c, :], b[2 + c % 4][:, 0:S], mod[:, l, G1 + c:G1 + c + 1], xT[:, c, :],
                        ALU.mult, ALU.add).then_inc(x_attn, 1)

            def pick_group(scores8, best, index, number):
                for t in range(TT):
                    then(nc.vector.max(best[:, t, :], scores8[:, t, :]))
                    then(nc.vector.max_index(index[:, t, :], best[:, t, :], scores8[:, t, :]))
                then(nc.vector.tensor_copy(number, index[:, :, 0:2]))

            def choose(l, sel, number):
                E = EXPERTS[l]
                r = route_work(l)
                io = K(C_IOTA, GROUPS).unsqueeze(1).broadcast_to([P, TT, GROUPS])
                then(tt(r["gmask"], io, number[:, :, 0:1].broadcast_to([P, TT, GROUPS]), ALU.is_equal))
                wide = r["gmask"].unsqueeze(3).broadcast_to([P, TT, GROUPS, E // GROUPS])
                by_group = lambda a: a.rearrange("p t (g e) -> p t g e", g=GROUPS)
                then(nc.vector.tensor_copy(by_group(r["masked"]), wide))
                then(ts(r["fill"], r["masked"], -1.0, -NEG, ALU.add, ALU.mult))
                then(tt(r["masked"], r["masked"], sel, ALU.mult))
                then(tt(r["masked"], r["masked"], r["fill"], ALU.add))
                for t in range(TT):
                    then(nc.vector.max(r["best"][:, t, :], r["masked"][:, t, :]))
                    then(nc.vector.max_index(r["index"][:, t, :], r["best"][:, t, :], r["masked"][:, t, :]))
                then(nc.vector.tensor_copy(r["number"], r["index"][:, :, 0:2]))
                ie = K(C_IOTA, E).unsqueeze(1).broadcast_to([P, TT, E])
                for n in range(2):
                    then(tt(r["hot"][n], ie, r["number"][:, :, n:n + 1].broadcast_to([P, TT, E]), ALU.is_equal))
                tt(route_mask(l), r["hot"][0], r["hot"][1], ALU.add).then_inc(mask_ready, 1)
                dve.wait_ge(mask_ready, turn(mask_ready))

            def route(l):
                E, M = EXPERTS[l], MOE[l]
                r = route_work(l)
                if l < 2:
                    dve.wait_ge(score_ready, turn(score_ready))
                    score = route_score(l)
                    then(tt(r["sel"], score, rb[:, :].unsqueeze(1).broadcast_to([P, TT, 16]), ALU.add))
                    g = r["sel"].rearrange("p t (g e) -> p (t g) e", g=GROUPS)
                    s6 = r["sums"]
                    for first, n, at in ((0, 3, 0), (1, 2, 3), (2, 1, 5)):
                        then(tt(s6[:, :, at:at + n], g[:, :, first + 1:4],
                                g[:, :, first:first + 1].broadcast_to([P, TT * GROUPS, n]), ALU.add))
                    then(nc.vector.memset(r["g8"], FAR))
                    then(nc.vector.tensor_reduce(r["g8"][:, :, 0:GROUPS], s6.rearrange("p (t g) s -> p t g s", t=TT),
                                                 AX.X, ALU.max))
                    pick_group(r["g8"], r["best"], r["index"], r["number"])
                    choose(l, r["sel"], r["number"])
                    mask = route_mask(l)
                    gate = r["gate"]
                    then(tt(gate, mask, score, ALU.mult))
                    then(nc.vector.tensor_reduce(r["total"], gate, AX.X, ALU.add))
                    then(nc.vector.reciprocal(r["inv"], r["total"]))
                    then(tt(gate, gate, r["inv"].unsqueeze(2).broadcast_to([P, TT, E]), ALU.mult))
                else:
                    dve.wait_ge(logits_ps, 3)
                    lg = r["logits"]
                    then(tt(lg, b[6][:, 0:TT * 36].rearrange("p (t e) -> p t e", t=TT),
                            rb2[:, :].unsqueeze(1).broadcast_to([P, TT, 36]), ALU.add))
                    then(nc.vector.memset(r["g8"], FAR))
                    then(nc.vector.tensor_copy(r["g8"][:, :, 0:GROUPS], lg[:, :, 0:GROUPS]))
                    pick_group(r["g8"], r["best"], r["index"], r["number"])
                    then(tt(route_gap[:, :, 0:GROUPS], lg[:, :, 0:GROUPS],
                            r["best"][:, :, 0:1].broadcast_to([P, TT, GROUPS]), ALU.subtract))
                    choose(l, lg[:, :, GROUPS:36], r["number"])
                    tt(route_gap[:, :, 4:5], r["best"][:, :, 1:2], r["best"][:, :, 0:1], ALU.subtract).then_inc(gap_ready, 1)
                    dve.wait_ge(gap_exp, 1)
                    then(nc.vector.tensor_reduce(r["total"], route_gap_exp[:, :, 0:GROUPS], AX.X, ALU.add))
                    e1 = route_gap_exp[:, :, 4:5]
                    total = r["total"].unsqueeze(2)
                    then(stt(total, e1, 1.0, total, ALU.add, ALU.mult))
                    then(nc.vector.reciprocal(r["inv"], r["total"]))
                    then(tt(r["inv1"].unsqueeze(2), r["inv"].unsqueeze(2), e1, ALU.mult))
                    gate = r["gate"]
                    then(tt(gate, r["hot"][0], r["inv"].unsqueeze(2).broadcast_to([P, TT, E]), ALU.mult))
                    then(tt(r["hot"][1], r["hot"][1], r["inv1"].unsqueeze(2).broadcast_to([P, TT, E]), ALU.mult))
                    then(tt(gate, gate, r["hot"][1], ALU.add))
                dve.wait_ge(rank_ps, turn(rank_ps))
                last = ROUNDS * E
                then(stt(r["masked"], b[7][:, 0:TT * E].rearrange("p (t e) -> p t e", t=TT), 1.0, route_mask(l),
                         ALU.add, ALU.mult))
                nc.vector.memset(slot_of[:, :, last:last + 2], -1.0).then_inc(M["hid_ready"], 2)
                nc.vector.memset(gate_of[:, :, last:last + 2], 0.0).then_inc(M["added"], 4)
                for n in range(ROUNDS):
                    ts(slot_of[:, :, n * E:(n + 1) * E], r["masked"], -1.0 - SLOTS * n, None, ALU.add)
                    then(nc.vector.tensor_copy(gate_of[:, :, n * E:(n + 1) * E], gate))
                then(nc.vector.tensor_reduce(r["most"], b[7][:, TT * E:(TT + 1) * E], AX.X, ALU.max))
                then(ts(r["steps"], K(C_IOTA + 1, ROUNDS - 1), float(SLOTS), None, ALU.mult))
                then(ts(r["steps"], r["steps"], r["most"], None, ALU.is_lt))
                then(nc.vector.tensor_reduce(r["most"], r["steps"], AX.X, ALU.add))
                then(nc.vector.tensor_copy(nit[:, 1:2], r["most"]))
                ts(nit[:, 0:1], r["most"], E / 2.0, E / 2.0, ALU.mult, ALU.add).then_inc(n_ready, 1)

            def experts(l):
                M = MOE[l]
                iota = K(C_IOTA, SLOTS).unsqueeze(1).unsqueeze(1).broadcast_to([P, TT, 2, SLOTS])
                as4 = lambda a: a.rearrange("p t (a s) -> p t a s", a=2)

                def pick_pair(at):
                    tt(as4(pick), iota, slot_of[:, :, at].unsqueeze(3).broadcast_to([P, TT, 2, SLOTS]),
                       ALU.is_equal).then_inc(M["pick_ready"], 1)

                def gate_pair(at):
                    tt(as4(pick_g), as4(pick), gate_of[:, :, at].unsqueeze(3).broadcast_to([P, TT, 2, SLOTS]),
                       ALU.mult).then_inc(M["pickg_ready"], 1)

                dve.wait_ge(n_ready, l + 1)
                n = dve.value_load(nit[0:1, 0:1], min_val=1, max_val=ROUNDS * EXPERTS[l] // 2)
                pick_pair(slice(0, 2))
                dve.wait_ge(M["pick_ready"], 1)
                gate_pair(slice(0, 2))
                dve.wait_ge(M["gather_ps"], 1)
                nc.vector.tensor_copy(x_sel[:, 4:6, :], b[1][:, 0:2 * P].rearrange("p (k s) -> p k s", k=2)
                                      ).then_inc(M["y_b"], 1)
                nc.vector.tensor_copy(x_sel[:, 6:8, :], b[1][:, 2 * P:4 * P].rearrange("p (k s) -> p k s", k=2)
                                      ).then_inc(M["sel_b"], 1)
                with dve.Fori(0, n) as i:
                    nxt = bass.ds(2 * i + 2, 2)
                    dve.wait_ge(M["silu_ready"], 2 * i + 1)
                    tt(hid[:, 0, :], gate_act[:, 0, :], b[2][:, 256:512], ALU.mult).then_inc(M["hid_ready"], 1)
                    dve.wait_ge(M["gather_ps"], i + 1)
                    pick_pair(nxt)
                    dve.wait_ge(M["silu_ready"], 2 * i + 2)
                    tt(hid[:, 1, :], gate_act[:, 1, :], b[3][:, 256:512], ALU.mult).then_inc(M["hid_ready"], 1)
                    dve.wait_ge(M["gate_turned"], i + 1)
                    dve.wait_ge(M["pick_ready"], i + 2)
                    gate_pair(nxt)
                    dve.wait_ge(M["gather_ps"], i + 2)
                    nc.vector.tensor_copy(x_sel[:, 4:8, :], b[1].rearrange("p (k s) -> p k s", k=4)).then_inc(M["sel_b"], 1)
                    dve.wait_ge(M["down_ps"], 2 * i + 2)
                    nc.vector.tensor_copy(y_sel[:, 512:1024], b[5]).then_inc(M["y_b"], 1)
                    for r in range(4):
                        dve.wait_ge(M["comb_ps"], 4 * i + r + 1)
                        for k in range(2):
                            c = 2 * r + k
                            last = stt(xT[:, c, :], b[6 + r % 2][:, k * S:(k + 1) * S], mod[:, l, G2 + c:G2 + c + 1],
                                       xT[:, c, :], ALU.mult, ALU.add)
                        last.then_inc(M["added"], 1)

            def hybrid():
                norm(xT[:, :, :], 0, gain1[:, 2, :], mod[:, 2, SH1:SH1 + KT])
                norm(cT, S, gainc, modc[:, SH1:SH1 + KT])
                dve.wait_ge(in_ready, 4)
                by_head = lambda a: a.rearrange("p t (h d) -> p (t h) d", d=HEAD)
                then(tt(vm_sq, vm, vm, ALU.mult))
                nc.vector.tensor_reduce(vm_stat[:, 0:8], by_head(vm_sq), AX.X, ALU.add).then_inc(vm_sums, 1)
                dve.wait_ge(vm_rt, 1)
                then(nc.vector.reciprocal(vm_stat[:, 16:24], vm_stat[:, 8:16]))
                tt(by_head(vm), by_head(vm), vm_stat[:, 16:24].unsqueeze(2).broadcast_to([P, 8, HEAD]),
                   ALU.mult).then_inc(vm_ready, 1)
                dve.wait_ge(mix_ps, 1)
                tt(ymix[:, 0:2, :], uT, b[5].rearrange("p (j t) -> p j t", j=2), ALU.mult).then_inc(ymix_ready, 1)
                dve.wait_ge(rt_ready, turn(rt_ready, 2))
                then(nc.vector.reciprocal(sq[0:32, 6 * S:8 * S], sq[0:32, 6 * S:8 * S]))
                nc.vector.reciprocal(rstd[0:32, :], rt[0:32, :]).then_inc(rs_ready, 1)
                two = lambda a: a.rearrange("p (j t) -> p j t", j=2)
                for g in range(3):
                    dve.wait_ge(bc_ps, turn(bc_ps))
                    if g < 2:
                        last = stt(q2[:, 2 * g:2 * g + 2, :], q2[:, 2 * g:2 * g + 2, :], qscale[:, 2:3], two(b[g]),
                                   ALU.mult, ALU.mult)
                    else:
                        last = stt(k2, k2, vec[:, GAIN_K2:GAIN_K2 + 1], b[2], ALU.mult, ALU.mult)
                    last.then_inc(norm_ready, 1)
                dve.wait_ge(norm_ready, turn(norm_ready, 16 + 8 + 16 + 3))
                for g in range(3):
                    dve.wait_ge(bc_ps, turn(bc_ps))
                    n = 2 if g < 2 else 1
                    a = q2[:, 2 * g:2 * g + 2, :] if g < 2 else k2[:, 0:S].unsqueeze(1)
                    rot = b[g][:, 0:n * S].rearrange("p (j t) -> p j t", j=n)
                    tmp = sq[:, 0:n * S].rearrange("p (j t) -> p j t", j=n)
                    table = lambda at: K(at, S).unsqueeze(1).broadcast_to([P, n, S])
                    then(tt(tmp, rot, table(C_SIN), ALU.mult))
                    then(tt(a, a, table(C_COS), ALU.mult))
                    tt(a, a, tmp, ALU.add).then_inc(norm_ready, 1)
                    dve.wait_ge(norm_ready, turn(norm_ready))

                for g in range(2):
                    dve.wait_ge(bc_ps, turn(bc_ps))
                    nc.vector.tensor_copy(kd[:, g, :], b[2 + g]).then_inc(norm_ready, 1)

                def maxima(u):
                    dve.wait_ge(scores_ps, turn(scores_ps))
                    then(nc.vector.tensor_reduce(stat[:, u % 2, 4:5], b[u % 2], AX.X, ALU.max))
                    ts(stat[:, u % 2, 0:1], stat[:, u % 2, 4:5], -1.0, None, ALU.mult).then_inc(max_ready, 1)

                maxima(0)
                for u in range(16):
                    if u < 15:
                        maxima(u + 1)
                    dve.wait_ge(exp_ready, turn(exp_ready))
                    then(nc.vector.reciprocal(stat[:, u % 2, 6:7], stat[:, u % 2, 2:3]))
                    ts(p2[:, u % 2, :], p2[:, u % 2, :], stat[:, u % 2, 6:7], None, ALU.mult).then_inc(prob_ready, 1)
                dve.wait_ge(ln_ready, 1)
                z8 = z.rearrange("p a b (h t) -> p (a b h) t", h=2)
                l8 = sq[:, :].rearrange("p (n t) -> p n t", n=8)
                then(stt(nlk, z8, 0.0, l8, ALU.max, ALU.add))
                then(stt(z8, z8, 0.0, l8, ALU.min, ALU.subtract))
                one = cst[:, C_ONE:C_ONE + 1].broadcast_to([P, S])
                then(nc.vector.memset(bpad[:, 0, :, 0:1], 0.0))
                then(nc.vector.memset(bpad[:, 1, :, S:S + 1], 0.0))
                then(nc.vector.memset(epad[:, 0, :, S:S + 1], 0.0))
                then(nc.vector.memset(epad[:, 1, :, 0:1], 0.0))
                for hp in range(2):
                    scan = nc.vector.tensor_tensor_scan
                    then(scan(bpad[:, 0, hp, 1:S + 1], one, z[:, 0, hp, 0:S], 0.0, ALU.mult, ALU.add))
                    then(scan(bpad[:, 1, hp, S - 1::-1], one, z[:, 1, hp, S - 1::-1], 0.0, ALU.mult, ALU.add))
                    then(scan(epad[:, 0, hp, S - 1::-1], one, z[:, 0, hp, 2 * S - 1:S - 1:-1], 0.0, ALU.mult, ALU.add))
                    then(scan(epad[:, 1, hp, 1:S + 1], one, z[:, 1, hp, S:2 * S], 0.0, ALU.mult, ALU.add))
                nlk5 = nlk.rearrange("p (a b h) t -> p a b h t", a=2, b=2)
                for d in range(2):
                    bx = bpad[:, d, :, 1:S + 1] if d == 0 else bpad[:, d, :, 0:S]
                    ex = epad[:, d, :, 1:S + 1] if d == 0 else epad[:, d, :, 0:S]
                    r0_ = ref_col(d, 0)
                    ref = bpad[:, d, :, r0_:r0_ + 15 * SUB + 1:SUB].unsqueeze(3).broadcast_to([P, 2, NSUB, SUB])
                    sub = lambda a: a.rearrange("p b (j t) -> p b j t", t=SUB)
                    then(tt(sub(bsub[:, d]), sub(bx), ref, ALU.subtract))
                    then(stt(lks[:, d], nlk5[:, d, :, 0, :], -1.0, bsub[:, d], ALU.mult, ALU.subtract))
                    xk, ck = (slice(S, 2 * S), slice(0, S)) if d == 0 else (slice(0, S), slice(S, 2 * S))
                    then(stt(LK[:, d, :, xk], nlk5[:, d, :, 0, :], -1.0, bx, ALU.mult, ALU.subtract))
                    last = tt(LK[:, d, :, ck], ex, nlk5[:, d, :, 1, :], ALU.subtract)
                    if d == 0:
                        then(last)
                    else:
                        last.then_inc(log_ready, 1)
                dve.wait_ge(qdec_ready, 1)
                then(tt(qq, qq, qh.unsqueeze(1).broadcast_to([P, 2, 2, S]), ALU.mult))

                def args(q):
                    d, i = divmod(q, SUB)
                    if q >= 4:
                        dve.wait_ge(sc_ps, q - 3)
                    pr = prod_of(q)
                    seen = seen_by(d, i)
                    key = lks[:, d].rearrange("p b (j t) -> p (b j) t", t=SUB)[:, :, i:i + 1]
                    tt(pr, bsub[:, d].rearrange("p b (j t) -> p (b j) t", t=SUB)[:, :, seen],
                       key.broadcast_to([P, 2 * NSUB, seen.stop - seen.start]), ALU.add).then_inc(arg_ready, 1)

                args(0)
                args(1)
                for q in range(2 * SUB):
                    d, i = divmod(q, SUB)
                    if q + 2 < 2 * SUB:
                        args(q + 2)
                    dve.wait_ge(prod_exp, q + 1)
                    pr = prod_of(q)
                    tt(pr, pr, qh.rearrange("p b (j t) -> p (b j) t", t=SUB)[:, :, seen_by(d, i)],
                       ALU.mult).then_inc(prod_ready, 1)
                dve.wait_ge(sc_ready, 1)
                for w, (hp, d) in enumerate(UNITS):
                    if w >= 1:
                        dve.wait_ge(dm_ps, w)
                    own = sc.rearrange("p a b -> p (a b)")[:, (d * 2 + hp) * 64:(d * 2 + hp + 1) * 64]
                    own = own.rearrange("p (n s) -> p n s", n=4).unsqueeze(2).broadcast_to([P, 4, P // SUB, SUB])
                    mask = K(C_DIAG + P * d).rearrange("p (j s) -> p j s", s=SUB).unsqueeze(1).broadcast_to([P, 4, P // SUB, SUB])
                    tt(dm.rearrange("p n (j s) -> p n j s", s=SUB), own, mask, ALU.mult).then_inc(dm_ready, 1)
                    dve.wait_ge(dm_ps, w + 1)
                    dve.wait_ge(sT_ready, w + 1)
                    for n in range(4):
                        t, m = divmod(n, 2)
                        kt = t + 2 if d == 0 else t
                        last = tt(sT[:, m, kt, cols(t)], sT[:, m, kt, cols(t)], b[6][:, cols(n)], ALU.add)
                    last.then_inc(sT_full, 1)
                head_norms(32)
                dve.wait_ge(bc_ps, turn(bc_ps))
                then(stt(o2, o2, vec[:, GAIN_O2:GAIN_O2 + 1], b[5].rearrange("p (j t) -> p j t", j=2), ALU.mult, ALU.mult))
                tt(ymix[:, 6:8, :], o2, gs, ALU.mult).then_inc(ymix_ready, 1)

            nc.vector.memset(eps[:, :], EPS).then_inc(eps_ready, 1)
            dve.wait_ge(const_in, 16 * len(const_loads))
            lam4 = lamrow.rearrange("p (n two d) -> p n two d", n=2, two=2)
            then(tt(lamtmp[:, 0:2 * HEAD].rearrange("p (n d) -> p n d", n=2), lam4[:, :, 0, :], lam4[:, :, 1, :], ALU.mult))
            nc.vector.tensor_reduce(lamtmp[:, 128:130], lamtmp[:, 0:2 * HEAD].rearrange("p (n d) -> p n d", n=2),
                                    AX.X, ALU.add).then_inc(lam_sums, 1)
            dve.wait_ge(vec_ps, 1)
            nc.vector.tensor_copy(vec[:, :], b[0][:, 0:N_VEC]).then_inc(vec_ready, 1)
            dve.wait_ge(lam_exp, 1)
            tt(lamtmp[:, 132:133], lamtmp[:, 131:132], lamtmp[:, 130:131], ALU.subtract).then_inc(lam_diff, 1)
            dve.wait_ge(vec_ready, 1)
            for n, (g, f) in enumerate(((GAIN_AQ, HEAD ** -0.5), (GAIN_BQ, HEAD ** -0.5), (GAIN_Q2, HEAD ** -0.5),
                                        (GAIN_SUB, 1.0 - LAMBDA_INIT))):
                then(ts(qscale[:, n:n + 1], vec[:, g:g + 1], f, None, ALU.mult))
            dve.wait_ge(lam_bc, 1)
            ts(nlam[:, :], b[6][:, 0:1], -LAMBDA_INIT, None, ALU.add).then_inc(lam_ready, 1)
            dve.wait_ge(lam_ready, 1)
            finish_mod(0)
            for l in range(2):
                norm(xT[:, :, :], 0, gain1[:, l, :], mod[:, l, SH1:SH1 + KT])
                qkv(l)
                attention(l)
                add_out(l)
                norm(xT[:, :, :], 0, gain2[:, l, :], mod[:, l, SH2:SH2 + KT])
                route(l)
                experts(l)
            hybrid()
            add_out(2)
            norm(xT[:, :, :], 0, gain2[:, 2, :], mod[:, 2, SH2:SH2 + KT])
            route(2)
            experts(2)


_OUTS = [((1, S, D), "float32")]
_INS = ["x", "c", "ada_w", "ada_b", "norm_mix_g", "norm_ffn_g", "t5_bias", "a_w_qkv", "a_q_gain", "a_k_gain",
        "a_lambda", "a_subln_g", "a_w_o", "b_w_qkv", "b_q_gain", "b_k_gain", "b_rel_bias", "b_w_o", "router_w",
        "router_bias", "moe_w_gate", "moe_w_up", "moe_w_down", "c_2", "ctx_2", "c_ctx_2", "w_mod_2", "b_mod_2",
        "norm1_w_2", "w_in_2", "w_s_2", "b_s_2", "q_norm_w_2", "k_norm_w_2", "hgrn_lb_logits_2", "hgrn_norm_w_2",
        "w_out_2", "norm2_w_2", "w_grp_2", "b_grp_2", "w_exp_2", "b_exp_2", "w1_2", "w3_2", "w2_2"]


def kernel(**inputs):
    import concourse.bacc as bacc
    from concourse.bass_utils import run_bass_kernel_spmd

    nc = bacc.Bacc("TRN2", target_bir_lowering=False, num_devices=1)
    arrays, args = {}, []
    named = [(n, np.ascontiguousarray(inputs[n])) for n in _INS]
    named += list(zip(("const", "const2", "bucket"), constants()))
    for name, a in named:
        arrays[f"in_{name}_dram"] = a
        args.append(nc.dram_tensor(f"in_{name}_dram", a.shape, mybir.dt.from_np(a.dtype), kind="ExternalInput").ap())
    for i, (shape, dtype) in enumerate(_OUTS):
        args.append(nc.dram_tensor(f"out_{i}_dram", shape, mybir.dt.from_np(np.dtype(dtype)), kind="ExternalOutput").ap())
    program(nc, *args)
    r = run_bass_kernel_spmd(nc, [arrays], core_ids=[0])
    return r.results[0]["out_0_dram"]
```

```python
from contextlib import ExitStack
import math

import numpy as np
import concourse.bass as bass
from concourse import mybir

F32 = mybir.dt.float32
I32 = mybir.dt.int32
U32 = mybir.dt.uint32
ALU = mybir.AluOpType
ACT = mybir.ActivationFunctionType
AX = mybir.AxisListType

P = 128
D = 1024
KT = D // P
S = 256
TT = S // P
FF = 512
FT = FF // P
CHUNK = 512
NSLOT = 6
SLOTS = 64
ROUNDS = S // SLOTS
HEAD = 64
EPS = 1e-6
NEG = -1e30
FAR = -3e38
LAMBDA_INIT = 0.8 - 0.6 * math.exp(-0.3 * 0)
SUB = 16
NSUB = S // SUB
N_COND = 3
N_MOD = 6 * KT
SH1, SC1, G1, SH2, SC2, G2 = (KT * n for n in range(6))
EXPERTS = (16, 16, 32)
GROUPS = 4

V_ADA = (0, 48, 128)
V_C, V_NORM1 = 96, 120
V_MIX, V_FFN = (176, 184, V_NORM1), (192, 200, 208)
V_GAIN = 216
GAIN_AQ, GAIN_AK, GAIN_BQ, GAIN_BK, GAIN_Q2, GAIN_K2, GAIN_O2, GAIN_SUB = range(V_GAIN, V_GAIN + 8)
N_VEC = V_GAIN + 8

C_ID, C_FLIP, C_TRI, C_ONE = 0, 128, 256, 384
C_SEL = 512
C_SEL8 = C_SEL + 512
C_IOTA = C_SEL8 + 128
C_COS, C_SIN = C_IOTA + 64, C_IOTA + 64 + 256
C_ROT = C_SIN + 256
C_DIAG = C_ROT + 128
C_DUP = C_DIAG + 256
C_MOD = C_DUP + 256
N_CST = C_MOD + 4
C2_SPREAD = 0
N_CST2 = 16 * P


def constants():
    c = np.zeros((P, N_CST), np.float32)
    p = np.arange(P)
    c[:, C_ID:C_ID + P] = np.eye(P)
    c[:, C_FLIP:C_FLIP + P] = np.eye(P)[::-1]
    c[:, C_TRI:C_TRI + P] = p[:, None] < p[None, :]
    c[:, C_ONE:C_ONE + P] = 1.0
    c2 = np.zeros((32, N_CST2), np.float32)
    for sl in range(16):
        c[p, C_SEL + 32 * sl + 2 * sl + p // HEAD] = 1.0
        c2[2 * sl + p // HEAD, C2_SPREAD + P * sl + p] = 1.0
    for h in range(8):
        c[:, C_SEL8 + 16 * h + 2 * h:C_SEL8 + 16 * h + 2 * h + 2] = 1.0
    c[:, C_IOTA:C_IOTA + 64] = np.arange(64)
    t = np.arange(S)
    inv = (1.0 / (np.float32(10000.0) ** (np.arange(0, 32, 2, dtype=np.float32) / np.float32(32)))).astype(np.float32)
    ang = np.stack([(t // 64).astype(np.float32)[:, None] * inv, (t % 64).astype(np.float32)[:, None] * inv], 1)
    d = p % HEAD
    c[:, C_COS:C_COS + S] = np.cos(ang)[:, d // 32, d % 16].T
    c[:, C_SIN:C_SIN + S] = np.sin(ang)[:, d // 32, d % 16].T
    for m in range(P):
        if (m % 32) < 16:
            c[m + 16, C_ROT + m] = -1.0
        else:
            c[m - 16, C_ROT + m] = 1.0
    same = p[:, None] // SUB == p[None, :] // SUB
    c[:, C_DIAG:C_DIAG + P] = same & (p[None, :] <= p[:, None])
    c[:, C_DIAG + P:C_DIAG + 2 * P] = same & (p[None, :] >= p[:, None])
    for g in range(2):
        c[g * HEAD + p % HEAD, C_DUP + P * g + p] = 1.0
    for cond in range(N_COND):
        c[cond::32, C_MOD + cond] = 1.0
    rel = np.arange(512) - 255
    n = np.abs(rel)
    far = 8 + (np.log(np.maximum(n, 1).astype(np.float32) / np.float32(8)) / np.float32(math.log(1024 / 8))
               * np.float32(8)).astype(np.int32)
    bucket = np.where(rel > 0, 16, 0) + np.where(n < 8, n, np.minimum(far, 15))
    onehot = (np.arange(32)[:, None] == bucket[None, :]).astype(np.float32)
    return c, c2, onehot


def make_turn():
    at = {}

    def turn(sem, n=1):
        at[sem.name] = at.get(sem.name, 0) + n
        return at[sem.name]

    return turn


def program(nc, x, c, ada_w, ada_b, norm_mix_g, norm_ffn_g, t5_bias, a_w_qkv, a_q_gain, a_k_gain, a_lambda,
            a_subln_g, a_w_o, b_w_qkv, b_q_gain, b_k_gain, b_rel_bias, b_w_o, router_w, router_bias,
            moe_w_gate, moe_w_up, moe_w_down, c_2, ctx_2, c_ctx_2, w_mod_2, b_mod_2, norm1_w_2, w_in_2,
            w_s_2, b_s_2, q_norm_w_2, k_norm_w_2, hgrn_lb_logits_2, hgrn_norm_w_2, w_out_2, norm2_w_2,
            w_grp_2, b_grp_2, w_exp_2, b_exp_2, w1_2, w3_2, w2_2, cst_d, cst2_d, bucket_d, out):
    with ExitStack() as ctx:
        def sb(name, shape, dt=F32):
            return ctx.enter_context(nc.sbuf_tensor(name, shape, dt))

        def sem(name):
            return ctx.enter_context(nc.semaphore(name))

        ring = [sb(f"ring{s}", [P, KT * CHUNK]) for s in range(NSLOT)]
        xT = sb("xT", [P, KT, S])
        hh = sb("hh", [P, KT, 2 * S])
        sq = sb("sq", [P, KT * S])
        cst, cst2 = sb("cst", [P, N_CST]), sb("cst2", [32, N_CST2])
        vec = sb("vec", [P, N_VEC])
        csil = sb("csil", [P, KT, 32])
        modrow = sb("modrow", [P, CHUNK])
        mod = sb("mod", [P, 3, N_MOD])
        modc = sb("modc", [P, 2 * KT])
        gain1, gain2 = sb("gain1", [P, 3, KT]), sb("gain2", [P, 3, KT])
        gainc = sb("gainc", [P, KT])
        qscale = sb("qscale", [P, 4])
        rt, rstd = sb("rt", [P, S]), sb("rstd", [P, S])
        rw, rb = sb("rw", [P, KT, 16]), sb("rb", [P, 16])
        rw2, rb2 = sb("rw2", [P, KT, 36]), sb("rb2", [P, 36])
        eps = sb("eps", [P, 1])
        nlam = sb("nlam", [P, 1])
        stat = sb("stat", [P, 2, 8])
        nit = sb("nit", [P, 2], I32)
        arena = sb("arena", [P, 13448])

        def view(at, *shape):
            n = int(np.prod(shape))
            v = arena[:, at:at + n]
            if len(shape) == 2:
                v = v.rearrange("p (a b) -> p a b", a=shape[0])
            elif len(shape) == 3:
                v = v.rearrange("p (a b c) -> p a b c", a=shape[0], b=shape[1])
            elif len(shape) == 4:
                v = v.rearrange("p (a b c d) -> p a b c d", a=shape[0], b=shape[1], c=shape[2])
            return v

        vecrow = view(0, 2, P)
        t5row = arena[0:8, 256:768]
        lamrow = arena[0:1, 768:1024]
        lamtmp = arena[0:1, 1024:1160]
        bucket = arena[0:32, 1160:1672]
        t5b = arena[0:32, 1672:1680]
        raw = view(0, 16, S)
        v_tok = view(4096, TT, D)
        bias = view(6144, 16, S)
        s_sb = view(10240, 2, 2, S)
        prob = view(11264, 2, 2, S)
        probT = view(12288, 2, 2, S)
        h_tok = view(0, TT, D)
        x_sel = view(2048, KT, 2 * SLOTS)
        hid, hidT = view(3072, FF), view(3584, FT, 2 * SLOTS)
        gate_act = sq[:, 0:FF]
        y_sel = view(4096, D)
        pick = view(5120, TT, 2 * SLOTS)
        pick_g = view(5376, TT, 2 * SLOTS)
        spread_g = view(5632, S)
        slot_of, gate_of = view(5888, TT, 130), view(6148, TT, 130)
        r0 = 6408
        ctx_tok = view(7300, TT, D)
        ws = view(9348, 4, P)
        bs = arena[0:1, 9860:10372]
        cT = view(10372, KT, S)
        uT, vm = view(0, 2, S), view(512, TT, S)
        q2, k2, vb = view(1024, 4, S), view(2048, 512), view(2560, 4, P)
        wsT = view(3072, 4, P)
        p2, pT2 = view(3584, 2, 512), view(4608, 4, S)
        qh, vh, gs = view(5632, 2, S), view(6144, 4, S), view(7168, 2, S)
        z = view(11400, 2, 2, 2 * S)
        bpad, epad = view(0, 2, 2, 257), view(1028, 2, 2, 257)
        bsub, lks, qq = view(2056, 2, 2, S), view(3080, 2, 2, S), view(4104, 2, 2, S)
        sc, dm = view(5128, 2, P), view(10752, 4, P)
        kk, sT = view(7680, 2, 512), view(8704, 2, 4, S)
        kd = view(7680, 2, 512)
        o2, osq = view(7680, 2, S), view(8192, 2, S)
        LK = z
        nlk = hh[:, :, S:2 * S]
        lnb = sq[:, :].rearrange("p (a b c) -> p a b c", a=2, b=2)
        oT = hh[:, :, S:2 * S]
        ymix = hh[:, :, 0:S]

        def K(at, n=P, rows=P):
            return cst[0:rows, at:at + n]

        ident, ones = K(C_ID), K(C_ONE)
        bank = [ctx.enter_context(nc.psum_tensor(f"bank{i}", [P, 512], F32)) for i in range(2)]
        pair = [ctx.enter_context(nc.psum_tensor(f"pair{i}", [P, 2, 512], F32)) for i in range(2)]
        b = [bank[0][:, :], bank[1][:, :], pair[0][:, 0, :], pair[0][:, 1, :], pair[1][:, 0, :], pair[1][:, 1, :]]
        bank6 = ctx.enter_context(nc.psum_tensor("bank6", [P, 512], F32))
        bank7 = ctx.enter_context(nc.psum_tensor("bank7", [P, 512], F32))
        b += [bank6[:, :], bank7[:, :]]
        t5_dram = nc.dram_tensor("t5_rows", (8, 512), F32, kind="Internal").ap()

        const_in, x_in = sem("const_in"), sem("x_in")
        t5_row, t5_out, bias_in = sem("t5_row"), sem("t5_out"), sem("bias_in")
        l2_in, out_done = sem("l2_in"), sem("out_done")
        full = [sem(f"slot_full{s}") for s in range(NSLOT)]
        dve_step, act_step = sem("dve_step"), sem("act_step")
        eps_ready, turned, vec_ready, csil_ready = sem("eps_ready"), sem("turned"), sem("vec_ready"), sem("csil_ready")
        x_ready, mod_rows, modrow_ready = sem("x_ready"), sem("mod_rows"), sem("modrow_ready")
        mod_cols, mod_ready = sem("mod_cols"), sem("mod_ready")
        lam_sums, lam_exp, lam_diff, lam_bc, lam_ready = (sem(n) for n in ("lam_sums", "lam_exp", "lam_diff", "lam_bc", "lam_ready"))
        t5_ps = sem("t5_ps")
        sq_ready, ssq_ps, rt_ready, h_ready = sem("sq_ready"), sem("ssq_ps"), sem("rt_ready"), sem("h_ready")
        qk_proj, raw_ready, rs_ready, bc_ps, norm_ready = (sem(n) for n in ("qk_proj", "raw_ready", "rs_ready", "bc_ps", "norm_ready"))
        v_proj, v_ready, flip_ps, bias_ready = (sem(n) for n in ("v_proj", "v_ready", "flip_ps", "bias_ready"))
        scores_ps, s_added, max_ready, exp_ready, prob_ready = (sem(n) for n in ("scores_ps", "s_added", "max_ready", "exp_ready", "prob_ready"))
        turn_ps, probT_ready, pv_ps, o_ready = (sem(n) for n in ("turn_ps", "probT_ready", "pv_ps", "o_ready"))
        out_proj, x_attn = sem("out_proj"), sem("x_attn")
        logits_ps, h_turned, h_tok_ready = sem("logits_ps"), sem("h_turned"), sem("h_tok_ready")
        score_ready, mask_ready, rank_ps, n_ready = (sem(n) for n in ("score_ready", "mask_ready", "rank_ps", "n_ready"))
        in_proj, in_ready = sem("in_proj"), sem("in_ready")
        vm_ready, mix_ps, ymix_ready = sem("vm_ready"), sem("mix_ps"), sem("ymix_ready")
        prod_ready, sc_ps, sc_ready, dm_ready = (sem(n) for n in ("prod_ready", "sc_ps", "sc_ready", "dm_ready"))
        kk_zero, kk_ready, off_ps, sT_ready, sT_full = (sem(n) for n in ("kk_zero", "kk_ready", "off_ps", "sT_ready", "sT_full"))
        arg_ready, prod_exp = sem("arg_ready"), sem("prod_exp")
        gap_ready, gap_exp = sem("gap_ready"), sem("gap_exp")
        vec_ps, ws_ready, vm_sums, vm_rt = sem("vec_ps"), sem("ws_ready"), sem("vm_sums"), sem("vm_rt")
        dm_ps, ln_ready, log_ready, qdec_ready = sem("dm_ps"), sem("ln_ready"), sem("log_ready"), sem("qdec_ready")
        out_tok = sem("out_tok")
        MOE = []
        for l in range(3):
            MOE.append({n: sem(f"{n}_{l}") for n in (
                "pick_ready", "pickg_ready", "gather_a", "gather_b", "sel_a", "sel_b", "gate_ps", "silu_ready", "up_ps",
                "hid_ready", "hid_turned", "hidT_ready", "gate_turned", "down_a", "down_b", "y_a", "y_b",
                "comb_ps", "added")})
            MOE[l]["done"] = (MOE[l]["gate_ps"], MOE[l]["up_ps"], MOE[l]["down_b"])
            MOE[l]["full"] = [sem(f"{n}_full_{l}") for n in ("gate", "up", "down")]

        def columns(w, n):
            return w[:, n * CHUNK:(n + 1) * CHUNK].rearrange("(k p) n -> p k n", p=P)

        MOD_W = (ada_w[0], ada_w[1], w_mod_2[0])
        QKV, W_O = (a_w_qkv[0], b_w_qkv[0], w_in_2[0]), (a_w_o[0], b_w_o[0], w_out_2[0])
        GATE_W = (moe_w_gate[0], moe_w_gate[1], w1_2[0])
        UP_W = (moe_w_up[0], moe_w_up[1], w3_2[0])
        DOWN_W = (moe_w_down[0], moe_w_down[1], w2_2[0])
        IN_PARTS = [["u0", "u1", "vm0", "vm1"], ["q0", "q1", "q2", "q3"],
                    ["k", "vb0", "vb1", "vb2", "vb3", "qh0", "qh1"], ["zf0", "zf1", "zb0", "zb1"],
                    ["vh0", "vh1", "vh2", "vh3", "g0", "g1"]]
        chunks = []

        MOD_START = range(0, 4)
        MOD_QK, MOD_ATTN = (range(4, 12), range(20, 28)), (range(12, 20), range(28, 36))

        def add_mod(g):
            chunks.append((columns(MOD_W[g // 12], g % 12), mod_rows, g + 1))
            mod_at[g] = len(chunks) - 1

        def add_out(l):
            for n in range(2):
                chunks.append((columns(W_O[l], n), out_proj, 8 * l + 4 * (n + 1)))

        moe_at, mod_at, qkv_at, out_at = [], {}, [], []
        for g in MOD_START:
            add_mod(g)
        for l in range(2):
            qkv_at.append([])
            for n in range(6):
                qkv_at[l].append(len(chunks))
                if n < 4:
                    chunks.append((columns(QKV[l], n), qk_proj, 16 * l + 4 * (n + 1)))
                    for g in MOD_QK[l][2 * n:2 * n + 2]:
                        add_mod(g)
                else:
                    chunks.append((columns(QKV[l], n), v_proj, 4 * l + 2 * (n - 3)))
            for g in MOD_ATTN[l]:
                add_mod(g)
            out_at.append(len(chunks))
            add_out(l)
            moe_at.append(len(chunks))
        done, in_at = 0, len(chunks)
        for n in range(5):
            done += len(IN_PARTS[n])
            chunks.append((columns(QKV[2], n), in_proj, done))
        out_at.append(len(chunks))
        add_out(2)
        moe_at.append(len(chunks))

        def slot_of_chunk(n):
            return n % NSLOT

        def moe_slot(l, a, m):
            return (moe_at[l] + 2 * m + a) % NSLOT

        const_loads = []

        def const(dst, src):
            const_loads.append((dst, src))

        const(cst[:, :], cst_d)
        const(cst2[:, :], cst2_d)
        const(bucket, bucket_d)
        const(t5b, t5_bias)
        rows = lambda r, n: arena[r % P:r % P + n, (r // P) * P:(r // P + 1) * P]
        as_rows = lambda a: a.rearrange("(r q) -> r q", q=P)
        for l in range(3):
            const(rows(V_ADA[l], 48), as_rows(b_mod_2[0] if l == 2 else ada_b[l]))
        const(rows(V_C, 8), as_rows(c[0]))
        const(rows(V_C + 8, 8), as_rows(c_2[0]))
        const(rows(V_C + 16, 8), as_rows(c_ctx_2))
        const(rows(V_NORM1, 8), as_rows(norm1_w_2[0]))
        for l in range(2):
            const(rows(V_MIX[l], 8), as_rows(norm_mix_g[l]))
            const(rows(V_FFN[l], 8), as_rows(norm_ffn_g[l]))
        const(rows(V_FFN[2], 8), as_rows(norm2_w_2[0]))
        for r, g in ((GAIN_AQ, a_q_gain), (GAIN_AK, a_k_gain), (GAIN_BQ, b_q_gain), (GAIN_BK, b_k_gain),
                     (GAIN_Q2, q_norm_w_2), (GAIN_K2, k_norm_w_2), (GAIN_O2, hgrn_norm_w_2)):
            for half in range(2):
                const(rows(r, 1)[:, half * HEAD:(half + 1) * HEAD], g)
        const(rows(GAIN_SUB, 1), a_subln_g)
        const(lamrow, a_lambda.rearrange("a n d -> a (n d)"))
        const(rw[:, :, :], router_w.rearrange("(k p) e -> p k e", p=P))
        const(rb[:, :], router_bias.partition_broadcast(P))
        const(rw2[:, :, 0:GROUPS], w_grp_2[0].rearrange("(k p) e -> p k e", p=P))
        const(rw2[:, :, GROUPS:36], w_exp_2[0].rearrange("(k p) e -> p k e", p=P))
        const(rb2[:, 0:GROUPS], b_grp_2[0].partition_broadcast(P))
        const(rb2[:, GROUPS:36], b_exp_2[0].partition_broadcast(P))

        block = ctx.enter_context(nc.Block())

        @block.sync
        def _(sp):
            turn = make_turn()
            for dst, src in const_loads:
                sp.dma_start(dst, src, allow_slow_non_contiguous=True).then_inc(const_in, 16)
            sp.dma_start(sq[:, :].rearrange("p (t d) -> p t d", t=TT),
                         x[0].rearrange("(t p) d -> p t d", p=P)).then_inc(x_in, 16)

            def load(n):
                src, _, _ = chunks[n]
                if n >= NSLOT and n - NSLOT not in fenced:
                    _, used, value = chunks[n - NSLOT]
                    sp.wait_ge(used, value)
                k = src.shape[1]
                s = slot_of_chunk(n)
                sp.dma_start(ring[s][:, :].rearrange("p (k n) -> p k n", k=k), src).then_inc(full[s], 16)

            fenced = set()
            more_rounds = [None] * 3

            def expert(l, a, m, e):
                s = moe_slot(l, a, m)
                w = (GATE_W, UP_W, DOWN_W)[m][l]
                src = w[bass.ds(e, 1)].rearrange("a (k p) n -> p (a k) n", p=P)
                sp.dma_start(ring[s][:, :].rearrange("p (k n) -> p k n", k=FT if m == 2 else KT),
                             src).then_inc(MOE[l]["full"][m], 16)

            def load_hybrid():
                sp.wait_ge(x_attn, 16)
                sp.dma_start(ctx_tok, ctx_2[0].rearrange("(t p) d -> p t d", p=P)).then_inc(l2_in, 16)
                sp.dma_start(ws, w_s_2[0].rearrange("h t s -> t h s")).then_inc(l2_in, 16)
                sp.dma_start(bs, b_s_2.rearrange("a h t -> a (h t)")).then_inc(l2_in, 16)

            def experts(l):
                E, M = EXPERTS[l], MOE[l]
                for m in range(3):
                    for a in range(2):
                        n = moe_at[l] + 2 * m + a - NSLOT
                        _, used, value = chunks[n]
                        sp.wait_ge(used, value)
                        expert(l, a, m, a)
                if l == 1:
                    load_hybrid()
                with sp.Fori(1, E // 2) as i:
                    for m in range(3):
                        for a in range(2):
                            sp.wait_ge(M["done"][m], i)
                            expert(l, a, m, 2 * i + a)
                sp.wait_ge(n_ready, turn(n_ready))
                more = sp.value_load(nit[0:1, 1:2], min_val=0, max_val=ROUNDS - 1)
                with sp.If(more > 0):
                    with sp.Fori(0, more) as r:
                        with sp.Fori(0, E // 2) as i:
                            for m in range(3):
                                for a in range(2):
                                    sp.wait_ge(M["done"][m], r * (E // 2) + i + E // 2)
                                    expert(l, a, m, 2 * i + a)
                more_rounds[l] = more

            def after_experts(l, n):
                for k in range(NSLOT):
                    sp.wait_ge(MOE[l]["done"][k // 2], more_rounds[l] * (EXPERTS[l] // 2) + EXPERTS[l] // 2)
                    fenced.add(n + k - NSLOT)
                    load(n + k)

            for n in range(12):
                load(n)
                if n == 0:
                    sp.wait_ge(t5_row, turn(t5_row))
                    sp.dma_start(t5_dram, t5row).then_inc(t5_out, 16)
            sp.wait_ge(t5_out, 16)
            sp.dma_start(bias[:, 0:8, :], bass.AP(t5_dram.tensor, 0, [[1, P], [512, 8], [1, S]])).then_inc(bias_in, 16)
            for n in range(12, moe_at[0]):
                load(n)
            experts(0)
            after_experts(0, moe_at[0])
            sp.wait_ge(MOE[0]["added"], more_rounds[0] * (EXPERTS[0] // 2 * 4) + (EXPERTS[0] // 2 * 4 + 2))
            sp.dma_start(bias[:, :, :], bass.AP(b_rel_bias.tensor, 1, [[1, P], [513, 16], [1, S]])).then_inc(bias_in, 16)
            for n in range(moe_at[0] + NSLOT, moe_at[1]):
                load(n)
            experts(1)
            after_experts(1, moe_at[1])
            for n in range(moe_at[1] + NSLOT, moe_at[2]):
                load(n)
            experts(2)
            for t in range(TT):
                sp.wait_ge(out_tok, 2 * (t + 1))
                sp.dma_start(out[0, t * P:(t + 1) * P, :], sq[:, t * D:(t + 1) * D]).then_inc(out_done, 16)
            sp.wait_ge(out_done, 16 * TT)

        sums = (b[7], b[4])
        R8 = [ring[s][:, :].rearrange("p (k n) -> p k n", k=KT) for s in range(NSLOT)]
        R4 = [ring[s][:, :].rearrange("p (k n) -> p k n", k=FT) for s in range(NSLOT)]

        def cols(t):
            return slice(t * P, (t + 1) * P)

        def half(m):
            return slice(m * HEAD, (m + 1) * HEAD)

        def mod_columns(g):
            l, n = divmod(g, 12)
            width = 2 if l == 2 and n < 4 else 1
            bank = b[0] if any(g in r for r in MOD_ATTN) else b[7]
            return bank[:, 0:4 * width].rearrange("p (n w) -> p n w", w=width), width

        def before(d, j):
            return slice(0, S + SUB * j) if d == 0 else slice(SUB * (j + 1), 2 * S)

        def ref_col(d, j):
            return SUB * j if d == 0 else SUB * (j + 1)

        def key_tiles(d, j):
            if d == 0:
                return (0, 1, 2) if j < NSUB // 2 else (0, 1, 2, 3)
            return (0, 1, 2, 3) if j < NSUB // 2 else (1, 2, 3)

        def seen_by(d, i):
            return slice(i, SUB) if d == 0 else slice(0, i + 1)

        def prod_of(q):
            d, i = divmod(q, SUB)
            buf = sq[:, q % 4 * 512:(q % 4 + 1) * 512]
            return buf.rearrange("p (n t) -> p n t", t=SUB)[:, :, seen_by(d, i)]

        vm_sq, vm_stat = view(3584, TT, S), arena[:, 4096:4120]

        def route_layout(E):
            at, r = r0, {}
            for name, shape in (("score", (TT, 16)), ("sel", (TT, 16)), ("sums", (TT * GROUPS, 6)), ("logits", (TT, 36)),
                                ("g8", (TT, 8)), ("best", (TT, 8)), ("number", (TT, 2)), ("gmask", (TT, GROUPS)),
                                ("masked", (TT, E)), ("fill", (TT, E)), ("hot0", (TT, E)), ("hot1", (TT, E)),
                                ("mask", (TT, E)), ("gate", (TT, E)), ("total", (TT,)), ("inv", (TT,)), ("inv1", (TT,)),
                                ("most", (1,)), ("steps", (ROUNDS - 1,)), ("gap", (TT, 5)), ("gap_exp", (TT, 5))):
                r[name] = view(at, *shape)
                at += int(np.prod(shape))
            r["index"] = arena[:, at:at + TT * 8].bitcast(U32).rearrange("p (t n) -> p t n", t=TT)
            r["hot"] = (r["hot0"], r["hot1"])
            assert at + TT * 8 <= 7300
            return r

        ROUTE = [route_layout(E) for E in EXPERTS]
        route_work = lambda l: ROUTE[l]
        route_mask = lambda l: ROUTE[l]["mask"]
        route_score = lambda l: ROUTE[l]["score"]
        route_gap, route_gap_exp = ROUTE[2]["gap"], ROUTE[2]["gap_exp"]
        UNITS = [(hp, d) for hp in range(2) for d in range(2)]
        PARTS = [(n, part) for n in range(5) for part in IN_PARTS[n]]

        @block.tensor
        def _(pe):
            turn = make_turn()
            mm = nc.tensor.matmul

            def chunk_in(n):
                s = slot_of_chunk(n)
                pe.wait_ge(full[s], turn(full[s], 16))
                return R8[s]

            def mod_products(g, bank):
                w = chunk_in(mod_at[g])
                for k in range(KT):
                    q = slice(k % 4 * 32, k % 4 * 32 + 32)
                    last = mm(bank[q, :], csil[:, k, :], w[:, k, :], start=(k < 4), stop=(k >= KT - 4))
                last.then_inc(mod_rows, 1)

            def mod_turn(g):
                o, width = mod_columns(g)
                pe.wait_ge(modrow_ready, g + 1)
                if g >= 1:
                    pe.wait_ge(mod_ready, g)
                cond = C_MOD + (g // 12 == 2)
                for s4 in range(4):
                    last = mm(o[:, s4, :], modrow[:, cols(s4)], K(cond, width), start=True, stop=True)
                last.then_inc(mod_cols, 1)

            def square_sums():
                pe.wait_ge(sq_ready, turn(sq_ready))
                for k in range(KT):
                    last = mm(b[7][:, 0:S], ones, sq[:, k * S:(k + 1) * S], start=(k == 0), stop=(k == KT - 1))
                last.then_inc(ssq_ps, 1)

            def qkv(l):
                at = qkv_at[l]
                pe.wait_ge(h_ready, turn(h_ready))

                def project(sl):
                    if sl % 4 == 0:
                        project.w = chunk_in(at[sl // 4])
                    for k in range(KT):
                        last = mm(b[sl % 2][:, 0:S], project.w[:, k, cols(sl % 4)], hh[:, k, 0:S],
                                  start=(k == 0), stop=(k == KT - 1))
                    last.then_inc(qk_proj, 1)

                def sums(sl):
                    pe.wait_ge(raw_ready, turn(raw_ready))
                    last = mm(b[2][0:32, 0:S], K(C_SEL + 32 * sl, 32), sq[:, (sl % 8) * S:(sl % 8 + 1) * S],
                              start=(sl == 0), stop=(sl == 15))
                    if sl == 15:
                        last.then_inc(ssq_ps, 1)

                project(0)
                for sl in range(1, 16):
                    project(sl)
                    sums(sl - 1)
                    if sl % 2 == 1:
                        mod_products(MOD_QK[l][sl // 2], b[3])
                    else:
                        mod_turn(MOD_QK[l][sl // 2 - 1])
                sums(15)
                mod_turn(MOD_QK[l][-1])
                for n in range(2):
                    w = chunk_in(at[4 + n])
                    for t in range(TT):
                        if n == 1:
                            pe.wait_ge(v_ready, turn(v_ready))
                        for k in range(KT):
                            last = mm(b[t], hh[:, k, cols(t)], w[:, k, :], start=(k == 0), stop=(k == KT - 1))
                        last.then_inc(v_proj, 1)
                pe.wait_ge(bias_in, turn(bias_in, 16))
                pe.wait_ge(mod_ready, MOD_QK[l][-1] + 1)
                flips = 4 * (l + 1)
                for n in range(flips):
                    if n >= 2:
                        pe.wait_ge(bias_ready, turn(bias_ready))
                    mm(b[6 + n % 2], K(C_FLIP), bias[:, 2 * n:2 * n + 2, :], start=True, stop=True).then_inc(flip_ps, 1)
                pe.wait_ge(rs_ready, turn(rs_ready))
                for sl in range(16):
                    if sl >= 2:
                        pe.wait_ge(norm_ready, turn(norm_ready))
                    at2 = C2_SPREAD + P * sl
                    mm(b[4 + sl % 2][:, 0:S], cst2[0:32, at2:at2 + P], rstd[0:32, :],
                       start=True, stop=True).then_inc(bc_ps, 1)
                pe.wait_ge(norm_ready, turn(norm_ready, 2))
                pe.wait_ge(bias_ready, turn(bias_ready, 2))
                pe.wait_ge(v_ready, turn(v_ready, 2))

            def attention(l):
                def scores(u):
                    h, qt = divmod(u, TT)
                    if u >= 2:
                        pe.wait_ge(s_added, turn(s_added))
                    for m in range(2):
                        last = mm(pair[u % 2][:, m, 0:P * (qt + 1)], raw[half(m), h, cols(qt)],
                                  raw[half(m), 8 + h, 0:P * (qt + 1)], start=True, stop=True)
                    last.then_inc(scores_ps, 1)

                maps = 1 if l == 0 else 2

                def transposes(u):
                    qt = u % TT
                    pe.wait_ge(prob_ready, turn(prob_ready))
                    if u >= 1:
                        pe.wait_ge(probT_ready, 16 * l + u)
                    for kt in range(qt + 1):
                        for m in range(maps):
                            last = nc.tensor.transpose(b[6][:, cols(kt * maps + m)], prob[:, u % 2, m, cols(kt)], ident)
                    last.then_inc(turn_ps, 1)

                def values(h):
                    pe.wait_ge(probT_ready, 16 * l + 2 * h + 2)
                    if h >= 1:
                        pe.wait_ge(o_ready, 8 * l + h)
                    wide = P // maps
                    for m in range(maps):
                        rows = slice(m * wide, (m + 1) * wide)
                        for kt in range(TT):
                            last = mm(b[7][rows, kt * P:S], v_tok[:, kt, h * P + m * wide:h * P + (m + 1) * wide],
                                      probT[:, kt, m, kt * P:S], start=(kt == 0), stop=(kt == TT - 1))
                    last.then_inc(pv_ps, 1)

                scores(0)
                for u in range(16):
                    if u < 15:
                        scores(u + 1)
                    if u % 2 == 1:
                        mod_products(MOD_ATTN[l][u // 2], b[1])
                    transposes(u)
                    if u % 2 == 0 and u >= 2:
                        mod_turn(MOD_ATTN[l][u // 2 - 1])
                    if u % TT == TT - 1:
                        values(u // TT)
                mod_turn(MOD_ATTN[l][-1])
                pe.wait_ge(o_ready, turn(o_ready, 8))
                if l == 0:
                    for h in range(8):
                        last = mm(b[6][0:16, 0:S], K(C_SEL8 + 16 * h, 16), sq[:, h * S:(h + 1) * S],
                                  start=(h == 0), stop=(h == 7))
                    last.then_inc(ssq_ps, 1)
                    pe.wait_ge(rs_ready, turn(rs_ready))
                    for h in range(8):
                        if h >= 2:
                            pe.wait_ge(norm_ready, turn(norm_ready))
                        at2 = C2_SPREAD + P * h
                        mm(b[4 + h % 2][:, 0:S], cst2[0:16, at2:at2 + P], rstd[0:16, :],
                           start=True, stop=True).then_inc(bc_ps, 1)
                    pe.wait_ge(norm_ready, turn(norm_ready, 2))

            def project_out(l, src):
                for n in range(2):
                    w = chunk_in(out_at[l] + n)
                    for s4 in range(4):
                        c = 4 * n + s4
                        if c >= 4:
                            pe.wait_ge(x_attn, 8 * l + c - 3)
                        for k in range(KT):
                            last = mm(b[2 + c % 4][:, 0:S], w[:, k, cols(s4)], src[:, k, :],
                                      start=(k == 0), stop=(k == KT - 1))
                        last.then_inc(out_proj, 1)

            def route(l):
                E = EXPERTS[l]
                w, width = (rw2, 36) if l == 2 else (rw, 16)
                pe.wait_ge(h_ready, turn(h_ready))
                for t in range(TT):
                    for k in range(KT):
                        last = mm(b[6][:, t * width:(t + 1) * width], hh[:, k, cols(t)], w[:, k, :],
                                  start=(k == 0), stop=(k == KT - 1))
                last.then_inc(logits_ps, 1)
                for t in range(TT):
                    for k in range(KT):
                        last = nc.tensor.transpose(b[2 * t + k // 4][:, cols(k % 4)], hh[:, k, cols(t)], ident)
                        if k % 4 == 3:
                            last.then_inc(h_turned, 1)
                pe.wait_ge(mask_ready, turn(mask_ready))
                mask = route_mask(l)
                mm(b[7][:, 0:E], K(C_TRI), mask[:, 0, :], start=True, stop=True)
                for n, first in ((1, K(C_TRI)), (2, ones)):
                    mm(b[7][:, n * E:(n + 1) * E], first, mask[:, 1, :], start=True, stop=False)
                    last = mm(b[7][:, n * E:(n + 1) * E], ones, mask[:, 0, :], start=False, stop=True)
                last.then_inc(rank_ps, 1)

            def experts(l):
                M = MOE[l]

                def gather(part):
                    for k in range(4 * part, 4 * part + 4):
                        for t in range(TT):
                            last = mm(b[part][:, cols(k % 4)], h_tok[:, t, cols(k)], pick[:, t, :],
                                      start=(t == 0), stop=(t == TT - 1))
                    last.then_inc(M["gather_b" if part else "gather_a"], 1)

                def project(i, m):
                    pe.wait_ge(M["full"][m], 32 * i + 32)
                    for k in range(KT):
                        for a in range(2):
                            last = mm(b[2 + m][half(a), :], x_sel[:, k, half(a)], R8[moe_slot(l, a, m)][:, k, :],
                                      start=(k == 0), stop=(k == KT - 1))
                    last.then_inc(M["up_ps" if m else "gate_ps"], 1)

                def down(n):
                    for f in range(FT):
                        for a in range(2):
                            last = mm(b[5 + n][half(a), :], hidT[:, f, half(a)],
                                      R4[moe_slot(l, a, 2)][:, f, n * 512:(n + 1) * 512],
                                      start=(f == 0), stop=(f == FT - 1))
                    last.then_inc(M["down_b" if n else "down_a"], 1)

                pe.wait_ge(n_ready, l + 1)
                n = pe.value_load(nit[0:1, 0:1], min_val=1, max_val=ROUNDS * EXPERTS[l] // 2)
                pe.wait_ge(h_tok_ready, turn(h_tok_ready, 4))
                pe.wait_ge(M["pick_ready"], 1)
                gather(0)
                gather(1)
                with pe.Fori(0, n) as i:
                    pe.wait_ge(M["sel_a"], i + 1)
                    pe.wait_ge(M["sel_b"], i + 1)
                    project(i, 0)
                    project(i, 1)
                    pe.wait_ge(M["pickg_ready"], i + 1)
                    pe.wait_ge(M["silu_ready"], i + 1)
                    for t in range(TT):
                        last = nc.tensor.transpose(b[2][:, cols(t)], pick_g[:, t, :], ident)
                    last.then_inc(M["gate_turned"], 1)
                    pe.wait_ge(M["pick_ready"], i + 2)
                    gather(0)
                    pe.wait_ge(M["hid_ready"], i + 1)
                    pe.wait_ge(M["added"], 4 * i + 2)
                    for f in range(FT):
                        last = nc.tensor.transpose(b[4][:, cols(f)], hid[:, cols(f)], ident)
                    last.then_inc(M["hid_turned"], 1)
                    gather(1)
                    pe.wait_ge(M["hidT_ready"], i + 1)
                    pe.wait_ge(M["full"][2], 32 * i + 32)
                    down(0)
                    down(1)
                    pe.wait_ge(M["y_a"], i + 1)
                    for r in range(4):
                        if r == 2:
                            pe.wait_ge(M["y_b"], i + 1)
                        pe.wait_ge(M["added"], 4 * i + r + 1)
                        for k in range(2):
                            last = mm(sums[r % 2][:, k * S:(k + 1) * S], y_sel[:, cols(2 * r + k)], spread_g,
                                      start=True, stop=True)
                        last.then_inc(M["comb_ps"], 1)
                pe.wait_ge(M["sel_a"], n + 1)
                pe.wait_ge(M["sel_b"], n + 1)
                pe.wait_ge(M["added"], n * 4 + 2)

            def turn_tokens(src, last_sem):
                for k in range(KT):
                    for t in range(TT):
                        last = nc.tensor.transpose(b[1 + k // 2][:, cols(k % 2 * TT + t)], src(t, k), ident)
                    if k % 2 == 1:
                        last.then_inc(last_sem, 1)

            def hybrid():
                pe.wait_ge(l2_in, 48)
                turn_tokens(lambda t, k: ctx_tok[:, t, cols(k)], turned)
                square_sums()
                square_sums()
                pe.wait_ge(h_ready, turn(h_ready, 2))
                for idx, (n, part) in enumerate(PARTS):
                    if part == IN_PARTS[n][0]:
                        w = chunk_in(in_at + n)
                    if idx >= 4:
                        pe.wait_ge(in_ready, idx - 3)
                    name, num = part.rstrip("0123456789"), part[len(part.rstrip("0123456789")):]
                    num = int(num or 0)
                    o = b[idx % 4]
                    for k in range(KT):
                        f = dict(start=(k == 0), stop=(k == KT - 1))
                        if name == "u":
                            last = mm(o[:, 0:S], w[:, k, cols(num)], hh[:, k, 0:S], **f)
                        elif name == "vm":
                            last = mm(o[:, 0:S], hh[:, k, cols(num)], w[:, k, 256:512], **f)
                        elif name == "q":
                            last = mm(o[:, 0:S], w[:, k, cols(num)], hh[:, k, 0:S], **f)
                        elif name == "k":
                            last = mm(o, w[:, k, 0:P], hh[:, k, :], **f)
                        elif name == "vb":
                            last = mm(o[:, 0:P], hh[:, k, cols(num)], w[:, k, P:2 * P], **f)
                        elif name == "qh":
                            last = mm(o[:, 0:S], w[:, k, cols(2 + num)], hh[:, k, 0:S], **f)
                        elif name in ("zf", "zb"):
                            last = mm(o, w[:, k, cols(num + 2 * (name == "zb"))], hh[:, k, :], **f)
                        elif name == "vh":
                            last = mm(o[:, 0:S], hh[:, k, cols(num)], w[:, k, 0:256], **f)
                        else:
                            last = mm(o[:, 0:S], w[:, k, cols(2 + num)], hh[:, k, 0:S], **f)
                    last.then_inc(in_proj, 1)
                for h in range(4):
                    last = nc.tensor.transpose(b[4][:, cols(h)], ws[:, h, :], ident)
                last.then_inc(turned, 1)
                pe.wait_ge(ws_ready, 1)
                pe.wait_ge(vm_ready, 1)
                for h in range(4):
                    for t in range(TT):
                        o = b[5][half(h % 2), cols(h // 2 * TT + t)]
                        mm(o, vm[:, t, half(h)], wsT[:, h, :], start=True, stop=False)
                        last = mm(o, K(C_ONE, HEAD, 1), bs[:, cols(h)], start=False, stop=True)
                last.then_inc(mix_ps, 1)
                pe.wait_ge(in_ready, len(PARTS))
                pe.wait_ge(raw_ready, turn(raw_ready, 2))
                for j in range(4):
                    mm(b[6][0:32, 0:S], K(C_SEL + 32 * j, 32), sq[:, j * S:(j + 1) * S], start=(j == 0), stop=(j == 3))
                mm(b[7][0:32, :], K(C_SEL, 32), sq[:, 4 * S:6 * S], start=True, stop=True).then_inc(ssq_ps, 1)
                pe.wait_ge(rs_ready, turn(rs_ready))
                for j in range(4):
                    at2 = C2_SPREAD + P * j
                    last = mm(b[j // 2][:, j % 2 * S:(j % 2 + 1) * S], cst2[0:32, at2:at2 + P], rstd[0:32, :],
                              start=True, stop=True)
                    if j % 2 == 1:
                        last.then_inc(bc_ps, 1)
                mm(b[2], cst2[0:32, C2_SPREAD:C2_SPREAD + P], sq[0:32, 6 * S:8 * S], start=True, stop=True).then_inc(bc_ps, 1)
                for g in range(3):
                    pe.wait_ge(norm_ready, turn(norm_ready))
                    if g < 2:
                        last = mm(b[g], K(C_ROT), q2[:, 2 * g:2 * g + 2, :], start=True, stop=True)
                    else:
                        last = mm(b[2][:, 0:S], K(C_ROT), k2[:, 0:S], start=True, stop=True)
                    last.then_inc(bc_ps, 1)
                pe.wait_ge(norm_ready, turn(norm_ready, 3))
                for g in range(2):
                    mm(b[2 + g], K(C_DUP + P * g), k2, start=True, stop=True).then_inc(bc_ps, 1)
                pe.wait_ge(norm_ready, turn(norm_ready, 2))
                pe.wait_ge(ymix_ready, 1)

                def scores(u):
                    hd, qt = divmod(u, TT)
                    if u >= 2:
                        pe.wait_ge(exp_ready, 32 + u - 1)
                    mm(b[u % 2], q2[half(hd % 2), hd // 2, cols(qt)], kd[half(hd % 2), hd // 4, :],
                       start=True, stop=True).then_inc(scores_ps, 1)

                def transposes(u):
                    pe.wait_ge(prob_ready, turn(prob_ready))
                    if u >= 2:
                        pe.wait_ge(probT_ready, 32 + u - 1)
                    for kt in range(4):
                        last = nc.tensor.transpose(b[2 + u % 2][:, cols(kt)], p2[:, u % 2, cols(kt)], ident)
                    last.then_inc(turn_ps, 1)

                def values(hd):
                    pe.wait_ge(probT_ready, 32 + 2 * hd + 2)
                    if hd >= 2:
                        pe.wait_ge(o_ready, 16 + hd - 1)
                    for kt in range(4):
                        last = mm(b[4 + hd % 2][half(hd % 2), 0:S], vb[:, kt, half(hd // 4)], pT2[:, kt, :],
                                  start=(kt == 0), stop=(kt == 3))
                    last.then_inc(pv_ps, 1)

                scores(0)
                for u in range(16):
                    if u < 15:
                        scores(u + 1)
                    transposes(u)
                    if u % TT == TT - 1:
                        values(u // TT)
                pe.wait_ge(o_ready, 24)
                for q in range(2 * SUB):
                    d, i = divmod(q, SUB)
                    pe.wait_ge(prod_ready, q + 1)
                    prod = sq[:, q % 4 * 512:(q % 4 + 1) * 512]
                    for hp in range(2):
                        for t in range(TT):
                            at5 = ((d * 2 + hp) * TT + t) * 32 + i
                            last = mm(b[5][:, at5:at5 + 17:16], prod[:, hp * S + t * P:hp * S + (t + 1) * P],
                                      K(C_SEL, 2), start=True, stop=True)
                    last.then_inc(sc_ps, 1)
                for w, (hp, d) in enumerate(UNITS):
                    pe.wait_ge(dm_ready, w + 1)
                    for n in range(4):
                        last = nc.tensor.transpose(b[6][:, cols(n)], dm[:, n, :], ident)
                    last.then_inc(dm_ps, 1)
                    if w >= 1:
                        pe.wait_ge(sT_ready, w)
                    for jj in range(NSUB):
                        j = jj if d == 0 else NSUB - 1 - jj
                        pe.wait_ge(kk_ready, w * NSUB + jj + 1)
                        for m in range(2):
                            for kt in key_tiles(d, j):
                                o = b[2 * m + kt // 2][:, kt % 2 * S + j * SUB:kt % 2 * S + (j + 1) * SUB]
                                last = mm(o, kk[half(m), jj % 2, cols(kt)],
                                          qq[half(m), d, hp, j * SUB:(j + 1) * SUB], start=True, stop=True)
                        last.then_inc(off_ps, 1)
                    pe.wait_ge(sT_full, w + 1)
                    for m in range(2):
                        for n in range(4):
                            kt = n if d == 0 else (2, 3, 0, 1)[n]
                            tok = (2, 3, 0, 1)[kt] if d == 0 else kt
                            t0, t1 = (P, S) if (d, tok) == (0, 1) else (0, P) if (d, tok) == (1, 0) else (0, S)
                            last = mm(b[4][half(m), hp * S + t0:hp * S + t1], vh[:, tok, half(2 * hp + m)],
                                      sT[:, m, kt, t0:t1], start=(d == 0 and n == 0), stop=(d == 1 and n == 3))
                last.then_inc(pv_ps, 1)
                pe.wait_ge(o_ready, 25)
                for j in range(2):
                    last = mm(b[6][0:32, 0:S], K(C_SEL + 32 * j, 32), osq[:, j, :], start=(j == 0), stop=(j == 1))
                last.then_inc(ssq_ps, 1)
                pe.wait_ge(rs_ready, turn(rs_ready))
                for j in range(2):
                    at2 = C2_SPREAD + P * j
                    last = mm(b[5][:, j * S:(j + 1) * S], cst2[0:32, at2:at2 + P], rstd[0:32, :], start=True, stop=True)
                last.then_inc(bc_ps, 1)
                pe.wait_ge(ymix_ready, 2)

            pe.wait_ge(const_in, 16 * len(const_loads))
            nc.tensor.transpose(b[0][:, 0:P], vecrow[:, 0, :], ident)
            rest = N_VEC - P
            nc.tensor.transpose(b[0][:, P:N_VEC], vecrow[0:rest, 1, :], K(C_ID, rest, rest)).then_inc(vec_ps, 1)
            mm(b[5][0:8, :], t5b, bucket, start=True, stop=True).then_inc(t5_ps, 1)
            pe.wait_ge(x_in, 16)
            turn_tokens(lambda t, k: sq[:, t * D + k * P:t * D + (k + 1) * P], turned)
            pe.wait_ge(lam_diff, 1)
            mm(b[6][:, 0:1], K(C_ONE, P, 1), lamtmp[:, 132:133], start=True, stop=True).then_inc(lam_bc, 1)
            pe.wait_ge(csil_ready, 1)
            for g in MOD_START:
                mod_products(g, b[0])
                mod_turn(g)
            pe.wait_ge(mod_ready, len(MOD_START))
            for l in range(2):
                square_sums()
                qkv(l)
                attention(l)
                project_out(l, oT)
                square_sums()
                route(l)
                experts(l)
            hybrid()
            project_out(2, ymix)
            square_sums()
            route(2)
            experts(2)
            for t in range(TT):
                for k in range(KT):
                    last = nc.tensor.transpose(b[2 * t + k // 4][:, cols(k % 4)], xT[:, k, cols(t)], ident)
                    if k % 4 == 3:
                        last.then_inc(turned, 1)

        @block.scalar
        def _(act):
            turn = make_turn()
            fn = nc.scalar.activation

            def squares(src):
                fn(sq[:, :].rearrange("p (k t) -> p k t", k=KT), src, ACT.Square).then_inc(sq_ready, 1)

            def root(src, dst, n, rows=P):
                fn(dst, src, ACT.Sqrt, bias=eps[0:rows, :], scale=1.0 / n).then_inc(rt_ready, 1)

            def norm(src):
                squares(src)
                act.wait_ge(ssq_ps, turn(ssq_ps))
                root(b[7][:, 0:S], rt[:, :], D)

            def mod_copy(g, bank):
                act.wait_ge(mod_rows, g + 1)
                fn(modrow[:, :], bank, ACT.Copy).then_inc(modrow_ready, 1)

            def qkv(l):
                for sl in range(16):
                    act.wait_ge(qk_proj, turn(qk_proj))
                    fn(raw[:, sl, :], b[sl % 2][:, 0:S], ACT.Copy)
                    fn(sq[:, (sl % 8) * S:(sl % 8 + 1) * S], b[sl % 2][:, 0:S], ACT.Square).then_inc(raw_ready, 1)
                    if sl % 2 == 1:
                        mod_copy(MOD_QK[l][sl // 2], b[3])
                act.wait_ge(ssq_ps, turn(ssq_ps))
                root(b[2][0:32, 0:S], rt[0:32, :], HEAD, 32)
                for n in range(2):
                    for t in range(TT):
                        act.wait_ge(v_proj, turn(v_proj))
                        fn(v_tok[:, t, n * 512:(n + 1) * 512], b[t], ACT.Copy).then_inc(v_ready, 1)

            def attention(l):
                maps = 1 if l == 0 else 2

                def exps(u):
                    act.wait_ge(max_ready, turn(max_ready))
                    wide = P * (u % TT + 1)
                    for m in range(2):
                        last = fn(prob[:, u % 2, m, 0:wide], s_sb[:, u % 2, m, 0:wide], ACT.Exp,
                                  bias=stat[:, u % 2, m:m + 1], accum_out=stat[:, u % 2, 2 + m:3 + m])
                    last.then_inc(exp_ready, 1)

                exps(0)
                for u in range(16):
                    h, qt = divmod(u, TT)
                    if u < 15:
                        exps(u + 1)
                    if u % 2 == 1:
                        mod_copy(MOD_ATTN[l][u // 2], b[1])
                    act.wait_ge(turn_ps, turn(turn_ps))
                    fn(probT[:, 0:qt + 1, 0:maps, cols(qt)],
                       b[6][:, 0:(qt + 1) * maps * P].rearrange("p (k m q) -> p k m q", k=qt + 1, m=maps),
                       ACT.Copy).then_inc(probT_ready, 1)
                    if qt == TT - 1:
                        act.wait_ge(pv_ps, turn(pv_ps))
                        last = fn(oT[:, h, :], b[7][:, 0:S], ACT.Copy)
                        if l == 0:
                            last = fn(sq[:, h * S:(h + 1) * S], b[7][:, 0:S], ACT.Square)
                        last.then_inc(o_ready, 1)
                if l == 0:
                    act.wait_ge(ssq_ps, turn(ssq_ps))
                    root(b[6][0:16, 0:S], rt[0:16, :], P, 16)

            def route(l):
                act.wait_ge(logits_ps, turn(logits_ps))
                if l < 2:
                    fn(route_score(l), b[6][:, 0:TT * 16].rearrange("p (t e) -> p t e", t=TT),
                       ACT.Sigmoid).then_inc(score_ready, 1)
                for n in range(4):
                    act.wait_ge(h_turned, turn(h_turned))
                    fn(h_tok[:, n // 2, n % 2 * 512:(n % 2 + 1) * 512], b[n], ACT.Copy).then_inc(h_tok_ready, 1)
                if l == 2:
                    act.wait_ge(gap_ready, 1)
                    fn(route_gap_exp, route_gap, ACT.Exp).then_inc(gap_exp, 1)

            def experts(l):
                M = MOE[l]
                act.wait_ge(n_ready, l + 1)
                n = act.value_load(nit[0:1, 0:1], min_val=1, max_val=ROUNDS * EXPERTS[l] // 2)
                act.wait_ge(M["gather_a"], 1)
                fn(x_sel[:, 0:4, :], b[0].rearrange("p (k s) -> p k s", k=4), ACT.Copy).then_inc(M["sel_a"], 1)
                with act.Fori(0, n) as i:
                    act.wait_ge(M["gate_ps"], i + 1)
                    fn(gate_act, b[2], ACT.Silu).then_inc(M["silu_ready"], 1)
                    act.wait_ge(M["gate_turned"], i + 1)
                    fn(spread_g, b[2][:, 0:S], ACT.Copy)
                    act.wait_ge(M["gather_a"], i + 2)
                    fn(x_sel[:, 0:4, :], b[0].rearrange("p (k s) -> p k s", k=4), ACT.Copy).then_inc(M["sel_a"], 1)
                    act.wait_ge(M["hid_turned"], i + 1)
                    fn(hidT, b[4].rearrange("p (f s) -> p f s", f=FT), ACT.Copy).then_inc(M["hidT_ready"], 1)
                    act.wait_ge(M["down_a"], i + 1)
                    fn(y_sel[:, 0:512], b[5], ACT.Copy).then_inc(M["y_a"], 1)
                act.wait_ge(M["added"], n * 4 + 2)

            def hybrid():
                for n in range(4):
                    act.wait_ge(turned, turn(turned))
                    fn(cT[:, 2 * n:2 * n + 2, :], b[1 + n].rearrange("p (k t) -> p k t", k=2), ACT.Copy).then_inc(act_step, 1)
                norm(xT[:, :, :])
                act.wait_ge(h_ready, 5)
                act.wait_ge(act_step, 4)
                norm(cT)
                for idx, (n, part) in enumerate(PARTS):
                    act.wait_ge(in_proj, idx + 1)
                    o = b[idx % 4]
                    num = int(part[-1]) if part[-1].isdigit() else 0
                    name = part[:-1] if part[-1].isdigit() else part
                    if name in ("u", "vm"):
                        last = fn((uT if name == "u" else vm)[:, num, :], o[:, 0:S], ACT.Gelu_apprx_tanh)
                    elif name in ("qh", "g"):
                        last = fn((qh if name == "qh" else gs)[:, num, :], o[:, 0:S], ACT.Silu)
                    elif name == "k":
                        last = fn(k2, o, ACT.Copy)
                    elif name in ("zf", "zb"):
                        last = fn(z[:, int(name == "zb"), num, :], o, ACT.Copy)
                    elif name == "vb":
                        last = fn(vb[:, num, :], o[:, 0:P], ACT.Copy)
                    else:
                        last = fn((q2 if name == "q" else vh)[:, num, :], o[:, 0:S], ACT.Copy)
                    last.then_inc(in_ready, 1)
                act.wait_ge(turned, turn(turned))
                fn(wsT, b[4].rearrange("p (h t) -> p h t", h=4), ACT.Copy).then_inc(ws_ready, 1)
                act.wait_ge(vm_sums, 1)
                fn(vm_stat[:, 8:16], vm_stat[:, 0:8], ACT.Sqrt, bias=eps[:, :], scale=1.0 / HEAD).then_inc(vm_rt, 1)
                act.wait_ge(in_ready, len(PARTS))
                fn(sq[:, 0:4 * S], q2.rearrange("p j t -> p (j t)"), ACT.Square).then_inc(raw_ready, 1)
                fn(sq[:, 4 * S:6 * S], k2, ACT.Square).then_inc(raw_ready, 1)
                act.wait_ge(ssq_ps, turn(ssq_ps))
                root(b[6][0:32, 0:S], rt[0:32, :], HEAD, 32)
                root(b[7][0:32, :], sq[0:32, 6 * S:8 * S], HEAD, 32)

                def exps(u):
                    act.wait_ge(max_ready, turn(max_ready))
                    fn(p2[:, u % 2, :], b[u % 2], ACT.Exp, bias=stat[:, u % 2, 0:1],
                       accum_out=stat[:, u % 2, 2:3]).then_inc(exp_ready, 1)

                exps(0)
                for u in range(16):
                    hd, qt = divmod(u, TT)
                    if u < 15:
                        exps(u + 1)
                    act.wait_ge(turn_ps, turn(turn_ps))
                    fn(pT2[:, :, cols(qt)], b[2 + u % 2].rearrange("p (k q) -> p k q", k=4), ACT.Copy).then_inc(probT_ready, 1)
                    if qt == TT - 1:
                        act.wait_ge(pv_ps, turn(pv_ps))
                        fn(ymix[half(hd % 2), 2 + hd // 2, :], b[4 + hd % 2][half(hd % 2), 0:S], ACT.Copy).then_inc(o_ready, 1)
                zz = z.rearrange("p a b t -> p (a b t)")
                act.wait_ge(norm_ready, 16 + 8 + 16 + 8)
                fn(sq[:, :], zz, ACT.Abs).then_inc(act_step, 1)
                act.wait_ge(act_step, 5)
                fn(sq[:, :], sq[:, :], ACT.Exp, scale=-1.0).then_inc(act_step, 1)
                act.wait_ge(act_step, 6)
                fn(sq[:, :], sq[:, :], ACT.Ln, bias=1.0).then_inc(ln_ready, 1)
                act.wait_ge(log_ready, 1)
                fn(qq.rearrange("p a b t -> p (a b t)"), bsub.rearrange("p a b t -> p (a b t)"), ACT.Exp).then_inc(qdec_ready, 1)
                for q in range(2 * SUB):
                    act.wait_ge(arg_ready, q + 1)
                    pr = prod_of(q)
                    fn(pr, pr, ACT.Exp).then_inc(prod_exp, 1)
                act.wait_ge(sc_ps, 2 * SUB)
                fn(sc.rearrange("p a b -> p (a b)"), b[5][:, 0:256], ACT.Copy).then_inc(sc_ready, 1)
                for w, (hp, d) in enumerate(UNITS):
                    act.wait_ge(kk_zero, w + 1)
                    for jj in range(NSUB):
                        j = jj if d == 0 else NSUB - 1 - jj
                        if jj >= 2:
                            act.wait_ge(off_ps, w * NSUB + jj - 1)
                        r = ref_col(d, j)
                        fn(kk[:, jj % 2, before(d, j)], LK[:, d, hp, before(d, j)], ACT.Exp,
                           bias=bpad[:, d, hp, r:r + 1]).then_inc(kk_ready, 1)
                    act.wait_ge(off_ps, (w + 1) * NSUB)
                    for n in range(4):
                        last = fn(sT[:, n // 2, n % 2 * 2:n % 2 * 2 + 2, :], b[n].rearrange("p (k t) -> p k t", k=2), ACT.Copy)
                    last.then_inc(sT_ready, 1)
                act.wait_ge(pv_ps, turn(pv_ps))
                fn(o2, b[4].rearrange("p (j t) -> p j t", j=2), ACT.Copy)
                fn(osq, b[4].rearrange("p (j t) -> p j t", j=2), ACT.Square).then_inc(o_ready, 1)
                act.wait_ge(ssq_ps, turn(ssq_ps))
                root(b[6][0:32, 0:S], rt[0:32, :], HEAD, 32)

            act.wait_ge(eps_ready, 1)
            act.wait_ge(t5_ps, 1)
            fn(t5row, b[5][0:8, :], ACT.Copy).then_inc(t5_row, 1)
            act.wait_ge(vec_ready, 1)
            fn(csil[:, :, 0:N_COND], vec[:, V_C:V_C + N_COND * KT].rearrange("p (a k) -> p k a", k=KT),
               ACT.Silu).then_inc(csil_ready, 1)
            act.wait_ge(lam_sums, 1)
            fn(lamtmp[:, 130:132], lamtmp[:, 128:130], ACT.Exp).then_inc(lam_exp, 1)
            for n in range(4):
                act.wait_ge(turned, turn(turned))
                fn(xT[:, 2 * n:2 * n + 2, :], b[1 + n].rearrange("p (k t) -> p k t", k=2), ACT.Copy).then_inc(x_ready, 1)
            act.wait_ge(x_ready, 4)
            for g in MOD_START:
                mod_copy(g, b[0])
            for l in range(2):
                norm(xT[:, :, :])
                qkv(l)
                attention(l)
                act.wait_ge(x_attn, 8 * (l + 1))
                norm(xT[:, :, :])
                route(l)
                experts(l)
            hybrid()
            act.wait_ge(x_attn, 24)
            norm(xT[:, :, :])
            route(2)
            experts(2)
            for n in range(4):
                act.wait_ge(turned, turn(turned))
                fn(sq[:, n * 512:(n + 1) * 512], b[n], ACT.Copy).then_inc(out_tok, 1)

        @block.gpsimd
        def _(pool):
            for w in range(len(UNITS)):
                if w == 0:
                    pool.wait_ge(log_ready, 1)
                else:
                    pool.wait_ge(off_ps, w * NSUB)
                nc.gpsimd.memset(kk, 0.0).then_inc(kk_zero, 1)

        @block.vector
        def _(dve):
            turn = make_turn()
            steps = [0]
            tt, ts, stt = nc.vector.tensor_tensor, nc.vector.tensor_scalar, nc.vector.scalar_tensor_tensor

            def then(ins):
                steps[0] += 1
                ins.then_inc(dve_step, 1)
                dve.wait_ge(dve_step, steps[0])

            def mod_add(g):
                l, n = divmod(g, 12)
                o, width = mod_columns(g)
                v = V_ADA[l] + 4 * n
                dve.wait_ge(mod_cols, g + 1)
                if width == 2:
                    then(tt(modc[:, 4 * n:4 * n + 4], o[:, :, 1], vec[:, v:v + 4], ALU.add))
                tt(mod[:, l, 4 * n:4 * n + 4], o[:, :, 0], vec[:, v:v + 4], ALU.add).then_inc(mod_ready, 1)
                dve.wait_ge(mod_ready, g + 1)
                if n == 3:
                    then(stt(gain1[:, l, :], mod[:, l, SC1:SC1 + KT], 1.0, vec[:, V_MIX[l]:V_MIX[l] + KT],
                             ALU.add, ALU.mult))
                    if l == 2:
                        then(stt(gainc[:, :], modc[:, SC1:SC1 + KT], 1.0, vec[:, V_NORM1:V_NORM1 + KT],
                                 ALU.add, ALU.mult))
                if n == 9:
                    then(stt(gain2[:, l, :], mod[:, l, SC2:SC2 + KT], 1.0, vec[:, V_FFN[l]:V_FFN[l] + KT],
                             ALU.add, ALU.mult))

            def norm(src, at, gain, shift):
                dve.wait_ge(rt_ready, turn(rt_ready))
                then(nc.vector.reciprocal(rstd[:, :], rt[:, :]))
                xn = sq[:, :].rearrange("p (k t) -> p k t", k=KT)
                then(tt(xn, src, rstd[:, :].unsqueeze(1).broadcast_to([P, KT, S]), ALU.mult))
                for k in range(KT):
                    last = ts(hh[:, k, at:at + S], xn[:, k, :], gain[:, k:k + 1], shift[:, k:k + 1], ALU.mult, ALU.add)
                last.then_inc(h_ready, 1)

            def head_norms(rows):
                dve.wait_ge(rt_ready, turn(rt_ready))
                nc.vector.reciprocal(rstd[0:rows, :], rt[0:rows, :]).then_inc(rs_ready, 1)

            def qkv(l):
                for g in MOD_QK[l]:
                    mod_add(g)
                head_norms(32)
                flips = 4 * (l + 1)
                for n in range(flips):
                    dve.wait_ge(flip_ps, turn(flip_ps))
                    nc.vector.tensor_copy(bias[:, 2 * n:2 * n + 2, :],
                                          b[6 + n % 2].rearrange("p (h j) -> p h j", h=2)).then_inc(bias_ready, 1)
                dve.wait_ge(bias_ready, turn(bias_ready, flips))
                then(nc.vector.memset(bias[0:64, 0:2 * flips, P + 64:S], NEG))
                for sl in range(16):
                    dve.wait_ge(bc_ps, turn(bc_ps))
                    gain = qscale[:, l:l + 1] if sl < 8 else vec[:, GAIN_AK + 2 * l:GAIN_AK + 2 * l + 1]
                    stt(raw[:, sl, :], raw[:, sl, :], gain, b[4 + sl % 2][:, 0:S], ALU.mult, ALU.mult).then_inc(norm_ready, 1)

            def attention(l):
                def maxima(u):
                    h, qt = divmod(u, TT)
                    wide, n = P * (qt + 1), u % 2
                    dve.wait_ge(scores_ps, turn(scores_ps))
                    by_key = slice(P - qt * P, S)
                    if l == 0:
                        bb = bias[:, h, by_key].unsqueeze(1).broadcast_to([P, 2, wide])
                    else:
                        bb = bias[:, 2 * h:2 * h + 2, by_key]
                    tt(s_sb[:, n, :, 0:wide], pair[n][:, :, 0:wide], bb, ALU.add).then_inc(s_added, 1)
                    dve.wait_ge(s_added, turn(s_added))
                    then(nc.vector.tensor_reduce(stat[:, n, 4:6], s_sb[:, n, :, 0:wide], AX.X, ALU.max))
                    ts(stat[:, n, 0:2], stat[:, n, 4:6], -1.0, None, ALU.mult).then_inc(max_ready, 1)

                def weights(u):
                    wide, n = P * (u % TT + 1), u % 2
                    dve.wait_ge(exp_ready, turn(exp_ready))
                    then(nc.vector.reciprocal(stat[:, n, 6:8], stat[:, n, 2:4]))
                    p0, p1 = prob[:, n, 0, 0:wide], prob[:, n, 1, 0:wide]
                    if l == 0:
                        then(tt(stat[:, n, 7:8], stat[:, n, 7:8], nlam[:, :], ALU.mult))
                        then(ts(p0, p0, stat[:, n, 6:7], None, ALU.mult))
                        last = stt(p0, p1, stat[:, n, 7:8], p0, ALU.mult, ALU.add)
                    else:
                        ts(p0, p0, stat[:, n, 6:7], None, ALU.mult)
                        last = ts(p1, p1, stat[:, n, 7:8], None, ALU.mult)
                    last.then_inc(prob_ready, 1)

                maxima(0)
                for u in range(16):
                    if u < 15:
                        maxima(u + 1)
                    weights(u)
                    if u % 2 == 1 and u >= 3:
                        mod_add(MOD_ATTN[l][u // 2 - 1])
                mod_add(MOD_ATTN[l][-1])
                if l == 0:
                    head_norms(16)
                    for h in range(8):
                        dve.wait_ge(bc_ps, turn(bc_ps))
                        stt(oT[:, h, :], oT[:, h, :], qscale[:, 3:4], b[4 + h % 2][:, 0:S],
                            ALU.mult, ALU.mult).then_inc(norm_ready, 1)

            def add_out(l):
                for c in range(KT):
                    dve.wait_ge(out_proj, turn(out_proj))
                    stt(xT[:, c, :], b[2 + c % 4][:, 0:S], mod[:, l, G1 + c:G1 + c + 1], xT[:, c, :],
                        ALU.mult, ALU.add).then_inc(x_attn, 1)

            def pick_group(scores8, best, index, number):
                for t in range(TT):
                    then(nc.vector.max(best[:, t, :], scores8[:, t, :]))
                    then(nc.vector.max_index(index[:, t, :], best[:, t, :], scores8[:, t, :]))
                then(nc.vector.tensor_copy(number, index[:, :, 0:2]))

            def choose(l, sel, number):
                E = EXPERTS[l]
                r = route_work(l)
                io = K(C_IOTA, GROUPS).unsqueeze(1).broadcast_to([P, TT, GROUPS])
                then(tt(r["gmask"], io, number[:, :, 0:1].broadcast_to([P, TT, GROUPS]), ALU.is_equal))
                wide = r["gmask"].unsqueeze(3).broadcast_to([P, TT, GROUPS, E // GROUPS])
                by_group = lambda a: a.rearrange("p t (g e) -> p t g e", g=GROUPS)
                then(nc.vector.tensor_copy(by_group(r["masked"]), wide))
                then(ts(r["fill"], r["masked"], -1.0, -NEG, ALU.add, ALU.mult))
                then(tt(r["masked"], r["masked"], sel, ALU.mult))
                then(tt(r["masked"], r["masked"], r["fill"], ALU.add))
                for t in range(TT):
                    then(nc.vector.max(r["best"][:, t, :], r["masked"][:, t, :]))
                    then(nc.vector.max_index(r["index"][:, t, :], r["best"][:, t, :], r["masked"][:, t, :]))
                then(nc.vector.tensor_copy(r["number"], r["index"][:, :, 0:2]))
                ie = K(C_IOTA, E).unsqueeze(1).broadcast_to([P, TT, E])
                for n in range(2):
                    then(tt(r["hot"][n], ie, r["number"][:, :, n:n + 1].broadcast_to([P, TT, E]), ALU.is_equal))
                tt(route_mask(l), r["hot"][0], r["hot"][1], ALU.add).then_inc(mask_ready, 1)
                dve.wait_ge(mask_ready, turn(mask_ready))

            def route(l):
                E, M = EXPERTS[l], MOE[l]
                r = route_work(l)
                if l < 2:
                    dve.wait_ge(score_ready, turn(score_ready))
                    score = route_score(l)
                    then(tt(r["sel"], score, rb[:, :].unsqueeze(1).broadcast_to([P, TT, 16]), ALU.add))
                    g = r["sel"].rearrange("p t (g e) -> p (t g) e", g=GROUPS)
                    s6 = r["sums"]
                    for first, n, at in ((0, 3, 0), (1, 2, 3), (2, 1, 5)):
                        then(tt(s6[:, :, at:at + n], g[:, :, first + 1:4],
                                g[:, :, first:first + 1].broadcast_to([P, TT * GROUPS, n]), ALU.add))
                    then(nc.vector.memset(r["g8"], FAR))
                    then(nc.vector.tensor_reduce(r["g8"][:, :, 0:GROUPS], s6.rearrange("p (t g) s -> p t g s", t=TT),
                                                 AX.X, ALU.max))
                    pick_group(r["g8"], r["best"], r["index"], r["number"])
                    choose(l, r["sel"], r["number"])
                    mask = route_mask(l)
                    gate = r["gate"]
                    then(tt(gate, mask, score, ALU.mult))
                    then(nc.vector.tensor_reduce(r["total"], gate, AX.X, ALU.add))
                    then(nc.vector.reciprocal(r["inv"], r["total"]))
                    then(tt(gate, gate, r["inv"].unsqueeze(2).broadcast_to([P, TT, E]), ALU.mult))
                else:
                    dve.wait_ge(logits_ps, 3)
                    lg = r["logits"]
                    then(tt(lg, b[6][:, 0:TT * 36].rearrange("p (t e) -> p t e", t=TT),
                            rb2[:, :].unsqueeze(1).broadcast_to([P, TT, 36]), ALU.add))
                    then(nc.vector.memset(r["g8"], FAR))
                    then(nc.vector.tensor_copy(r["g8"][:, :, 0:GROUPS], lg[:, :, 0:GROUPS]))
                    pick_group(r["g8"], r["best"], r["index"], r["number"])
                    then(tt(route_gap[:, :, 0:GROUPS], lg[:, :, 0:GROUPS],
                            r["best"][:, :, 0:1].broadcast_to([P, TT, GROUPS]), ALU.subtract))
                    choose(l, lg[:, :, GROUPS:36], r["number"])
                    tt(route_gap[:, :, 4:5], r["best"][:, :, 1:2], r["best"][:, :, 0:1], ALU.subtract).then_inc(gap_ready, 1)
                    dve.wait_ge(gap_exp, 1)
                    then(nc.vector.tensor_reduce(r["total"], route_gap_exp[:, :, 0:GROUPS], AX.X, ALU.add))
                    e1 = route_gap_exp[:, :, 4:5]
                    total = r["total"].unsqueeze(2)
                    then(stt(total, e1, 1.0, total, ALU.add, ALU.mult))
                    then(nc.vector.reciprocal(r["inv"], r["total"]))
                    then(tt(r["inv1"].unsqueeze(2), r["inv"].unsqueeze(2), e1, ALU.mult))
                    gate = r["gate"]
                    then(tt(gate, r["hot"][0], r["inv"].unsqueeze(2).broadcast_to([P, TT, E]), ALU.mult))
                    then(tt(r["hot"][1], r["hot"][1], r["inv1"].unsqueeze(2).broadcast_to([P, TT, E]), ALU.mult))
                    then(tt(gate, gate, r["hot"][1], ALU.add))
                dve.wait_ge(rank_ps, turn(rank_ps))
                last = ROUNDS * E
                then(stt(r["masked"], b[7][:, 0:TT * E].rearrange("p (t e) -> p t e", t=TT), 1.0, route_mask(l),
                         ALU.add, ALU.mult))
                nc.vector.memset(slot_of[:, :, last:last + 2], -1.0)
                nc.vector.memset(gate_of[:, :, last:last + 2], 0.0).then_inc(M["added"], 2)
                for n in range(ROUNDS):
                    ts(slot_of[:, :, n * E:(n + 1) * E], r["masked"], -1.0 - SLOTS * n, None, ALU.add)
                    then(nc.vector.tensor_copy(gate_of[:, :, n * E:(n + 1) * E], gate))
                then(nc.vector.tensor_reduce(r["most"], b[7][:, TT * E:(TT + 1) * E], AX.X, ALU.max))
                then(ts(r["steps"], K(C_IOTA + 1, ROUNDS - 1), float(SLOTS), None, ALU.mult))
                then(ts(r["steps"], r["steps"], r["most"], None, ALU.is_lt))
                then(nc.vector.tensor_reduce(r["most"], r["steps"], AX.X, ALU.add))
                then(nc.vector.tensor_copy(nit[:, 1:2], r["most"]))
                ts(nit[:, 0:1], r["most"], E / 2.0, E / 2.0, ALU.mult, ALU.add).then_inc(n_ready, 1)

            def experts(l):
                M = MOE[l]
                iota = K(C_IOTA, SLOTS).unsqueeze(1).unsqueeze(1).broadcast_to([P, TT, 2, SLOTS])
                as4 = lambda a: a.rearrange("p t (a s) -> p t a s", a=2)

                def pick_pair(at):
                    tt(as4(pick), iota, slot_of[:, :, at].unsqueeze(3).broadcast_to([P, TT, 2, SLOTS]),
                       ALU.is_equal).then_inc(M["pick_ready"], 1)

                def gate_pair(at):
                    tt(as4(pick_g), as4(pick), gate_of[:, :, at].unsqueeze(3).broadcast_to([P, TT, 2, SLOTS]),
                       ALU.mult).then_inc(M["pickg_ready"], 1)

                dve.wait_ge(n_ready, l + 1)
                n = dve.value_load(nit[0:1, 0:1], min_val=1, max_val=ROUNDS * EXPERTS[l] // 2)
                pick_pair(slice(0, 2))
                dve.wait_ge(M["pick_ready"], 1)
                gate_pair(slice(0, 2))
                second = lambda: nc.vector.tensor_copy(x_sel[:, 4:8, :], b[1].rearrange("p (k s) -> p k s", k=4))
                dve.wait_ge(M["gather_b"], 1)
                second().then_inc(M["sel_b"], 1)
                with dve.Fori(0, n) as i:
                    nxt = bass.ds(2 * i + 2, 2)
                    dve.wait_ge(M["gather_b"], i + 1)
                    dve.wait_ge(M["pickg_ready"], i + 1)
                    pick_pair(nxt)
                    dve.wait_ge(M["silu_ready"], i + 1)
                    dve.wait_ge(M["up_ps"], i + 1)
                    tt(hid, gate_act, b[3], ALU.mult).then_inc(M["hid_ready"], 1)
                    dve.wait_ge(M["gate_turned"], i + 1)
                    dve.wait_ge(M["pick_ready"], i + 2)
                    gate_pair(nxt)
                    dve.wait_ge(M["gather_b"], i + 2)
                    second().then_inc(M["sel_b"], 1)
                    dve.wait_ge(M["down_b"], i + 1)
                    nc.vector.tensor_copy(y_sel[:, 512:1024], b[6]).then_inc(M["y_b"], 1)
                    for r in range(4):
                        dve.wait_ge(M["comb_ps"], 4 * i + r + 1)
                        for k in range(2 * r, 2 * r + 2):
                            last = stt(xT[:, k, :], sums[r % 2][:, k % 2 * S:(k % 2 + 1) * S],
                                       mod[:, l, G2 + k:G2 + k + 1], xT[:, k, :], ALU.mult, ALU.add)
                        last.then_inc(M["added"], 1)

            def hybrid():
                norm(xT[:, :, :], 0, gain1[:, 2, :], mod[:, 2, SH1:SH1 + KT])
                norm(cT, S, gainc, modc[:, SH1:SH1 + KT])
                dve.wait_ge(in_ready, 4)
                by_head = lambda a: a.rearrange("p t (h d) -> p (t h) d", d=HEAD)
                then(tt(vm_sq, vm, vm, ALU.mult))
                nc.vector.tensor_reduce(vm_stat[:, 0:8], by_head(vm_sq), AX.X, ALU.add).then_inc(vm_sums, 1)
                dve.wait_ge(vm_rt, 1)
                then(nc.vector.reciprocal(vm_stat[:, 16:24], vm_stat[:, 8:16]))
                tt(by_head(vm), by_head(vm), vm_stat[:, 16:24].unsqueeze(2).broadcast_to([P, 8, HEAD]),
                   ALU.mult).then_inc(vm_ready, 1)
                dve.wait_ge(mix_ps, 1)
                tt(ymix[:, 0:2, :], uT, b[5].rearrange("p (j t) -> p j t", j=2), ALU.mult).then_inc(ymix_ready, 1)
                dve.wait_ge(rt_ready, turn(rt_ready, 2))
                then(nc.vector.reciprocal(sq[0:32, 6 * S:8 * S], sq[0:32, 6 * S:8 * S]))
                nc.vector.reciprocal(rstd[0:32, :], rt[0:32, :]).then_inc(rs_ready, 1)
                two = lambda a: a.rearrange("p (j t) -> p j t", j=2)
                for g in range(3):
                    dve.wait_ge(bc_ps, turn(bc_ps))
                    if g < 2:
                        last = stt(q2[:, 2 * g:2 * g + 2, :], q2[:, 2 * g:2 * g + 2, :], qscale[:, 2:3], two(b[g]),
                                   ALU.mult, ALU.mult)
                    else:
                        last = stt(k2, k2, vec[:, GAIN_K2:GAIN_K2 + 1], b[2], ALU.mult, ALU.mult)
                    last.then_inc(norm_ready, 1)
                dve.wait_ge(norm_ready, turn(norm_ready, 16 + 8 + 16 + 3))
                for g in range(3):
                    dve.wait_ge(bc_ps, turn(bc_ps))
                    n = 2 if g < 2 else 1
                    a = q2[:, 2 * g:2 * g + 2, :] if g < 2 else k2[:, 0:S].unsqueeze(1)
                    rot = b[g][:, 0:n * S].rearrange("p (j t) -> p j t", j=n)
                    tmp = sq[:, 0:n * S].rearrange("p (j t) -> p j t", j=n)
                    table = lambda at: K(at, S).unsqueeze(1).broadcast_to([P, n, S])
                    then(tt(tmp, rot, table(C_SIN), ALU.mult))
                    then(tt(a, a, table(C_COS), ALU.mult))
                    tt(a, a, tmp, ALU.add).then_inc(norm_ready, 1)
                    dve.wait_ge(norm_ready, turn(norm_ready))

                for g in range(2):
                    dve.wait_ge(bc_ps, turn(bc_ps))
                    nc.vector.tensor_copy(kd[:, g, :], b[2 + g]).then_inc(norm_ready, 1)

                def maxima(u):
                    dve.wait_ge(scores_ps, turn(scores_ps))
                    then(nc.vector.tensor_reduce(stat[:, u % 2, 4:5], b[u % 2], AX.X, ALU.max))
                    ts(stat[:, u % 2, 0:1], stat[:, u % 2, 4:5], -1.0, None, ALU.mult).then_inc(max_ready, 1)

                maxima(0)
                for u in range(16):
                    if u < 15:
                        maxima(u + 1)
                    dve.wait_ge(exp_ready, turn(exp_ready))
                    then(nc.vector.reciprocal(stat[:, u % 2, 6:7], stat[:, u % 2, 2:3]))
                    ts(p2[:, u % 2, :], p2[:, u % 2, :], stat[:, u % 2, 6:7], None, ALU.mult).then_inc(prob_ready, 1)
                dve.wait_ge(ln_ready, 1)
                z8 = z.rearrange("p a b (h t) -> p (a b h) t", h=2)
                l8 = sq[:, :].rearrange("p (n t) -> p n t", n=8)
                then(stt(nlk, z8, 0.0, l8, ALU.max, ALU.add))
                then(stt(z8, z8, 0.0, l8, ALU.min, ALU.subtract))
                one = cst[:, C_ONE:C_ONE + 1].broadcast_to([P, S])
                then(nc.vector.memset(bpad[:, 0, :, 0:1], 0.0))
                then(nc.vector.memset(bpad[:, 1, :, S:S + 1], 0.0))
                then(nc.vector.memset(epad[:, 0, :, S:S + 1], 0.0))
                then(nc.vector.memset(epad[:, 1, :, 0:1], 0.0))
                for hp in range(2):
                    scan = nc.vector.tensor_tensor_scan
                    then(scan(bpad[:, 0, hp, 1:S + 1], one, z[:, 0, hp, 0:S], 0.0, ALU.mult, ALU.add))
                    then(scan(bpad[:, 1, hp, S - 1::-1], one, z[:, 1, hp, S - 1::-1], 0.0, ALU.mult, ALU.add))
                    then(scan(epad[:, 0, hp, S - 1::-1], one, z[:, 0, hp, 2 * S - 1:S - 1:-1], 0.0, ALU.mult, ALU.add))
                    then(scan(epad[:, 1, hp, 1:S + 1], one, z[:, 1, hp, S:2 * S], 0.0, ALU.mult, ALU.add))
                nlk5 = nlk.rearrange("p (a b h) t -> p a b h t", a=2, b=2)
                for d in range(2):
                    bx = bpad[:, d, :, 1:S + 1] if d == 0 else bpad[:, d, :, 0:S]
                    ex = epad[:, d, :, 1:S + 1] if d == 0 else epad[:, d, :, 0:S]
                    r0_ = ref_col(d, 0)
                    ref = bpad[:, d, :, r0_:r0_ + 15 * SUB + 1:SUB].unsqueeze(3).broadcast_to([P, 2, NSUB, SUB])
                    sub = lambda a: a.rearrange("p b (j t) -> p b j t", t=SUB)
                    then(tt(sub(bsub[:, d]), sub(bx), ref, ALU.subtract))
                    then(stt(lks[:, d], nlk5[:, d, :, 0, :], -1.0, bsub[:, d], ALU.mult, ALU.subtract))
                    xk, ck = (slice(S, 2 * S), slice(0, S)) if d == 0 else (slice(0, S), slice(S, 2 * S))
                    then(stt(LK[:, d, :, xk], nlk5[:, d, :, 0, :], -1.0, bx, ALU.mult, ALU.subtract))
                    last = tt(LK[:, d, :, ck], ex, nlk5[:, d, :, 1, :], ALU.subtract)
                    if d == 0:
                        then(last)
                    else:
                        last.then_inc(log_ready, 1)
                dve.wait_ge(qdec_ready, 1)
                then(tt(qq, qq, qh.unsqueeze(1).broadcast_to([P, 2, 2, S]), ALU.mult))

                def args(q):
                    d, i = divmod(q, SUB)
                    if q >= 4:
                        dve.wait_ge(sc_ps, q - 3)
                    pr = prod_of(q)
                    seen = seen_by(d, i)
                    key = lks[:, d].rearrange("p b (j t) -> p (b j) t", t=SUB)[:, :, i:i + 1]
                    tt(pr, bsub[:, d].rearrange("p b (j t) -> p (b j) t", t=SUB)[:, :, seen],
                       key.broadcast_to([P, 2 * NSUB, seen.stop - seen.start]), ALU.add).then_inc(arg_ready, 1)

                args(0)
                args(1)
                for q in range(2 * SUB):
                    d, i = divmod(q, SUB)
                    if q + 2 < 2 * SUB:
                        args(q + 2)
                    dve.wait_ge(prod_exp, q + 1)
                    pr = prod_of(q)
                    tt(pr, pr, qh.rearrange("p b (j t) -> p (b j) t", t=SUB)[:, :, seen_by(d, i)],
                       ALU.mult).then_inc(prod_ready, 1)
                dve.wait_ge(sc_ready, 1)
                for w, (hp, d) in enumerate(UNITS):
                    if w >= 1:
                        dve.wait_ge(dm_ps, w)
                    own = sc.rearrange("p a b -> p (a b)")[:, (d * 2 + hp) * 64:(d * 2 + hp + 1) * 64]
                    own = own.rearrange("p (n s) -> p n s", n=4).unsqueeze(2).broadcast_to([P, 4, P // SUB, SUB])
                    mask = K(C_DIAG + P * d).rearrange("p (j s) -> p j s", s=SUB).unsqueeze(1).broadcast_to([P, 4, P // SUB, SUB])
                    tt(dm.rearrange("p n (j s) -> p n j s", s=SUB), own, mask, ALU.mult).then_inc(dm_ready, 1)
                    dve.wait_ge(dm_ps, w + 1)
                    dve.wait_ge(sT_ready, w + 1)
                    for n in range(4):
                        t, m = divmod(n, 2)
                        kt = t + 2 if d == 0 else t
                        last = tt(sT[:, m, kt, cols(t)], sT[:, m, kt, cols(t)], b[6][:, cols(n)], ALU.add)
                    last.then_inc(sT_full, 1)
                head_norms(32)
                dve.wait_ge(bc_ps, turn(bc_ps))
                then(stt(o2, o2, vec[:, GAIN_O2:GAIN_O2 + 1], b[5].rearrange("p (j t) -> p j t", j=2), ALU.mult, ALU.mult))
                tt(ymix[:, 6:8, :], o2, gs, ALU.mult).then_inc(ymix_ready, 1)

            nc.vector.memset(csil[:, :, :], 0.0)
            nc.vector.memset(eps[:, :], EPS).then_inc(eps_ready, 1)
            dve.wait_ge(const_in, 16 * len(const_loads))
            lam4 = lamrow.rearrange("p (n two d) -> p n two d", n=2, two=2)
            then(tt(lamtmp[:, 0:2 * HEAD].rearrange("p (n d) -> p n d", n=2), lam4[:, :, 0, :], lam4[:, :, 1, :], ALU.mult))
            nc.vector.tensor_reduce(lamtmp[:, 128:130], lamtmp[:, 0:2 * HEAD].rearrange("p (n d) -> p n d", n=2),
                                    AX.X, ALU.add).then_inc(lam_sums, 1)
            dve.wait_ge(vec_ps, 1)
            nc.vector.tensor_copy(vec[:, :], b[0][:, 0:N_VEC]).then_inc(vec_ready, 1)
            dve.wait_ge(lam_exp, 1)
            tt(lamtmp[:, 132:133], lamtmp[:, 131:132], lamtmp[:, 130:131], ALU.subtract).then_inc(lam_diff, 1)
            dve.wait_ge(vec_ready, 1)
            for n, (g, f) in enumerate(((GAIN_AQ, HEAD ** -0.5), (GAIN_BQ, HEAD ** -0.5), (GAIN_Q2, HEAD ** -0.5),
                                        (GAIN_SUB, 1.0 - LAMBDA_INIT))):
                then(ts(qscale[:, n:n + 1], vec[:, g:g + 1], f, None, ALU.mult))
            dve.wait_ge(lam_bc, 1)
            ts(nlam[:, :], b[6][:, 0:1], -LAMBDA_INIT, None, ALU.add).then_inc(lam_ready, 1)
            dve.wait_ge(lam_ready, 1)
            for g in MOD_START:
                mod_add(g)
            for l in range(2):
                norm(xT[:, :, :], 0, gain1[:, l, :], mod[:, l, SH1:SH1 + KT])
                qkv(l)
                attention(l)
                add_out(l)
                norm(xT[:, :, :], 0, gain2[:, l, :], mod[:, l, SH2:SH2 + KT])
                route(l)
                experts(l)
            hybrid()
            add_out(2)
            norm(xT[:, :, :], 0, gain2[:, 2, :], mod[:, 2, SH2:SH2 + KT])
            route(2)
            experts(2)


_OUTS = [((1, S, D), "float32")]
_INS = ["x", "c", "ada_w", "ada_b", "norm_mix_g", "norm_ffn_g", "t5_bias", "a_w_qkv", "a_q_gain", "a_k_gain",
        "a_lambda", "a_subln_g", "a_w_o", "b_w_qkv", "b_q_gain", "b_k_gain", "b_rel_bias", "b_w_o", "router_w",
        "router_bias", "moe_w_gate", "moe_w_up", "moe_w_down", "c_2", "ctx_2", "c_ctx_2", "w_mod_2", "b_mod_2",
        "norm1_w_2", "w_in_2", "w_s_2", "b_s_2", "q_norm_w_2", "k_norm_w_2", "hgrn_lb_logits_2", "hgrn_norm_w_2",
        "w_out_2", "norm2_w_2", "w_grp_2", "b_grp_2", "w_exp_2", "b_exp_2", "w1_2", "w3_2", "w2_2"]


def kernel(**inputs):
    import concourse.bacc as bacc
    from concourse.bass_utils import run_bass_kernel_spmd

    nc = bacc.Bacc("TRN2", target_bir_lowering=False, num_devices=1)
    arrays, args = {}, []
    named = [(n, np.ascontiguousarray(inputs[n])) for n in _INS]
    named += list(zip(("const", "const2", "bucket"), constants()))
    for name, a in named:
        arrays[f"in_{name}_dram"] = a
        args.append(nc.dram_tensor(f"in_{name}_dram", a.shape, mybir.dt.from_np(a.dtype), kind="ExternalInput").ap())
    for i, (shape, dtype) in enumerate(_OUTS):
        args.append(nc.dram_tensor(f"out_{i}_dram", shape, mybir.dt.from_np(np.dtype(dtype)), kind="ExternalOutput").ap())
    program(nc, *args)
    r = run_bass_kernel_spmd(nc, [arrays], core_ids=[0])
    return r.results[0]["out_0_dram"]
```

```python
from contextlib import ExitStack
import math

import numpy as np
import concourse.bass as bass
from concourse import mybir

F32 = mybir.dt.float32
I32 = mybir.dt.int32
U32 = mybir.dt.uint32
ALU = mybir.AluOpType
ACT = mybir.ActivationFunctionType
AX = mybir.AxisListType

P = 128
D = 1024
KT = D // P
S = 256
TT = S // P
FF = 512
FT = FF // P
CHUNK = 512
NSLOT = 6
SLOTS = 64
ROUNDS = S // SLOTS
HEAD = 64
EPS = 1e-6
NEG = -1e30
FAR = -3e38
LAMBDA_INIT = 0.8 - 0.6 * math.exp(-0.3 * 0)
SUB = 16
NSUB = S // SUB
N_COND = 3
N_MOD = 6 * KT
SH1, SC1, G1, SH2, SC2, G2 = (KT * n for n in range(6))
EXPERTS = (16, 16, 32)
GROUPS = 4

V_ADA = (0, 48, 128)
V_C, V_NORM1 = 96, 120
V_MIX, V_FFN = (176, 184, V_NORM1), (192, 200, 208)
V_GAIN = 216
GAIN_AQ, GAIN_AK, GAIN_BQ, GAIN_BK, GAIN_Q2, GAIN_K2, GAIN_O2, GAIN_SUB = range(V_GAIN, V_GAIN + 8)
N_VEC = V_GAIN + 8

C_ID, C_FLIP, C_TRI, C_ONE = 0, 128, 256, 384
C_SEL = 512
C_SEL8 = C_SEL + 512
C_IOTA = C_SEL8 + 128
C_COS, C_SIN = C_IOTA + 64, C_IOTA + 64 + 256
C_ROT = C_SIN + 256
C_DIAG = C_ROT + 128
C_DUP = C_DIAG + 256
C_MOD = C_DUP + 256
N_CST = C_MOD + 4
C2_SPREAD = 0
N_CST2 = 16 * P


def constants():
    c = np.zeros((P, N_CST), np.float32)
    p = np.arange(P)
    c[:, C_ID:C_ID + P] = np.eye(P)
    c[:, C_FLIP:C_FLIP + P] = np.eye(P)[::-1]
    c[:, C_TRI:C_TRI + P] = p[:, None] < p[None, :]
    c[:, C_ONE:C_ONE + P] = 1.0
    c2 = np.zeros((32, N_CST2), np.float32)
    for sl in range(16):
        c[p, C_SEL + 32 * sl + 2 * sl + p // HEAD] = 1.0
        c2[2 * sl + p // HEAD, C2_SPREAD + P * sl + p] = 1.0
    for h in range(8):
        c[:, C_SEL8 + 16 * h + 2 * h:C_SEL8 + 16 * h + 2 * h + 2] = 1.0
    c[:, C_IOTA:C_IOTA + 64] = np.arange(64)
    t = np.arange(S)
    inv = (1.0 / (np.float32(10000.0) ** (np.arange(0, 32, 2, dtype=np.float32) / np.float32(32)))).astype(np.float32)
    ang = np.stack([(t // 64).astype(np.float32)[:, None] * inv, (t % 64).astype(np.float32)[:, None] * inv], 1)
    d = p % HEAD
    c[:, C_COS:C_COS + S] = np.cos(ang)[:, d // 32, d % 16].T
    c[:, C_SIN:C_SIN + S] = np.sin(ang)[:, d // 32, d % 16].T
    for m in range(P):
        if (m % 32) < 16:
            c[m + 16, C_ROT + m] = -1.0
        else:
            c[m - 16, C_ROT + m] = 1.0
    same = p[:, None] // SUB == p[None, :] // SUB
    c[:, C_DIAG:C_DIAG + P] = same & (p[None, :] <= p[:, None])
    c[:, C_DIAG + P:C_DIAG + 2 * P] = same & (p[None, :] >= p[:, None])
    for g in range(2):
        c[g * HEAD + p % HEAD, C_DUP + P * g + p] = 1.0
    for cond in range(N_COND):
        c[cond::32, C_MOD + cond] = 1.0
    rel = np.arange(512) - 255
    n = np.abs(rel)
    far = 8 + (np.log(np.maximum(n, 1).astype(np.float32) / np.float32(8)) / np.float32(math.log(1024 / 8))
               * np.float32(8)).astype(np.int32)
    bucket = np.where(rel > 0, 16, 0) + np.where(n < 8, n, np.minimum(far, 15))
    onehot = (np.arange(32)[:, None] == bucket[None, :]).astype(np.float32)
    return c, c2, onehot


def make_turn():
    at = {}

    def turn(sem, n=1):
        at[sem.name] = at.get(sem.name, 0) + n
        return at[sem.name]

    return turn


def program(nc, x, c, ada_w, ada_b, norm_mix_g, norm_ffn_g, t5_bias, a_w_qkv, a_q_gain, a_k_gain, a_lambda,
            a_subln_g, a_w_o, b_w_qkv, b_q_gain, b_k_gain, b_rel_bias, b_w_o, router_w, router_bias,
            moe_w_gate, moe_w_up, moe_w_down, c_2, ctx_2, c_ctx_2, w_mod_2, b_mod_2, norm1_w_2, w_in_2,
            w_s_2, b_s_2, q_norm_w_2, k_norm_w_2, hgrn_lb_logits_2, hgrn_norm_w_2, w_out_2, norm2_w_2,
            w_grp_2, b_grp_2, w_exp_2, b_exp_2, w1_2, w3_2, w2_2, cst_d, cst2_d, bucket_d, out):
    with ExitStack() as ctx:
        def sb(name, shape, dt=F32):
            return ctx.enter_context(nc.sbuf_tensor(name, shape, dt))

        def sem(name):
            return ctx.enter_context(nc.semaphore(name))

        ring = [sb(f"ring{s}", [P, KT * CHUNK]) for s in range(NSLOT)]
        xT = sb("xT", [P, KT, S])
        hh = sb("hh", [P, KT, 2 * S])
        sq = sb("sq", [P, KT * S])
        cst, cst2 = sb("cst", [P, N_CST]), sb("cst2", [32, N_CST2])
        vec = sb("vec", [P, N_VEC])
        csil = sb("csil", [P, KT, 32])
        modrow = sb("modrow", [P, CHUNK])
        mod = sb("mod", [P, 3, N_MOD])
        modc = sb("modc", [P, 2 * KT])
        gain1, gain2 = sb("gain1", [P, 3, KT]), sb("gain2", [P, 3, KT])
        gainc = sb("gainc", [P, KT])
        qscale = sb("qscale", [P, 4])
        rt, rstd = sb("rt", [P, S]), sb("rstd", [P, S])
        rw, rb = sb("rw", [P, KT, 16]), sb("rb", [P, 16])
        rw2, rb2 = sb("rw2", [P, KT, 36]), sb("rb2", [P, 36])
        eps = sb("eps", [P, 1])
        nlam = sb("nlam", [P, 1])
        stat = sb("stat", [P, 4, 8])
        nit = sb("nit", [P, 2], I32)
        arena = sb("arena", [P, 13448])

        def view(at, *shape):
            n = int(np.prod(shape))
            v = arena[:, at:at + n]
            if len(shape) == 2:
                v = v.rearrange("p (a b) -> p a b", a=shape[0])
            elif len(shape) == 3:
                v = v.rearrange("p (a b c) -> p a b c", a=shape[0], b=shape[1])
            elif len(shape) == 4:
                v = v.rearrange("p (a b c d) -> p a b c d", a=shape[0], b=shape[1], c=shape[2])
            return v

        vecrow = view(0, 2, P)
        t5row = arena[0:8, 256:768]
        lamrow = arena[0:1, 768:1024]
        lamtmp = arena[0:1, 1024:1160]
        bucket = arena[0:32, 1160:1672]
        t5b = arena[0:32, 1672:1680]
        raw = view(0, 16, S)
        v_tok = view(4096, TT, D)
        bias = view(6144, 16, S)
        s_sb = view(10240, 4, 2, S)
        probT = view(12288, 2, 2, S)
        h_tok = view(0, TT, D)
        x_sel = view(2048, KT, 2 * SLOTS)
        hid, hidT = view(3072, FF), view(3584, FT, 2 * SLOTS)
        gate_act = sq[:, 0:FF]
        y_sel = view(4096, D)
        pick = view(5120, TT, 2 * SLOTS)
        pick_g = view(5376, TT, 2 * SLOTS)
        spread_g = view(5632, S)
        slot_of, gate_of = view(5888, TT, 130), view(6148, TT, 130)
        r0 = 6408
        ctx_tok = view(7300, TT, D)
        ws = view(9348, 4, P)
        bs = arena[0:1, 9860:10372]
        cT = view(10372, KT, S)
        uT, vm = view(0, 2, S), view(512, TT, S)
        q2, k2, vb = view(1024, 4, S), view(2048, 512), view(2560, 4, P)
        wsT = view(3072, 4, P)
        p2, pT2 = view(8704, 4, 512), view(4608, 4, S)
        qh, vh, gs = view(5632, 2, S), view(6144, 4, S), view(7168, 2, S)
        z = view(11400, 2, 2, 2 * S)
        bsub, epad, qq = view(3584, 2, 2, S), view(4608, 2, 2, S), view(4608, 2, 2, S)
        sc, dm = view(2056, 2, P), view(10752, 4, P)
        key_tok = view(8704, 2, 2, 4, P)
        step, decay = view(11264, 2, 2, NSUB), view(11328, 2, 2, NSUB)
        dmT = view(0, 2, 4, P)
        sc_rows = arena[0:64, 1024:1536]
        kd = view(7680, 2, 512)
        o2, osq = view(7680, 2, S), view(8192, 2, S)
        LK = z
        lnb = sq[:, :].rearrange("p (a b c) -> p a b c", a=2, b=2)
        oT = hh[:, :, S:2 * S]
        ymix = hh[:, :, 0:S]

        def K(at, n=P, rows=P):
            return cst[0:rows, at:at + n]

        ident, ones = K(C_ID), K(C_ONE)
        bank = [ctx.enter_context(nc.psum_tensor(f"bank{i}", [P, 512], F32)) for i in range(2)]
        pair = [ctx.enter_context(nc.psum_tensor(f"pair{i}", [P, 2, 512], F32)) for i in range(2)]
        b = [bank[0][:, :], bank[1][:, :], pair[0][:, 0, :], pair[0][:, 1, :], pair[1][:, 0, :], pair[1][:, 1, :]]
        bank6 = ctx.enter_context(nc.psum_tensor("bank6", [P, 512], F32))
        bank7 = ctx.enter_context(nc.psum_tensor("bank7", [P, 512], F32))
        b += [bank6[:, :], bank7[:, :]]
        t5_dram = nc.dram_tensor("t5_rows", (8, 512), F32, kind="Internal").ap()

        const_in, x_in = sem("const_in"), sem("x_in")
        t5_row, t5_out, bias_in = sem("t5_row"), sem("t5_out"), sem("bias_in")
        l2_in, out_done = sem("l2_in"), sem("out_done")
        full = [sem(f"slot_full{s}") for s in range(NSLOT)]
        dve_step, act_step = sem("dve_step"), sem("act_step")
        eps_ready, turned, vec_ready, csil_ready = sem("eps_ready"), sem("turned"), sem("vec_ready"), sem("csil_ready")
        x_ready, mod_rows, modrow_ready = sem("x_ready"), sem("mod_rows"), sem("modrow_ready")
        mod_cols, mod_ready = sem("mod_cols"), sem("mod_ready")
        lam_step, lam_exp, lam_bc = sem("lam_step"), sem("lam_exp"), sem("lam_bc")
        t5_ps = sem("t5_ps")
        sq_ready, ssq_ps, rt_ready, h_ready = sem("sq_ready"), sem("ssq_ps"), sem("rt_ready"), sem("h_ready")
        qk_proj, raw_ready, rs_ready, bc_ps, norm_ready = (sem(n) for n in ("qk_proj", "raw_ready", "rs_ready", "bc_ps", "norm_ready"))
        v_proj, v_ready, flip_ps, bias_ready = (sem(n) for n in ("v_proj", "v_ready", "flip_ps", "bias_ready"))
        scores_ps, s_added, max_ready, exp_ready, prob_ready = (sem(n) for n in ("scores_ps", "s_added", "max_ready", "exp_ready", "prob_ready"))
        turn_ps, probT_ready, pv_ps, o_ready = (sem(n) for n in ("turn_ps", "probT_ready", "pv_ps", "o_ready"))
        out_proj, x_attn = sem("out_proj"), sem("x_attn")
        logits_ps, h_turned, h_tok_ready = sem("logits_ps"), sem("h_turned"), sem("h_tok_ready")
        score_ready, mask_ready, rank_ps, n_ready = (sem(n) for n in ("score_ready", "mask_ready", "rank_ps", "n_ready"))
        in_proj, in_ready = sem("in_proj"), sem("in_ready")
        vm_ready, mix_ps, ymix_ready = sem("vm_ready"), sem("mix_ps"), sem("ymix_ready")
        prod_ready, sc_ps, sc_ready, dm_ready = (sem(n) for n in ("prod_ready", "sc_ps", "sc_ready", "dm_ready"))
        keys_turned, key_tok_ready, spread_v = sem("keys_turned"), sem("key_tok_ready"), sem("spread_v")
        update_ps, state_ready = sem("update_ps"), sem("state_ready")
        out_ps, dmT_ready, o2_ready = sem("out_ps"), sem("dmT_ready"), sem("o2_ready")
        arg_ready, prod_exp = sem("arg_ready"), sem("prod_exp")
        gap_ready, gap_exp = sem("gap_ready"), sem("gap_exp")
        vec_ps, vm_sums, vm_rt = sem("vec_ps"), sem("vm_sums"), sem("vm_rt")
        dm_ps, ln_ready, log_ready, decays_ready = sem("dm_ps"), sem("ln_ready"), sem("log_ready"), sem("decays_ready")
        out_tok = sem("out_tok")
        MOE = []
        for l in range(3):
            MOE.append({n: sem(f"{n}_{l}") for n in (
                "pick_ready", "pickg_ready", "gather_a", "gather_b", "sel_a", "sel_b", "gate_ps", "silu_ready", "up_ps",
                "hid_ready", "hid_turned", "hidT_ready", "gate_turned", "down_a", "down_b", "y_a", "y_b",
                "comb_ps", "added")})
            MOE[l]["done"] = (MOE[l]["gate_ps"], MOE[l]["up_ps"], MOE[l]["down_b"])
            MOE[l]["full"] = [sem(f"{n}_full_{l}") for n in ("gate", "up", "down")]

        def columns(w, n):
            return w[:, n * CHUNK:(n + 1) * CHUNK].rearrange("(k p) n -> p k n", p=P)

        MOD_W = (ada_w[0], ada_w[1], w_mod_2[0])
        QKV, W_O = (a_w_qkv[0], b_w_qkv[0], w_in_2[0]), (a_w_o[0], b_w_o[0], w_out_2[0])
        GATE_W = (moe_w_gate[0], moe_w_gate[1], w1_2[0])
        UP_W = (moe_w_up[0], moe_w_up[1], w3_2[0])
        DOWN_W = (moe_w_down[0], moe_w_down[1], w2_2[0])
        IN_PARTS = [["u0", "u1", "vm0", "vm1"], ["q0", "q1", "q2", "q3"],
                    ["k", "vb0", "vb1", "vb2", "vb3", "qh0", "qh1"], ["zf0", "zf1", "zb0", "zb1"],
                    ["vh0", "vh1", "vh2", "vh3", "g0", "g1"]]
        IN_ORDER = (3, 4, 0, 1, 2)
        PARTS = [(n, part) for n in IN_ORDER for part in IN_PARTS[n]]
        parts_to = lambda last: 1 + [part for _, part in PARTS].index(last)
        chunks = []

        MOD_START = range(0, 4)
        MOD_QK, MOD_ATTN = (range(4, 12), range(20, 28)), (range(12, 20), range(28, 36))

        MOD_ON_DVE = set(range(4, 12)) | set(range(20, 24))
        rows_copied = lambda g: sum(n not in MOD_ON_DVE for n in range(g + 1))

        def add_mod(g):
            chunks.append((columns(MOD_W[g // 12], g % 12), mod_rows, g + 1))
            mod_at[g] = len(chunks) - 1

        def add_out(l):
            for n in range(2):
                chunks.append((columns(W_O[l], n), out_proj, 8 * l + 4 * (n + 1)))

        moe_at, mod_at, qkv_at, out_at = [], {}, [], []
        for g in MOD_START:
            add_mod(g)
        for l in range(2):
            qkv_at.append([])
            for n in range(6):
                qkv_at[l].append(len(chunks))
                if n < 4:
                    chunks.append((columns(QKV[l], n), qk_proj, 16 * l + 4 * (n + 1)))
                    for g in MOD_QK[l][2 * n:2 * n + 2]:
                        add_mod(g)
                else:
                    chunks.append((columns(QKV[l], n), v_proj, 4 * l + 2 * (n - 3)))
            for g in MOD_ATTN[l]:
                add_mod(g)
            out_at.append(len(chunks))
            add_out(l)
            moe_at.append(len(chunks))
        done, in_at = 0, len(chunks)
        for n in IN_ORDER:
            done += len(IN_PARTS[n])
            chunks.append((columns(QKV[2], n), in_proj, done))
        out_at.append(len(chunks))
        add_out(2)
        moe_at.append(len(chunks))

        def slot_of_chunk(n):
            return n % NSLOT

        def moe_slot(l, a, m):
            return (moe_at[l] + 2 * m + a) % NSLOT

        UNITS = [(hp, d) for hp in range(2) for d in range(2)]

        const_loads = []

        def const(dst, src):
            const_loads.append((dst, src))

        const(cst[:, :], cst_d)
        const(cst2[:, :], cst2_d)
        const(bucket, bucket_d)
        const(t5b, t5_bias)
        rows = lambda r, n: arena[r % P:r % P + n, (r // P) * P:(r // P + 1) * P]
        as_rows = lambda a: a.rearrange("(r q) -> r q", q=P)
        for l in range(3):
            const(rows(V_ADA[l], 48), as_rows(b_mod_2[0] if l == 2 else ada_b[l]))
        const(rows(V_C, 8), as_rows(c[0]))
        const(rows(V_C + 8, 8), as_rows(c_2[0]))
        const(rows(V_C + 16, 8), as_rows(c_ctx_2))
        const(rows(V_NORM1, 8), as_rows(norm1_w_2[0]))
        for l in range(2):
            const(rows(V_MIX[l], 8), as_rows(norm_mix_g[l]))
            const(rows(V_FFN[l], 8), as_rows(norm_ffn_g[l]))
        const(rows(V_FFN[2], 8), as_rows(norm2_w_2[0]))
        for r, g in ((GAIN_AQ, a_q_gain), (GAIN_AK, a_k_gain), (GAIN_BQ, b_q_gain), (GAIN_BK, b_k_gain),
                     (GAIN_Q2, q_norm_w_2), (GAIN_K2, k_norm_w_2), (GAIN_O2, hgrn_norm_w_2)):
            for half in range(2):
                const(rows(r, 1)[:, half * HEAD:(half + 1) * HEAD], g)
        const(rows(GAIN_SUB, 1), a_subln_g)
        const(lamrow, a_lambda.rearrange("a n d -> a (n d)"))
        const(rw[:, :, :], router_w.rearrange("(k p) e -> p k e", p=P))
        const(rb[:, :], router_bias.partition_broadcast(P))
        const(rw2[:, :, 0:GROUPS], w_grp_2[0].rearrange("(k p) e -> p k e", p=P))
        const(rw2[:, :, GROUPS:36], w_exp_2[0].rearrange("(k p) e -> p k e", p=P))
        const(rb2[:, 0:GROUPS], b_grp_2[0].partition_broadcast(P))
        const(rb2[:, GROUPS:36], b_exp_2[0].partition_broadcast(P))

        block = ctx.enter_context(nc.Block())

        @block.sync
        def _(sp):
            turn = make_turn()
            for dst, src in const_loads:
                sp.dma_start(dst, src, allow_slow_non_contiguous=True).then_inc(const_in, 16)
            sp.dma_start(sq[:, :].rearrange("p (t d) -> p t d", t=TT),
                         x[0].rearrange("(t p) d -> p t d", p=P)).then_inc(x_in, 16)

            def load(n):
                src, _, _ = chunks[n]
                if n >= NSLOT and n - NSLOT not in fenced:
                    _, used, value = chunks[n - NSLOT]
                    sp.wait_ge(used, value)
                k = src.shape[1]
                s = slot_of_chunk(n)
                sp.dma_start(ring[s][:, :].rearrange("p (k n) -> p k n", k=k), src).then_inc(full[s], 16)

            fenced = set()
            more_rounds = [None] * 3

            def expert(l, a, m, e):
                s = moe_slot(l, a, m)
                w = (GATE_W, UP_W, DOWN_W)[m][l]
                src = w[bass.ds(e, 1)].rearrange("a (k p) n -> p (a k) n", p=P)
                sp.dma_start(ring[s][:, :].rearrange("p (k n) -> p k n", k=FT if m == 2 else KT),
                             src).then_inc(MOE[l]["full"][m], 16)

            def load_hybrid():
                sp.wait_ge(x_attn, 16)
                sp.dma_start(ctx_tok, ctx_2[0].rearrange("(t p) d -> p t d", p=P)).then_inc(l2_in, 16)
                sp.dma_start(ws, w_s_2[0].rearrange("h t s -> t h s")).then_inc(l2_in, 16)
                sp.dma_start(bs, b_s_2.rearrange("a h t -> a (h t)")).then_inc(l2_in, 16)

            def experts(l):
                E, M = EXPERTS[l], MOE[l]
                for m in range(3):
                    for a in range(2):
                        n = moe_at[l] + 2 * m + a - NSLOT
                        _, used, value = chunks[n]
                        sp.wait_ge(used, value)
                        if l == 2 and m + a == 0:
                            sp.wait_ge(out_ps, 3)
                        expert(l, a, m, a)
                if l == 1:
                    load_hybrid()
                with sp.Fori(1, E // 2) as i:
                    for m in range(3):
                        for a in range(2):
                            sp.wait_ge(M["done"][m], i)
                            expert(l, a, m, 2 * i + a)
                sp.wait_ge(n_ready, turn(n_ready))
                more = sp.value_load(nit[0:1, 1:2], min_val=0, max_val=ROUNDS - 1)
                with sp.If(more > 0):
                    with sp.Fori(0, more) as r:
                        with sp.Fori(0, E // 2) as i:
                            for m in range(3):
                                for a in range(2):
                                    sp.wait_ge(M["done"][m], r * (E // 2) + i + E // 2)
                                    expert(l, a, m, 2 * i + a)
                more_rounds[l] = more

            def after_experts(l, n):
                for k in range(NSLOT):
                    sp.wait_ge(MOE[l]["done"][k // 2], more_rounds[l] * (EXPERTS[l] // 2) + EXPERTS[l] // 2)
                    fenced.add(n + k - NSLOT)
                    load(n + k)

            for n in range(12):
                load(n)
                if n == 0:
                    sp.wait_ge(t5_row, turn(t5_row))
                    sp.dma_start(t5_dram, t5row).then_inc(t5_out, 16)
            sp.wait_ge(t5_out, 16)
            sp.dma_start(bias[:, 0:8, :], bass.AP(t5_dram.tensor, 0, [[1, P], [512, 8], [1, S]])).then_inc(bias_in, 16)
            for n in range(12, moe_at[0]):
                load(n)
            experts(0)
            after_experts(0, moe_at[0])
            sp.wait_ge(MOE[0]["added"], more_rounds[0] * (EXPERTS[0] // 2 * 4) + (EXPERTS[0] // 2 * 4 + 2))
            sp.dma_start(bias[:, :, :], bass.AP(b_rel_bias.tensor, 1, [[1, P], [513, 16], [1, S]])).then_inc(bias_in, 16)
            for n in range(moe_at[0] + NSLOT, moe_at[1]):
                load(n)
            experts(1)
            after_experts(1, moe_at[1])
            for n in range(moe_at[1] + NSLOT, moe_at[2]):
                load(n)
            experts(2)
            for t in range(TT):
                sp.wait_ge(out_tok, 2 * (t + 1))
                sp.dma_start(out[0, t * P:(t + 1) * P, :], sq[:, t * D:(t + 1) * D]).then_inc(out_done, 16)
            sp.wait_ge(out_done, 16 * TT)

        score_bank = lambda u: b[2 + u % 4].rearrange("p (m k) -> p m k", m=2)
        score2_bank = lambda u: b[(0, 1, 6, 7)[u % 4]]
        sums = (b[7], b[4])
        R8 = [ring[s][:, :].rearrange("p (k n) -> p k n", k=KT) for s in range(NSLOT)]
        R4 = [ring[s][:, :].rearrange("p (k n) -> p k n", k=FT) for s in range(NSLOT)]

        def cols(t):
            return slice(t * P, (t + 1) * P)

        def half(m):
            return slice(m * HEAD, (m + 1) * HEAD)

        mod_acc = lambda g: arena[:, 10240 + CHUNK * (g % 2):10240 + CHUNK * (g % 2 + 1)]

        def mod_columns(g):
            l, n = divmod(g, 12)
            width = 2 if l == 2 and n < 4 else 1
            bank = b[0] if any(g in r for r in MOD_ATTN) else b[7]
            return bank[:, 0:4 * width].rearrange("p (n w) -> p n w", w=width), width

        slot = ring[moe_slot(2, 0, 0)]
        bpad = slot[:, 0:4 * (S + 1)].rearrange("p (a b t) -> p a b t", a=2, b=2)
        nlk = slot[:, 4 * (S + 1):4 * (S + 1) + 8 * S].rearrange("p (h a b t) -> p h a b t", h=2, a=2, b=2)
        lks = nlk[:, 0]
        state = ring[moe_slot(2, 1, 0)][:, :].rearrange("p (d h j v) -> p d h j v", d=2, h=2, j=NSUB)
        v_spread = ring[moe_slot(2, 0, 1)][:, :].rearrange("p (t h c) -> p t h c", t=TT, h=4)

        def sub_chunk(d, n):
            return n if d == 0 else NSUB - 1 - n

        def update_bank(d, hp, tile):
            return b[2 * tile + hp] if d == 0 else b[6 + hp] if tile == 1 else b[hp]

        def ref_col(d, j):
            return SUB * j if d == 0 else SUB * (j + 1)

        def seen_by(d, i):
            return slice(i, SUB) if d == 0 else slice(0, i + 1)

        def prod_of(q):
            d, i = divmod(q, SUB)
            buf = sq[:, q % 4 * 512:(q % 4 + 1) * 512]
            return buf.rearrange("p (n t) -> p n t", t=SUB)[:, :, seen_by(d, i)]

        vm_sq, vm_stat = view(7680, TT, S), arena[:, 8192:8216]

        def route_layout(E):
            at, r = r0, {}
            for name, shape in (("score", (TT, 16)), ("sel", (TT, 16)), ("sums", (TT * GROUPS, 6)), ("logits", (TT, 36)),
                                ("g8", (TT, 8)), ("best", (TT, 8)), ("number", (TT, 2)), ("gmask", (TT, GROUPS)),
                                ("masked", (TT, E)), ("fill", (TT, E)), ("hot0", (TT, E)), ("hot1", (TT, E)),
                                ("mask", (TT, E)), ("gate", (TT, E)), ("total", (TT,)), ("inv", (TT,)), ("inv1", (TT,)),
                                ("most", (1,)), ("steps", (ROUNDS - 1,)), ("gap", (TT, 5)), ("gap_exp", (TT, 5))):
                r[name] = view(at, *shape)
                at += int(np.prod(shape))
            r["index"] = arena[:, at:at + TT * 8].bitcast(U32).rearrange("p (t n) -> p t n", t=TT)
            r["hot"] = (r["hot0"], r["hot1"])
            assert at + TT * 8 <= 7300
            return r

        ROUTE = [route_layout(E) for E in EXPERTS]
        route_work = lambda l: ROUTE[l]
        route_mask = lambda l: ROUTE[l]["mask"]
        route_score = lambda l: ROUTE[l]["score"]
        route_gap, route_gap_exp = ROUTE[2]["gap"], ROUTE[2]["gap_exp"]

        @block.tensor
        def _(pe):
            turn = make_turn()
            mm = nc.tensor.matmul

            def chunk_in(n):
                s = slot_of_chunk(n)
                pe.wait_ge(full[s], 16 * (n // NSLOT + 1))
                return R8[s]

            def mod_products(g, bank):
                w = chunk_in(mod_at[g])
                for k in range(KT):
                    q = slice(k % 4 * 32, k % 4 * 32 + 32)
                    last = mm(bank[q, :], csil[:, k, :], w[:, k, :], start=(k < 4), stop=(k >= KT - 4))
                last.then_inc(mod_rows, 1)

            def mod_turn(g):
                o, width = mod_columns(g)
                if g in MOD_ON_DVE:
                    pe.wait_ge(mod_rows, g + 1)
                else:
                    pe.wait_ge(modrow_ready, rows_copied(g))
                if g >= 1:
                    pe.wait_ge(mod_ready, g)
                rows = mod_acc(g) if g in MOD_ON_DVE else modrow[:, :]
                one = K(C_ONE, 1) if g in MOD_ON_DVE else K(C_MOD + (g // 12 == 2), width)
                for s4 in range(4):
                    last = mm(o[:, s4, :], rows[:, cols(s4)], one, start=True, stop=True)
                last.then_inc(mod_cols, 1)

            def square_sum(k):
                pe.wait_ge(sq_ready, turn(sq_ready))
                last = mm(b[7][:, 0:S], ones, sq[:, k * S:(k + 1) * S], start=(k == 0), stop=(k == KT - 1))
                if k == KT - 1:
                    last.then_inc(ssq_ps, 1)

            def square_sums():
                pe.wait_ge(sq_ready, turn(sq_ready))
                for k in range(KT):
                    last = mm(b[7][:, 0:S], ones, sq[:, k * S:(k + 1) * S], start=(k == 0), stop=(k == KT - 1))
                last.then_inc(ssq_ps, 1)

            def qkv(l):
                at = qkv_at[l]
                pe.wait_ge(h_ready, turn(h_ready))

                def project(sl):
                    if sl % 4 == 0:
                        project.w = chunk_in(at[sl // 4])
                    for k in range(KT):
                        last = mm(b[sl % 2][:, 0:S], project.w[:, k, cols(sl % 4)], hh[:, k, 0:S],
                                  start=(k == 0), stop=(k == KT - 1))
                    last.then_inc(qk_proj, 1)

                def sums(sl):
                    pe.wait_ge(raw_ready, turn(raw_ready))
                    last = mm(b[2][0:32, 0:S], K(C_SEL + 32 * sl, 32), sq[:, (sl % 8) * S:(sl % 8 + 1) * S],
                              start=(sl == 0), stop=(sl == 15))
                    if sl == 15:
                        last.then_inc(ssq_ps, 1)

                project(0)
                for sl in range(1, 16):
                    project(sl)
                    sums(sl - 1)
                    if sl % 2 == 1:
                        if MOD_QK[l][sl // 2] not in MOD_ON_DVE:
                            mod_products(MOD_QK[l][sl // 2], b[3])
                    else:
                        mod_turn(MOD_QK[l][sl // 2 - 1])
                sums(15)
                mod_turn(MOD_QK[l][-1])
                flips = l + 1

                def flip(n):
                    if n >= 2:
                        pe.wait_ge(bias_ready, turn(bias_ready))
                    mm(b[6 + n % 2], K(C_FLIP), bias[:, 2 * n:2 * n + 2, :], start=True, stop=True).then_inc(flip_ps, 1)

                for g in range(4):
                    n, t = divmod(g, TT)
                    if t == 0:
                        w = chunk_in(at[4 + n])
                    if n == 1:
                        pe.wait_ge(v_ready, turn(v_ready))
                    for k in range(KT):
                        last = mm(b[t], hh[:, k, cols(t)], w[:, k, :], start=(k == 0), stop=(k == KT - 1))
                    last.then_inc(v_proj, 1)
                    if g == 0:
                        pe.wait_ge(bias_in, turn(bias_in, 16))
                        pe.wait_ge(mod_ready, MOD_QK[l][-1] + 1)
                        pe.wait_ge(rs_ready, turn(rs_ready))
                    for f in range(flips):
                        flip(flips * g + f)
                    for sl in range(4 * g, 4 * g + 4):
                        if sl >= 4:
                            pe.wait_ge(norm_ready, turn(norm_ready))
                        at2 = C2_SPREAD + P * sl
                        mm(b[2 + sl % 4][:, 0:S], cst2[0:32, at2:at2 + P], rstd[0:32, :],
                           start=True, stop=True).then_inc(bc_ps, 1)
                pe.wait_ge(norm_ready, turn(norm_ready, 4))
                pe.wait_ge(bias_ready, turn(bias_ready, 2))
                pe.wait_ge(v_ready, turn(v_ready, 2))

            def attention(l):
                def scores(u):
                    h, qt = divmod(u, TT)
                    if u >= 4:
                        pe.wait_ge(s_added, 16 * l + u - 3)
                    for m in range(2):
                        if m == 1:
                            pe.wait_ge(scores_ps, 32 * l + 2 * u + 1)
                        mm(score_bank(u)[:, m, 0:P * (qt + 1)], raw[half(m), h, cols(qt)],
                           raw[half(m), 8 + h, 0:P * (qt + 1)], start=True, stop=True).then_inc(scores_ps, 1)

                maps = 1 if l == 0 else 2

                def transposes(u):
                    qt = u % TT
                    pe.wait_ge(prob_ready, turn(prob_ready))
                    if u >= 1:
                        pe.wait_ge(probT_ready, 16 * l + u)
                    for kt in range(qt + 1):
                        for m in range(maps):
                            last = nc.tensor.transpose(b[6][:, cols(kt * maps + m)], s_sb[:, u % 4, m, cols(kt)], ident)
                    last.then_inc(turn_ps, 1)

                def values(h):
                    pe.wait_ge(probT_ready, 16 * l + 2 * h + 2)
                    if h >= 1:
                        pe.wait_ge(o_ready, 8 * l + h)
                    wide = P // maps
                    for m in range(maps):
                        rows = slice(m * wide, (m + 1) * wide)
                        for kt in range(TT):
                            last = mm(b[7][rows, kt * P:S], v_tok[:, kt, h * P + m * wide:h * P + (m + 1) * wide],
                                      probT[:, kt, m, kt * P:S], start=(kt == 0), stop=(kt == TT - 1))
                    last.then_inc(pv_ps, 1)

                scores(0)
                scores(1)
                for u in range(16):
                    if u < 14:
                        scores(u + 2)
                    if u % 2 == 1:
                        mod_products(MOD_ATTN[l][u // 2], b[1])
                    transposes(u)
                    if u % 2 == 0 and u >= 2:
                        mod_turn(MOD_ATTN[l][u // 2 - 1])
                    if u % TT == TT - 1:
                        values(u // TT)
                mod_turn(MOD_ATTN[l][-1])
                pe.wait_ge(o_ready, turn(o_ready, 8))
                if l == 0:
                    for h in range(8):
                        last = mm(b[6][0:16, 0:S], K(C_SEL8 + 16 * h, 16), sq[:, h * S:(h + 1) * S],
                                  start=(h == 0), stop=(h == 7))
                    last.then_inc(ssq_ps, 1)
                    pe.wait_ge(rs_ready, turn(rs_ready))
                    for h in range(8):
                        if h >= 2:
                            pe.wait_ge(norm_ready, turn(norm_ready))
                        at2 = C2_SPREAD + P * h
                        mm(b[4 + h % 2][:, 0:S], cst2[0:16, at2:at2 + P], rstd[0:16, :],
                           start=True, stop=True).then_inc(bc_ps, 1)
                    pe.wait_ge(norm_ready, turn(norm_ready, 2))

            def project_out(l, src):
                for n in range(2):
                    w = chunk_in(out_at[l] + n)
                    for s4 in range(4):
                        c = 4 * n + s4
                        if c >= 4:
                            pe.wait_ge(x_attn, 8 * l + c - 3)
                        for k in range(KT):
                            last = mm(b[2 + c % 4][:, 0:S], w[:, k, cols(s4)], src[:, k, :],
                                      start=(k == 0), stop=(k == KT - 1))
                        last.then_inc(out_proj, 1)
                        if c >= 2:
                            square_sum(c - 2)
                square_sum(KT - 2)
                square_sum(KT - 1)

            def route(l):
                E = EXPERTS[l]
                w, width = (rw2, 36) if l == 2 else (rw, 16)
                pe.wait_ge(h_ready, turn(h_ready))
                for t in range(TT):
                    for k in range(KT):
                        last = mm(b[6][:, t * width:(t + 1) * width], hh[:, k, cols(t)], w[:, k, :],
                                  start=(k == 0), stop=(k == KT - 1))
                last.then_inc(logits_ps, 1)
                for t in range(TT):
                    for k in range(KT):
                        last = nc.tensor.transpose(b[2 * t + k // 4][:, cols(k % 4)], hh[:, k, cols(t)], ident)
                        if k % 4 == 3:
                            last.then_inc(h_turned, 1)
                pe.wait_ge(mask_ready, turn(mask_ready))
                mask = route_mask(l)
                mm(b[7][:, 0:E], K(C_TRI), mask[:, 0, :], start=True, stop=True)
                for n, first in ((1, K(C_TRI)), (2, ones)):
                    mm(b[7][:, n * E:(n + 1) * E], first, mask[:, 1, :], start=True, stop=False)
                    last = mm(b[7][:, n * E:(n + 1) * E], ones, mask[:, 0, :], start=False, stop=True)
                last.then_inc(rank_ps, 1)

            def experts(l):
                M = MOE[l]

                def gather(part):
                    for k in range(4 * part, 4 * part + 4):
                        for t in range(TT):
                            last = mm(b[part][:, cols(k % 4)], h_tok[:, t, cols(k)], pick[:, t, :],
                                      start=(t == 0), stop=(t == TT - 1))
                    last.then_inc(M["gather_b" if part else "gather_a"], 1)

                def project(i, m):
                    pe.wait_ge(M["full"][m], 32 * i + 32)
                    for k in range(KT):
                        for a in range(2):
                            last = mm(b[2 + m][half(a), :], x_sel[:, k, half(a)], R8[moe_slot(l, a, m)][:, k, :],
                                      start=(k == 0), stop=(k == KT - 1))
                    last.then_inc(M["up_ps" if m else "gate_ps"], 1)

                def down(n):
                    for f in range(FT):
                        for a in range(2):
                            last = mm(b[5 + n][half(a), :], hidT[:, f, half(a)],
                                      R4[moe_slot(l, a, 2)][:, f, n * 512:(n + 1) * 512],
                                      start=(f == 0), stop=(f == FT - 1))
                    last.then_inc(M["down_b" if n else "down_a"], 1)

                pe.wait_ge(n_ready, l + 1)
                n = pe.value_load(nit[0:1, 0:1], min_val=1, max_val=ROUNDS * EXPERTS[l] // 2)
                pe.wait_ge(h_tok_ready, turn(h_tok_ready, 4))
                pe.wait_ge(M["pick_ready"], 1)
                gather(0)
                gather(1)
                with pe.Fori(0, n) as i:
                    pe.wait_ge(M["sel_a"], i + 1)
                    pe.wait_ge(M["sel_b"], i + 1)
                    project(i, 0)
                    project(i, 1)
                    pe.wait_ge(M["pickg_ready"], i + 1)
                    pe.wait_ge(M["silu_ready"], i + 1)
                    for t in range(TT):
                        last = nc.tensor.transpose(b[2][:, cols(t)], pick_g[:, t, :], ident)
                    last.then_inc(M["gate_turned"], 1)
                    pe.wait_ge(M["pick_ready"], i + 2)
                    gather(0)
                    pe.wait_ge(M["hid_ready"], i + 1)
                    pe.wait_ge(M["added"], 4 * i + 2)
                    for f in range(FT):
                        last = nc.tensor.transpose(b[4][:, cols(f)], hid[:, cols(f)], ident)
                    last.then_inc(M["hid_turned"], 1)
                    gather(1)
                    pe.wait_ge(M["hidT_ready"], i + 1)
                    pe.wait_ge(M["full"][2], 32 * i + 32)
                    down(0)
                    down(1)
                    pe.wait_ge(M["y_a"], i + 1)
                    for r in range(4):
                        if r == 2:
                            pe.wait_ge(M["y_b"], i + 1)
                        pe.wait_ge(M["added"], 4 * i + r + 1)
                        for k in range(2):
                            last = mm(sums[r % 2][:, k * S:(k + 1) * S], y_sel[:, cols(2 * r + k)], spread_g,
                                      start=True, stop=True)
                        last.then_inc(M["comb_ps"], 1)
                pe.wait_ge(M["sel_a"], n + 1)
                pe.wait_ge(M["sel_b"], n + 1)
                pe.wait_ge(M["added"], n * 4 + 2)

            def turn_tokens(src, last_sem):
                for k in range(KT):
                    for t in range(TT):
                        last = nc.tensor.transpose(b[1 + k // 2][:, cols(k % 2 * TT + t)], src(t, k), ident)
                    if k % 2 == 1:
                        last.then_inc(last_sem, 1)

            def hybrid():
                pe.wait_ge(l2_in, 48)
                turn_tokens(lambda t, k: ctx_tok[:, t, cols(k)], turned)
                square_sums()
                square_sums()
                pe.wait_ge(h_ready, turn(h_ready, 2))
                for idx, (n, part) in enumerate(PARTS):
                    if part == IN_PARTS[n][0]:
                        w = chunk_in(in_at + IN_ORDER.index(n))
                    if idx >= 4:
                        pe.wait_ge(in_ready, idx - 3)
                    name, num = part.rstrip("0123456789"), part[len(part.rstrip("0123456789")):]
                    num = int(num or 0)
                    o = b[idx % 4]
                    for k in range(KT):
                        f = dict(start=(k == 0), stop=(k == KT - 1))
                        if name == "u":
                            last = mm(o[:, 0:S], w[:, k, cols(num)], hh[:, k, 0:S], **f)
                        elif name == "vm":
                            last = mm(o[:, 0:S], hh[:, k, cols(num)], w[:, k, 256:512], **f)
                        elif name == "q":
                            last = mm(o[:, 0:S], w[:, k, cols(num)], hh[:, k, 0:S], **f)
                        elif name == "k":
                            last = mm(o, w[:, k, 0:P], hh[:, k, :], **f)
                        elif name == "vb":
                            last = mm(o[:, 0:P], hh[:, k, cols(num)], w[:, k, P:2 * P], **f)
                        elif name == "qh":
                            last = mm(o[:, 0:S], w[:, k, cols(2 + num)], hh[:, k, 0:S], **f)
                        elif name in ("zf", "zb"):
                            last = mm(o, w[:, k, cols(num + 2 * (name == "zb"))], hh[:, k, :], **f)
                        elif name == "vh":
                            last = mm(o[:, 0:S], hh[:, k, cols(num)], w[:, k, 0:256], **f)
                        else:
                            last = mm(o[:, 0:S], w[:, k, cols(2 + num)], hh[:, k, 0:S], **f)
                    last.then_inc(in_proj, 1)
                for h in range(4):
                    last = nc.tensor.transpose(b[4][:, cols(h)], ws[:, h, :], ident)
                last.then_inc(turned, 1)
                pe.wait_ge(in_ready, len(PARTS) + 1)
                pe.wait_ge(vm_ready, 1)
                for h in range(4):
                    for t in range(TT):
                        o = b[5][half(h % 2), cols(h // 2 * TT + t)]
                        mm(o, vm[:, t, half(h)], wsT[:, h, :], start=True, stop=False)
                        last = mm(o, K(C_ONE, HEAD, 1), bs[:, cols(h)], start=False, stop=True)
                last.then_inc(mix_ps, 1)
                pe.wait_ge(in_ready, len(PARTS))
                pe.wait_ge(raw_ready, turn(raw_ready, 2))
                for j in range(4):
                    mm(b[6][0:32, 0:S], K(C_SEL + 32 * j, 32), sq[:, j * S:(j + 1) * S], start=(j == 0), stop=(j == 3))
                mm(b[7][0:32, :], K(C_SEL, 32), sq[:, 4 * S:6 * S], start=True, stop=True).then_inc(ssq_ps, 1)
                pe.wait_ge(rs_ready, turn(rs_ready))
                for j in range(4):
                    at2 = C2_SPREAD + P * j
                    last = mm(b[j // 2][:, j % 2 * S:(j % 2 + 1) * S], cst2[0:32, at2:at2 + P], rstd[0:32, :],
                              start=True, stop=True)
                    if j % 2 == 1:
                        last.then_inc(bc_ps, 1)
                mm(b[2], cst2[0:32, C2_SPREAD:C2_SPREAD + P], sq[0:32, 6 * S:8 * S], start=True, stop=True).then_inc(bc_ps, 1)
                for g in range(3):
                    pe.wait_ge(norm_ready, turn(norm_ready))
                    if g < 2:
                        last = mm(b[g], K(C_ROT), q2[:, 2 * g:2 * g + 2, :], start=True, stop=True)
                    else:
                        last = mm(b[2][:, 0:S], K(C_ROT), k2[:, 0:S], start=True, stop=True)
                    last.then_inc(bc_ps, 1)
                pe.wait_ge(norm_ready, turn(norm_ready, 3))
                for g in range(2):
                    mm(b[2 + g], K(C_DUP + P * g), k2, start=True, stop=True).then_inc(bc_ps, 1)
                pe.wait_ge(norm_ready, turn(norm_ready, 2))
                pe.wait_ge(ymix_ready, 1)

                def scores(u):
                    hd, qt = divmod(u, TT)
                    if u >= 4:
                        pe.wait_ge(exp_ready, 32 + u - 3)
                    mm(score2_bank(u), q2[half(hd % 2), hd // 2, cols(qt)], kd[half(hd % 2), hd // 4, :],
                       start=True, stop=True).then_inc(scores_ps, 1)

                def transposes(u):
                    pe.wait_ge(prob_ready, turn(prob_ready))
                    if u >= 2:
                        pe.wait_ge(probT_ready, 32 + u - 1)
                    for kt in range(4):
                        last = nc.tensor.transpose(b[2 + u % 2][:, cols(kt)], p2[:, u % 4, cols(kt)], ident)
                    last.then_inc(turn_ps, 1)

                def values(hd):
                    pe.wait_ge(probT_ready, 32 + 2 * hd + 2)
                    if hd >= 2:
                        pe.wait_ge(o_ready, 16 + hd - 1)
                    for kt in range(4):
                        last = mm(b[4 + hd % 2][half(hd % 2), 0:S], vb[:, kt, half(hd // 4)], pT2[:, kt, :],
                                  start=(kt == 0), stop=(kt == 3))
                    last.then_inc(pv_ps, 1)

                scores(0)
                scores(1)
                for u in range(16):
                    if u < 14:
                        scores(u + 2)
                    transposes(u)
                    if u % TT == TT - 1:
                        values(u // TT)
                pe.wait_ge(o_ready, 24)
                pe.wait_ge(decays_ready, 1)
                for n in range(4):
                    for kt in range(4):
                        last = nc.tensor.transpose(b[n][:, cols(kt)], LK[:, n // 2, n % 2, cols(kt)], ident)
                    last.then_inc(keys_turned, 1)
                pe.wait_ge(key_tok_ready, 4)
                for d in range(2):
                    for hp in range(2):
                        for c in range(TT):
                            for m in range(2):
                                at5 = (d * 2 + hp) * HEAD
                                last = mm(b[5][half(m), at5:at5 + HEAD], key_tok[:, d, hp, TT + c, half(m)],
                                          vh[:, TT + c, half(2 * hp + m)], start=(c == 0), stop=(c == TT - 1))
                last.then_inc(keys_turned, 1)

                def updates(d, tile):
                    for hp in range(2):
                        for m in range(2):
                            last = mm(update_bank(d, hp, tile)[half(m), :], key_tok[:, d, hp, tile, half(m)],
                                      v_spread[:, tile, 2 * hp + m, :], start=True, stop=True)
                    last.then_inc(update_ps, 1)

                pe.wait_ge(spread_v, 1)
                updates(0, 0)
                updates(0, 1)
                updates(1, 1)
                pe.wait_ge(state_ready, 1)
                for q in range(2 * SUB):
                    d, i = divmod(q, SUB)
                    if q == 10:
                        pe.wait_ge(state_ready, NSUB // 2 + 1)
                        updates(1, 0)
                    pe.wait_ge(prod_ready, q + 1)
                    prod = sq[:, q % 4 * 512:(q % 4 + 1) * 512]
                    mm(b[5][32 * d:32 * d + 32, :], K(C_SEL + 32 * i, 32), prod, start=(i == 0), stop=(i == SUB - 1)
                       ).then_inc(sc_ps, 1)
                    if q >= 1:
                        pe.wait_ge(state_ready, d * (NSUB - 1) + i + 1)
                    j = sub_chunk(d, i)
                    own = slice(j * SUB, (j + 1) * SUB)
                    for hp in range(2):
                        for m in range(2):
                            last = mm(b[4 - d][half(m), hp * S + own.start:hp * S + own.stop], state[half(m), d, hp, i, :],
                                      qq[half(m), d, hp, own], start=True, stop=True)
                last.then_inc(out_ps, 1)
                pe.wait_ge(act_step, 7)
                for n in range(4):
                    last = nc.tensor.transpose(b[6][:, n * 64:(n + 1) * 64], sc_rows[:, cols(n)], K(C_ID, 64, 64))
                last.then_inc(sc_ps, 1)
                def turn_scores(w):
                    pe.wait_ge(dm_ready, w + 1)
                    if w >= 2:
                        pe.wait_ge(dmT_ready, w - 1)
                    for n in range(4):
                        last = nc.tensor.transpose((b[2], b[0])[w % 2][:, cols(n)], dm[:, n, :], ident)
                    last.then_inc(dm_ps, 1)

                for w in range(len(UNITS)):
                    turn_scores(w)
                for hp in range(2):
                    pe.wait_ge(dmT_ready, 2 * hp + 2)
                    for t in range(TT):
                        for m in range(2):
                            for d in range(2):
                                last = mm(b[7][half(m), hp * S + t * P:hp * S + (t + 1) * P], vh[:, t, half(2 * hp + m)],
                                          dmT[:, d, 2 * t + m, :], start=(d == 0), stop=(d == 1))
                    last.then_inc(out_ps, 1)
                pe.wait_ge(o_ready, 25)
                for j in range(2):
                    last = mm(b[6][0:32, 0:S], K(C_SEL + 32 * j, 32), osq[:, j, :], start=(j == 0), stop=(j == 1))
                last.then_inc(ssq_ps, 1)
                pe.wait_ge(rs_ready, turn(rs_ready))
                for j in range(2):
                    at2 = C2_SPREAD + P * j
                    last = mm(b[5][:, j * S:(j + 1) * S], cst2[0:32, at2:at2 + P], rstd[0:32, :], start=True, stop=True)
                last.then_inc(bc_ps, 1)
                pe.wait_ge(ymix_ready, 2)

            pe.wait_ge(const_in, 16 * len(const_loads))
            nc.tensor.transpose(b[0][:, 0:P], vecrow[:, 0, :], ident)
            rest = N_VEC - P
            nc.tensor.transpose(b[0][:, P:N_VEC], vecrow[0:rest, 1, :], K(C_ID, rest, rest)).then_inc(vec_ps, 1)
            mm(b[5][0:8, :], t5b, bucket, start=True, stop=True).then_inc(t5_ps, 1)
            pe.wait_ge(x_in, 16)
            turn_tokens(lambda t, k: sq[:, t * D + k * P:t * D + (k + 1) * P], turned)
            pe.wait_ge(lam_step, 2)
            mm(b[6][:, 0:1], K(C_ONE, P, 1), lamtmp[:, 132:133], start=True, stop=True).then_inc(lam_bc, 1)
            pe.wait_ge(csil_ready, 1)
            for g in MOD_START:
                mod_products(g, b[0])
                mod_turn(g)
            pe.wait_ge(mod_ready, len(MOD_START))
            for l in range(2):
                square_sums()
                qkv(l)
                attention(l)
                project_out(l, oT)
                route(l)
                experts(l)
            hybrid()
            project_out(2, ymix)
            route(2)
            experts(2)
            for t in range(TT):
                for k in range(KT):
                    last = nc.tensor.transpose(b[2 * t + k // 4][:, cols(k % 4)], xT[:, k, cols(t)], ident)
                    if k % 4 == 3:
                        last.then_inc(turned, 1)

        @block.scalar
        def _(act):
            turn = make_turn()
            fn = nc.scalar.activation

            def squares(src):
                fn(sq[:, :].rearrange("p (k t) -> p k t", k=KT), src, ACT.Square).then_inc(sq_ready, 1)

            def root(src, dst, n, rows=P):
                fn(dst, src, ACT.Sqrt, bias=eps[0:rows, :], scale=1.0 / n).then_inc(rt_ready, 1)

            def norm(src):
                squares(src)
                act.wait_ge(ssq_ps, turn(ssq_ps))
                root(b[7][:, 0:S], rt[:, :], D)

            def norm_attended(l):
                for k in range(KT):
                    act.wait_ge(x_attn, 8 * l + k + 1)
                    fn(sq[:, k * S:(k + 1) * S], xT[:, k, :], ACT.Square).then_inc(sq_ready, 1)
                act.wait_ge(ssq_ps, turn(ssq_ps))
                root(b[7][:, 0:S], rt[:, :], D)

            def mod_copy(g, bank):
                act.wait_ge(mod_rows, g + 1)
                fn(modrow[:, :], bank, ACT.Copy).then_inc(modrow_ready, 1)

            def qkv(l):
                for sl in range(16):
                    act.wait_ge(qk_proj, turn(qk_proj))
                    fn(raw[:, sl, :], b[sl % 2][:, 0:S], ACT.Copy)
                    fn(sq[:, (sl % 8) * S:(sl % 8 + 1) * S], b[sl % 2][:, 0:S], ACT.Square).then_inc(raw_ready, 1)
                    if sl % 2 == 1 and MOD_QK[l][sl // 2] not in MOD_ON_DVE:
                        mod_copy(MOD_QK[l][sl // 2], b[3])
                act.wait_ge(ssq_ps, turn(ssq_ps))
                root(b[2][0:32, 0:S], rt[0:32, :], HEAD, 32)
                for n in range(2):
                    for t in range(TT):
                        act.wait_ge(v_proj, turn(v_proj))
                        fn(v_tok[:, t, n * 512:(n + 1) * 512], b[t], ACT.Copy).then_inc(v_ready, 1)

            def attention(l):
                maps = 1 if l == 0 else 2

                def exps(u):
                    act.wait_ge(max_ready, turn(max_ready))
                    wide = P * (u % TT + 1)
                    for m in range(2):
                        sc_ = s_sb[:, u % 4, m, 0:wide]
                        last = fn(sc_, sc_, ACT.Exp, bias=stat[:, u % 4, m:m + 1],
                                  accum_out=stat[:, u % 4, 2 + m:3 + m])
                    last.then_inc(exp_ready, 1)

                exps(0)
                exps(1)
                for u in range(16):
                    h, qt = divmod(u, TT)
                    if u % 2 == 1:
                        mod_copy(MOD_ATTN[l][u // 2], b[1])
                    act.wait_ge(turn_ps, turn(turn_ps))
                    fn(probT[:, 0:qt + 1, 0:maps, cols(qt)],
                       b[6][:, 0:(qt + 1) * maps * P].rearrange("p (k m q) -> p k m q", k=qt + 1, m=maps),
                       ACT.Copy).then_inc(probT_ready, 1)
                    if u < 14:
                        exps(u + 2)
                    if qt == TT - 1:
                        act.wait_ge(pv_ps, turn(pv_ps))
                        last = fn(oT[:, h, :], b[7][:, 0:S], ACT.Copy)
                        if l == 0:
                            last = fn(sq[:, h * S:(h + 1) * S], b[7][:, 0:S], ACT.Square)
                        last.then_inc(o_ready, 1)
                if l == 0:
                    act.wait_ge(ssq_ps, turn(ssq_ps))
                    root(b[6][0:16, 0:S], rt[0:16, :], P, 16)

            def route(l):
                act.wait_ge(logits_ps, turn(logits_ps))
                if l < 2:
                    fn(route_score(l), b[6][:, 0:TT * 16].rearrange("p (t e) -> p t e", t=TT),
                       ACT.Sigmoid).then_inc(score_ready, 1)
                for n in range(4):
                    act.wait_ge(h_turned, turn(h_turned))
                    fn(h_tok[:, n // 2, n % 2 * 512:(n % 2 + 1) * 512], b[n], ACT.Copy).then_inc(h_tok_ready, 1)
                if l == 2:
                    act.wait_ge(gap_ready, 1)
                    fn(route_gap_exp, route_gap, ACT.Exp).then_inc(gap_exp, 1)

            def experts(l):
                M = MOE[l]
                act.wait_ge(n_ready, l + 1)
                n = act.value_load(nit[0:1, 0:1], min_val=1, max_val=ROUNDS * EXPERTS[l] // 2)
                act.wait_ge(M["gather_a"], 1)
                fn(x_sel[:, 0:4, :], b[0].rearrange("p (k s) -> p k s", k=4), ACT.Copy).then_inc(M["sel_a"], 1)
                with act.Fori(0, n) as i:
                    act.wait_ge(M["gate_ps"], i + 1)
                    fn(gate_act, b[2], ACT.Silu).then_inc(M["silu_ready"], 1)
                    act.wait_ge(M["gate_turned"], i + 1)
                    fn(spread_g, b[2][:, 0:S], ACT.Copy)
                    act.wait_ge(M["gather_a"], i + 2)
                    fn(x_sel[:, 0:4, :], b[0].rearrange("p (k s) -> p k s", k=4), ACT.Copy).then_inc(M["sel_a"], 1)
                    act.wait_ge(M["hid_turned"], i + 1)
                    fn(hidT, b[4].rearrange("p (f s) -> p f s", f=FT), ACT.Copy).then_inc(M["hidT_ready"], 1)
                    act.wait_ge(M["down_a"], i + 1)
                    fn(y_sel[:, 0:512], b[5], ACT.Copy).then_inc(M["y_a"], 1)
                act.wait_ge(M["added"], n * 4 + 2)

            def hybrid():
                for n in range(4):
                    act.wait_ge(turned, turn(turned))
                    fn(cT[:, 2 * n:2 * n + 2, :], b[1 + n].rearrange("p (k t) -> p k t", k=2), ACT.Copy).then_inc(act_step, 1)
                norm(xT[:, :, :])
                act.wait_ge(h_ready, 5)
                act.wait_ge(act_step, 4)
                norm(cT)
                zz = z.rearrange("p a b t -> p (a b t)")
                for idx, (n, part) in enumerate(PARTS):
                    act.wait_ge(in_proj, idx + 1)
                    o = b[idx % 4]
                    num = int(part[-1]) if part[-1].isdigit() else 0
                    name = part[:-1] if part[-1].isdigit() else part
                    if name in ("u", "vm"):
                        last = fn((uT if name == "u" else vm)[:, num, :], o[:, 0:S], ACT.Gelu_apprx_tanh)
                    elif name in ("qh", "g"):
                        last = fn((qh if name == "qh" else gs)[:, num, :], o[:, 0:S], ACT.Silu)
                    elif name == "k":
                        last = fn(k2, o, ACT.Copy)
                    elif name in ("zf", "zb"):
                        last = fn(z[:, int(name == "zb"), num, :], o, ACT.Copy)
                    elif name == "vb":
                        last = fn(vb[:, num, :], o[:, 0:P], ACT.Copy)
                    else:
                        last = fn((q2 if name == "q" else vh)[:, num, :], o[:, 0:S], ACT.Copy)
                    last.then_inc(in_ready, 1)
                    if part == "zb1":
                        act.wait_ge(in_ready, parts_to("zb1"))
                        fn(sq[:, :], zz, ACT.Abs).then_inc(act_step, 1)
                        act.wait_ge(act_step, 5)
                        fn(sq[:, :], sq[:, :], ACT.Exp, scale=-1.0).then_inc(act_step, 1)
                        act.wait_ge(act_step, 6)
                        fn(sq[:, :], sq[:, :], ACT.Ln, bias=1.0).then_inc(ln_ready, 1)
                act.wait_ge(turned, turn(turned))
                fn(wsT, b[4].rearrange("p (h t) -> p h t", h=4), ACT.Copy).then_inc(in_ready, 1)
                act.wait_ge(vm_sums, 1)
                fn(vm_stat[:, 8:16], vm_stat[:, 0:8], ACT.Sqrt, bias=eps[:, :], scale=1.0 / HEAD).then_inc(vm_rt, 1)
                act.wait_ge(in_ready, len(PARTS))
                act.wait_ge(log_ready, 1)
                fn(sq[:, 0:4 * S], q2.rearrange("p j t -> p (j t)"), ACT.Square).then_inc(raw_ready, 1)
                fn(sq[:, 4 * S:6 * S], k2, ACT.Square).then_inc(raw_ready, 1)
                act.wait_ge(ssq_ps, turn(ssq_ps))
                root(b[6][0:32, 0:S], rt[0:32, :], HEAD, 32)
                root(b[7][0:32, :], sq[0:32, 6 * S:8 * S], HEAD, 32)

                fn(decay, step, ACT.Exp)
                fn(zz, zz, ACT.Exp).then_inc(decays_ready, 1)

                def exps(u):
                    act.wait_ge(max_ready, turn(max_ready))
                    fn(p2[:, u % 4, :], score2_bank(u), ACT.Exp, bias=stat[:, u % 4, 0:1],
                       accum_out=stat[:, u % 4, 2:3]).then_inc(exp_ready, 1)

                exps(0)
                exps(1)
                for u in range(16):
                    hd, qt = divmod(u, TT)
                    act.wait_ge(turn_ps, turn(turn_ps))
                    fn(pT2[:, :, cols(qt)], b[2 + u % 2].rearrange("p (k q) -> p k q", k=4), ACT.Copy).then_inc(probT_ready, 1)
                    if u < 14:
                        exps(u + 2)
                    if qt == TT - 1:
                        act.wait_ge(pv_ps, turn(pv_ps))
                        fn(ymix[half(hd % 2), 2 + hd // 2, :], b[4 + hd % 2][half(hd % 2), 0:S], ACT.Copy).then_inc(o_ready, 1)
                fn(qq.rearrange("p a b t -> p (a b t)"), bsub.rearrange("p a b t -> p (a b t)"), ACT.Exp).then_inc(decays_ready, 1)
                for n in range(4):
                    act.wait_ge(keys_turned, n + 1)
                    fn(key_tok[:, n // 2, n % 2], b[n].rearrange("p (t k) -> p t k", t=4), ACT.Copy).then_inc(key_tok_ready, 1)
                for q in range(2 * SUB):
                    act.wait_ge(arg_ready, q + 1)
                    pr = prod_of(q)
                    fn(pr, pr, ACT.Exp).then_inc(prod_exp, 1)
                act.wait_ge(sc_ps, 2 * SUB)
                fn(sc_rows, b[5][0:64, :], ACT.Copy).then_inc(act_step, 1)
                act.wait_ge(sc_ps, 2 * SUB + 1)
                for d in range(2):
                    last = fn(sc[:, d, :].rearrange("p (n m i) -> p n m i", n=4, m=2),
                              b[6][:, 0:256].rearrange("p (n d i m) -> p n d m i", n=4, d=2, i=SUB)[:, :, d], ACT.Copy)
                last.then_inc(sc_ready, 1)
                act.wait_ge(out_ps, 1)
                fn(o2, b[4].rearrange("p (j t) -> p j t", j=2), ACT.Copy).then_inc(act_step, 1)
                for w in range(len(UNITS)):
                    act.wait_ge(dm_ps, w + 1)
                    if w >= 2:
                        act.wait_ge(out_ps, 2)
                    fn(dmT[:, w % 2], (b[2], b[0])[w % 2].rearrange("p (n t) -> p n t", n=4), ACT.Copy).then_inc(dmT_ready, 1)
                act.wait_ge(o2_ready, 1)
                fn(osq, o2, ACT.Square).then_inc(o_ready, 1)
                act.wait_ge(ssq_ps, turn(ssq_ps))
                root(b[6][0:32, 0:S], rt[0:32, :], HEAD, 32)

            act.wait_ge(eps_ready, 1)
            act.wait_ge(t5_ps, 1)
            fn(t5row, b[5][0:8, :], ACT.Copy).then_inc(t5_row, 1)
            act.wait_ge(vec_ready, 1)
            fn(csil[:, :, 0:N_COND], vec[:, V_C:V_C + N_COND * KT].rearrange("p (a k) -> p k a", k=KT),
               ACT.Silu).then_inc(csil_ready, 1)
            act.wait_ge(lam_step, 1)
            fn(lamtmp[:, 130:132], lamtmp[:, 128:130], ACT.Exp).then_inc(lam_exp, 1)
            for n in range(4):
                act.wait_ge(turned, turn(turned))
                fn(xT[:, 2 * n:2 * n + 2, :], b[1 + n].rearrange("p (k t) -> p k t", k=2), ACT.Copy).then_inc(x_ready, 1)
            act.wait_ge(x_ready, 4)
            for g in MOD_START:
                mod_copy(g, b[0])
            for l in range(2):
                norm(xT[:, :, :])
                qkv(l)
                attention(l)
                norm_attended(l)
                route(l)
                experts(l)
            hybrid()
            norm_attended(2)
            route(2)
            experts(2)
            for n in range(4):
                act.wait_ge(turned, turn(turned))
                fn(sq[:, n * 512:(n + 1) * 512], b[n], ACT.Copy).then_inc(out_tok, 1)

        @block.gpsimd
        def _(pool):
            pool.wait_ge(in_ready, len(PARTS))
            mask = cst[:, C_DIAG:C_DIAG + P:SUB].unsqueeze(2).broadcast_to([P, P // SUB, HEAD])
            for t in range(TT):
                for h in range(4):
                    last = nc.gpsimd.tensor_tensor(v_spread[:, t, h, :].rearrange("p (j v) -> p j v", v=HEAD),
                                                   vh[:, t, half(h)].unsqueeze(1).broadcast_to([P, P // SUB, HEAD]),
                                                   mask, ALU.mult)
            last.then_inc(spread_v, 1)
            pool.wait_ge(log_ready, 1)
            pool.wait_ge(max_ready, 16 + 16 + 1)
            for q in range(2 * SUB):
                d, i = divmod(q, SUB)
                if q >= 4:
                    pool.wait_ge(sc_ps, q - 3)
                seen = seen_by(d, i)
                key = lks[:, d].rearrange("p b (j t) -> p (b j) t", t=SUB)[:, :, i:i + 1]
                nc.gpsimd.tensor_tensor(prod_of(q), bsub[:, d].rearrange("p b (j t) -> p (b j) t", t=SUB)[:, :, seen],
                                        key.broadcast_to([P, 2 * NSUB, seen.stop - seen.start]), ALU.add).then_inc(arg_ready, 1)

        @block.vector
        def _(dve):
            turn = make_turn()
            steps = [0]
            tt, ts, stt = nc.vector.tensor_tensor, nc.vector.tensor_scalar, nc.vector.scalar_tensor_tensor

            def then(ins):
                steps[0] += 1
                ins.then_inc(dve_step, 1)
                dve.wait_ge(dve_step, steps[0])

            def mod_sum(g):
                n = mod_at[g]
                w, acc = R8[slot_of_chunk(n)], mod_acc(g)
                dve.wait_ge(full[slot_of_chunk(n)], 16 * (n // NSLOT + 1))
                then(ts(acc, w[:, 0, :], csil[:, 0, 0:1], None, ALU.mult))
                for k in range(1, KT):
                    last = stt(acc, w[:, k, :], csil[:, k, 0:1], acc, ALU.mult, ALU.add)
                    if k < KT - 1:
                        then(last)
                last.then_inc(mod_rows, 1)

            def mod_add(g):
                l, n = divmod(g, 12)
                o, width = mod_columns(g)
                v = V_ADA[l] + 4 * n
                dve.wait_ge(mod_cols, g + 1)
                if width == 2:
                    then(tt(modc[:, 4 * n:4 * n + 4], o[:, :, 1], vec[:, v:v + 4], ALU.add))
                tt(mod[:, l, 4 * n:4 * n + 4], o[:, :, 0], vec[:, v:v + 4], ALU.add).then_inc(mod_ready, 1)
                dve.wait_ge(mod_ready, g + 1)
                if n == 3:
                    then(stt(gain1[:, l, :], mod[:, l, SC1:SC1 + KT], 1.0, vec[:, V_MIX[l]:V_MIX[l] + KT],
                             ALU.add, ALU.mult))
                    if l == 2:
                        then(stt(gainc[:, :], modc[:, SC1:SC1 + KT], 1.0, vec[:, V_NORM1:V_NORM1 + KT],
                                 ALU.add, ALU.mult))
                if n == 9:
                    then(stt(gain2[:, l, :], mod[:, l, SC2:SC2 + KT], 1.0, vec[:, V_FFN[l]:V_FFN[l] + KT],
                             ALU.add, ALU.mult))

            def norm(src, at, gain, shift):
                dve.wait_ge(rt_ready, turn(rt_ready))
                then(nc.vector.reciprocal(rstd[:, :], rt[:, :]))
                xn = sq[:, :].rearrange("p (k t) -> p k t", k=KT)
                then(tt(xn, src, rstd[:, :].unsqueeze(1).broadcast_to([P, KT, S]), ALU.mult))
                for k in range(KT):
                    last = ts(hh[:, k, at:at + S], xn[:, k, :], gain[:, k:k + 1], shift[:, k:k + 1], ALU.mult, ALU.add)
                last.then_inc(h_ready, 1)

            def head_norms(rows):
                dve.wait_ge(rt_ready, turn(rt_ready))
                nc.vector.reciprocal(rstd[0:rows, :], rt[0:rows, :]).then_inc(rs_ready, 1)

            def qkv(l):
                for n, g in enumerate(MOD_QK[l]):
                    if g in MOD_ON_DVE:
                        mod_sum(g)
                    if n >= 1:
                        mod_add(g - 1)
                mod_add(MOD_QK[l][-1])
                head_norms(32)
                flips = l + 1
                for g in range(4):
                    for n in range(flips * g, flips * (g + 1)):
                        dve.wait_ge(flip_ps, turn(flip_ps))
                        nc.vector.tensor_copy(bias[:, 2 * n:2 * n + 2, :],
                                              b[6 + n % 2].rearrange("p (h j) -> p h j", h=2)).then_inc(bias_ready, 1)
                    for sl in range(4 * g, 4 * g + 4):
                        dve.wait_ge(bc_ps, turn(bc_ps))
                        gain = qscale[:, l:l + 1] if sl < 8 else vec[:, GAIN_AK + 2 * l:GAIN_AK + 2 * l + 1]
                        stt(raw[:, sl, :], raw[:, sl, :], gain, b[2 + sl % 4][:, 0:S], ALU.mult, ALU.mult).then_inc(norm_ready, 1)
                dve.wait_ge(bias_ready, turn(bias_ready, 4 * flips))
                then(nc.vector.memset(bias[0:64, 0:8 * flips, P + 64:S], NEG))

            def attention(l):
                def maxima(u):
                    h, qt = divmod(u, TT)
                    wide, n = P * (qt + 1), u % 4
                    if u >= 4:
                        dve.wait_ge(turn_ps, 16 * l + u - 3)
                    dve.wait_ge(scores_ps, turn(scores_ps, 2))
                    by_key = slice(P - qt * P, S)
                    if l == 0:
                        bb = bias[:, h, by_key].unsqueeze(1).broadcast_to([P, 2, wide])
                    else:
                        bb = bias[:, 2 * h:2 * h + 2, by_key]
                    tt(s_sb[:, n, :, 0:wide], score_bank(u)[:, :, 0:wide], bb, ALU.add).then_inc(s_added, 1)
                    dve.wait_ge(s_added, turn(s_added))
                    then(nc.vector.tensor_reduce(stat[:, n, 4:6], s_sb[:, n, :, 0:wide], AX.X, ALU.max))
                    ts(stat[:, n, 0:2], stat[:, n, 4:6], -1.0, None, ALU.mult).then_inc(max_ready, 1)

                def weights(u):
                    wide, n = P * (u % TT + 1), u % 4
                    dve.wait_ge(exp_ready, turn(exp_ready))
                    then(nc.vector.reciprocal(stat[:, n, 6:8], stat[:, n, 2:4]))
                    p0, p1 = s_sb[:, n, 0, 0:wide], s_sb[:, n, 1, 0:wide]
                    if l == 0:
                        then(tt(stat[:, n, 7:8], stat[:, n, 7:8], nlam[:, :], ALU.mult))
                        then(ts(p0, p0, stat[:, n, 6:7], None, ALU.mult))
                        last = stt(p0, p1, stat[:, n, 7:8], p0, ALU.mult, ALU.add)
                    else:
                        ts(p0, p0, stat[:, n, 6:7], None, ALU.mult)
                        last = ts(p1, p1, stat[:, n, 7:8], None, ALU.mult)
                    last.then_inc(prob_ready, 1)

                maxima(0)
                maxima(1)
                for u in range(16):
                    weights(u)
                    if u < 14:
                        maxima(u + 2)
                    if u % 2 == 1 and u >= 3:
                        mod_add(MOD_ATTN[l][u // 2 - 1])
                mod_add(MOD_ATTN[l][-1])
                if l == 0:
                    head_norms(16)
                    for h in range(8):
                        dve.wait_ge(bc_ps, turn(bc_ps))
                        stt(oT[:, h, :], oT[:, h, :], qscale[:, 3:4], b[4 + h % 2][:, 0:S],
                            ALU.mult, ALU.mult).then_inc(norm_ready, 1)

            def add_out(l):
                for c in range(KT):
                    dve.wait_ge(out_proj, turn(out_proj))
                    stt(xT[:, c, :], b[2 + c % 4][:, 0:S], mod[:, l, G1 + c:G1 + c + 1], xT[:, c, :],
                        ALU.mult, ALU.add).then_inc(x_attn, 1)

            def pick_group(scores8, best, index, number):
                for t in range(TT):
                    then(nc.vector.max(best[:, t, :], scores8[:, t, :]))
                    then(nc.vector.max_index(index[:, t, :], best[:, t, :], scores8[:, t, :]))
                then(nc.vector.tensor_copy(number, index[:, :, 0:2]))

            def choose(l, sel, number):
                E = EXPERTS[l]
                r = route_work(l)
                io = K(C_IOTA, GROUPS).unsqueeze(1).broadcast_to([P, TT, GROUPS])
                then(tt(r["gmask"], io, number[:, :, 0:1].broadcast_to([P, TT, GROUPS]), ALU.is_equal))
                wide = r["gmask"].unsqueeze(3).broadcast_to([P, TT, GROUPS, E // GROUPS])
                by_group = lambda a: a.rearrange("p t (g e) -> p t g e", g=GROUPS)
                then(nc.vector.tensor_copy(by_group(r["masked"]), wide))
                then(ts(r["fill"], r["masked"], -1.0, -NEG, ALU.add, ALU.mult))
                then(tt(r["masked"], r["masked"], sel, ALU.mult))
                then(tt(r["masked"], r["masked"], r["fill"], ALU.add))
                for t in range(TT):
                    then(nc.vector.max(r["best"][:, t, :], r["masked"][:, t, :]))
                    then(nc.vector.max_index(r["index"][:, t, :], r["best"][:, t, :], r["masked"][:, t, :]))
                then(nc.vector.tensor_copy(r["number"], r["index"][:, :, 0:2]))
                ie = K(C_IOTA, E).unsqueeze(1).broadcast_to([P, TT, E])
                for n in range(2):
                    then(tt(r["hot"][n], ie, r["number"][:, :, n:n + 1].broadcast_to([P, TT, E]), ALU.is_equal))
                tt(route_mask(l), r["hot"][0], r["hot"][1], ALU.add).then_inc(mask_ready, 1)
                dve.wait_ge(mask_ready, turn(mask_ready))

            def route(l):
                E, M = EXPERTS[l], MOE[l]
                r = route_work(l)
                if l < 2:
                    dve.wait_ge(score_ready, turn(score_ready))
                    score = route_score(l)
                    then(tt(r["sel"], score, rb[:, :].unsqueeze(1).broadcast_to([P, TT, 16]), ALU.add))
                    g = r["sel"].rearrange("p t (g e) -> p (t g) e", g=GROUPS)
                    s6 = r["sums"]
                    for first, n, at in ((0, 3, 0), (1, 2, 3), (2, 1, 5)):
                        then(tt(s6[:, :, at:at + n], g[:, :, first + 1:4],
                                g[:, :, first:first + 1].broadcast_to([P, TT * GROUPS, n]), ALU.add))
                    then(nc.vector.memset(r["g8"], FAR))
                    then(nc.vector.tensor_reduce(r["g8"][:, :, 0:GROUPS], s6.rearrange("p (t g) s -> p t g s", t=TT),
                                                 AX.X, ALU.max))
                    pick_group(r["g8"], r["best"], r["index"], r["number"])
                    choose(l, r["sel"], r["number"])
                    mask = route_mask(l)
                    gate = r["gate"]
                    then(tt(gate, mask, score, ALU.mult))
                    then(nc.vector.tensor_reduce(r["total"], gate, AX.X, ALU.add))
                    then(nc.vector.reciprocal(r["inv"], r["total"]))
                    then(tt(gate, gate, r["inv"].unsqueeze(2).broadcast_to([P, TT, E]), ALU.mult))
                else:
                    dve.wait_ge(logits_ps, 3)
                    lg = r["logits"]
                    then(tt(lg, b[6][:, 0:TT * 36].rearrange("p (t e) -> p t e", t=TT),
                            rb2[:, :].unsqueeze(1).broadcast_to([P, TT, 36]), ALU.add))
                    then(nc.vector.memset(r["g8"], FAR))
                    then(nc.vector.tensor_copy(r["g8"][:, :, 0:GROUPS], lg[:, :, 0:GROUPS]))
                    pick_group(r["g8"], r["best"], r["index"], r["number"])
                    then(tt(route_gap[:, :, 0:GROUPS], lg[:, :, 0:GROUPS],
                            r["best"][:, :, 0:1].broadcast_to([P, TT, GROUPS]), ALU.subtract))
                    choose(l, lg[:, :, GROUPS:36], r["number"])
                    tt(route_gap[:, :, 4:5], r["best"][:, :, 1:2], r["best"][:, :, 0:1], ALU.subtract).then_inc(gap_ready, 1)
                    dve.wait_ge(gap_exp, 1)
                    then(nc.vector.tensor_reduce(r["total"], route_gap_exp[:, :, 0:GROUPS], AX.X, ALU.add))
                    e1 = route_gap_exp[:, :, 4:5]
                    total = r["total"].unsqueeze(2)
                    then(stt(total, e1, 1.0, total, ALU.add, ALU.mult))
                    then(nc.vector.reciprocal(r["inv"], r["total"]))
                    then(tt(r["inv1"].unsqueeze(2), r["inv"].unsqueeze(2), e1, ALU.mult))
                    gate = r["gate"]
                    then(tt(gate, r["hot"][0], r["inv"].unsqueeze(2).broadcast_to([P, TT, E]), ALU.mult))
                    then(tt(r["hot"][1], r["hot"][1], r["inv1"].unsqueeze(2).broadcast_to([P, TT, E]), ALU.mult))
                    then(tt(gate, gate, r["hot"][1], ALU.add))
                dve.wait_ge(rank_ps, turn(rank_ps))
                last = ROUNDS * E
                then(stt(r["masked"], b[7][:, 0:TT * E].rearrange("p (t e) -> p t e", t=TT), 1.0, route_mask(l),
                         ALU.add, ALU.mult))
                nc.vector.memset(slot_of[:, :, last:last + 2], -1.0)
                nc.vector.memset(gate_of[:, :, last:last + 2], 0.0).then_inc(M["added"], 2)
                for n in range(ROUNDS):
                    ts(slot_of[:, :, n * E:(n + 1) * E], r["masked"], -1.0 - SLOTS * n, None, ALU.add)
                    then(nc.vector.tensor_copy(gate_of[:, :, n * E:(n + 1) * E], gate))
                then(nc.vector.tensor_reduce(r["most"], b[7][:, TT * E:(TT + 1) * E], AX.X, ALU.max))
                then(ts(r["steps"], K(C_IOTA + 1, ROUNDS - 1), float(SLOTS), None, ALU.mult))
                then(ts(r["steps"], r["steps"], r["most"], None, ALU.is_lt))
                then(nc.vector.tensor_reduce(r["most"], r["steps"], AX.X, ALU.add))
                then(nc.vector.tensor_copy(nit[:, 1:2], r["most"]))
                ts(nit[:, 0:1], r["most"], E / 2.0, E / 2.0, ALU.mult, ALU.add).then_inc(n_ready, 1)

            def experts(l):
                M = MOE[l]
                iota = K(C_IOTA, SLOTS).unsqueeze(1).unsqueeze(1).broadcast_to([P, TT, 2, SLOTS])
                as4 = lambda a: a.rearrange("p t (a s) -> p t a s", a=2)

                def pick_pair(at):
                    tt(as4(pick), iota, slot_of[:, :, at].unsqueeze(3).broadcast_to([P, TT, 2, SLOTS]),
                       ALU.is_equal).then_inc(M["pick_ready"], 1)

                def gate_pair(at):
                    tt(as4(pick_g), as4(pick), gate_of[:, :, at].unsqueeze(3).broadcast_to([P, TT, 2, SLOTS]),
                       ALU.mult).then_inc(M["pickg_ready"], 1)

                dve.wait_ge(n_ready, l + 1)
                n = dve.value_load(nit[0:1, 0:1], min_val=1, max_val=ROUNDS * EXPERTS[l] // 2)
                pick_pair(slice(0, 2))
                dve.wait_ge(M["pick_ready"], 1)
                gate_pair(slice(0, 2))
                second = lambda: nc.vector.tensor_copy(x_sel[:, 4:8, :], b[1].rearrange("p (k s) -> p k s", k=4))
                dve.wait_ge(M["gather_b"], 1)
                second().then_inc(M["sel_b"], 1)
                with dve.Fori(0, n) as i:
                    nxt = bass.ds(2 * i + 2, 2)
                    dve.wait_ge(M["gather_b"], i + 1)
                    dve.wait_ge(M["pickg_ready"], i + 1)
                    pick_pair(nxt)
                    dve.wait_ge(M["silu_ready"], i + 1)
                    dve.wait_ge(M["up_ps"], i + 1)
                    tt(hid, gate_act, b[3], ALU.mult).then_inc(M["hid_ready"], 1)
                    dve.wait_ge(M["gate_turned"], i + 1)
                    dve.wait_ge(M["pick_ready"], i + 2)
                    gate_pair(nxt)
                    dve.wait_ge(M["gather_b"], i + 2)
                    second().then_inc(M["sel_b"], 1)
                    dve.wait_ge(M["down_b"], i + 1)
                    nc.vector.tensor_copy(y_sel[:, 512:1024], b[6]).then_inc(M["y_b"], 1)
                    for r in range(4):
                        dve.wait_ge(M["comb_ps"], 4 * i + r + 1)
                        for k in range(2 * r, 2 * r + 2):
                            last = stt(xT[:, k, :], sums[r % 2][:, k % 2 * S:(k % 2 + 1) * S],
                                       mod[:, l, G2 + k:G2 + k + 1], xT[:, k, :], ALU.mult, ALU.add)
                        last.then_inc(M["added"], 1)

            def hybrid():
                norm(xT[:, :, :], 0, gain1[:, 2, :], mod[:, 2, SH1:SH1 + KT])
                norm(cT, S, gainc, modc[:, SH1:SH1 + KT])
                dve.wait_ge(ln_ready, 1)
                dve.wait_ge(in_proj, parts_to("g1"))
                l5 = sq[:, :].rearrange("p (n h t) -> p n h t", n=4, h=2)
                z5 = z.rearrange("p a b (h t) -> p (a b) h t", h=2)
                for h in range(2):
                    then(stt(nlk[:, h].rearrange("p a b t -> p (a b) t"), z5[:, :, h], 0.0, l5[:, :, h], ALU.max, ALU.add))
                z8, l8 = z.rearrange("p a b t -> p (a b t)"), sq[:, :]
                then(stt(z8, z8, 0.0, l8, ALU.min, ALU.subtract))
                one = cst[:, C_ONE:C_ONE + 1].broadcast_to([P, S])
                then(nc.vector.memset(bpad[:, 0, :, 0:1], 0.0))
                then(nc.vector.memset(bpad[:, 1, :, S:S + 1], 0.0))
                then(nc.vector.memset(epad[:, 0, :, S - 1:S], 0.0))
                then(nc.vector.memset(epad[:, 1, :, 0:1], 0.0))
                for hp in range(2):
                    scan = nc.vector.tensor_tensor_scan
                    then(scan(bpad[:, 0, hp, 1:S + 1], one, z[:, 0, hp, 0:S], 0.0, ALU.mult, ALU.add))
                    then(scan(bpad[:, 1, hp, S - 1::-1], one, z[:, 1, hp, S - 1::-1], 0.0, ALU.mult, ALU.add))
                    then(scan(epad[:, 0, hp, S - 2::-1], one[:, 1:S], z[:, 0, hp, 2 * S - 1:S:-1], 0.0, ALU.mult, ALU.add))
                    then(scan(epad[:, 1, hp, 1:S], one[:, 1:S], z[:, 1, hp, S:2 * S - 1], 0.0, ALU.mult, ALU.add))
                for d in range(2):
                    bx = bpad[:, d, :, 1:S + 1] if d == 0 else bpad[:, d, :, 0:S]
                    r0_ = ref_col(d, 0)
                    ref = bpad[:, d, :, r0_:r0_ + 15 * SUB + 1:SUB].unsqueeze(3).broadcast_to([P, 2, NSUB, SUB])
                    sub = lambda a: a.rearrange("p b (j t) -> p b j t", t=SUB)
                    then(tt(sub(bsub[:, d]), sub(bx), ref, ALU.subtract))
                    then(stt(lks[:, d], nlk[:, 0, d], -1.0, bsub[:, d], ALU.mult, ALU.subtract))
                    end = SUB - r0_
                    far = bpad[:, d, :, end:end + 15 * SUB + 1:SUB]
                    then(tt(step[:, d], far, bpad[:, d, :, r0_:r0_ + 15 * SUB + 1:SUB], ALU.subtract))
                    then(tt(sub(LK[:, d, :, 0:S]), sub(lks[:, d]), step[:, d].unsqueeze(3).broadcast_to([P, 2, NSUB, SUB]),
                            ALU.add))
                    last = tt(LK[:, d, :, S:2 * S], epad[:, d], nlk[:, 1, d], ALU.subtract)
                    if d == 0:
                        then(last)
                    else:
                        last.then_inc(log_ready, 1)
                dve.wait_ge(in_ready, parts_to("vm1"))
                by_head = lambda a: a.rearrange("p t (h d) -> p (t h) d", d=HEAD)
                then(tt(vm_sq, vm, vm, ALU.mult))
                nc.vector.tensor_reduce(vm_stat[:, 0:8], by_head(vm_sq), AX.X, ALU.add).then_inc(vm_sums, 1)
                dve.wait_ge(vm_rt, 1)
                then(nc.vector.reciprocal(vm_stat[:, 16:24], vm_stat[:, 8:16]))
                tt(by_head(vm), by_head(vm), vm_stat[:, 16:24].unsqueeze(2).broadcast_to([P, 8, HEAD]),
                   ALU.mult).then_inc(vm_ready, 1)
                dve.wait_ge(mix_ps, 1)
                tt(ymix[:, 0:2, :], uT, b[5].rearrange("p (j t) -> p j t", j=2), ALU.mult).then_inc(ymix_ready, 1)
                dve.wait_ge(rt_ready, turn(rt_ready, 2))
                then(nc.vector.reciprocal(sq[0:32, 6 * S:8 * S], sq[0:32, 6 * S:8 * S]))
                nc.vector.reciprocal(rstd[0:32, :], rt[0:32, :]).then_inc(rs_ready, 1)
                two = lambda a: a.rearrange("p (j t) -> p j t", j=2)
                for g in range(3):
                    dve.wait_ge(bc_ps, turn(bc_ps))
                    if g < 2:
                        last = stt(q2[:, 2 * g:2 * g + 2, :], q2[:, 2 * g:2 * g + 2, :], qscale[:, 2:3], two(b[g]),
                                   ALU.mult, ALU.mult)
                    else:
                        last = stt(k2, k2, vec[:, GAIN_K2:GAIN_K2 + 1], b[2], ALU.mult, ALU.mult)
                    last.then_inc(norm_ready, 1)
                dve.wait_ge(norm_ready, turn(norm_ready, 16 + 8 + 16 + 3))
                for g in range(3):
                    dve.wait_ge(bc_ps, turn(bc_ps))
                    n = 2 if g < 2 else 1
                    a = q2[:, 2 * g:2 * g + 2, :] if g < 2 else k2[:, 0:S].unsqueeze(1)
                    rot = b[g][:, 0:n * S].rearrange("p (j t) -> p j t", j=n)
                    tmp = sq[:, 0:n * S].rearrange("p (j t) -> p j t", j=n)
                    table = lambda at: K(at, S).unsqueeze(1).broadcast_to([P, n, S])
                    then(tt(tmp, rot, table(C_SIN), ALU.mult))
                    then(tt(a, a, table(C_COS), ALU.mult))
                    tt(a, a, tmp, ALU.add).then_inc(norm_ready, 1)
                    dve.wait_ge(norm_ready, turn(norm_ready))

                for g in range(2):
                    dve.wait_ge(bc_ps, turn(bc_ps))
                    nc.vector.tensor_copy(kd[:, g, :], b[2 + g]).then_inc(norm_ready, 1)

                def maxima(u):
                    dve.wait_ge(scores_ps, turn(scores_ps))
                    then(nc.vector.tensor_reduce(stat[:, u % 4, 4:5], score2_bank(u), AX.X, ALU.max))
                    ts(stat[:, u % 4, 0:1], stat[:, u % 4, 4:5], -1.0, None, ALU.mult).then_inc(max_ready, 1)

                maxima(0)
                maxima(1)
                for u in range(16):
                    dve.wait_ge(exp_ready, turn(exp_ready))
                    then(nc.vector.reciprocal(stat[:, u % 4, 6:7], stat[:, u % 4, 2:3]))
                    ts(p2[:, u % 4, :], p2[:, u % 4, :], stat[:, u % 4, 6:7], None, ALU.mult).then_inc(prob_ready, 1)
                    if u < 14:
                        maxima(u + 2)
                dve.wait_ge(decays_ready, 2)
                then(tt(qq, qq, qh.unsqueeze(1).broadcast_to([P, 2, 2, S]), ALU.mult))

                def advance(d, n):
                    j = sub_chunk(d, n)
                    dve.wait_ge(update_ps, 2 if d == 0 else 3 if j >= NSUB // 2 else 4)
                    if n >= 1:
                        dve.wait_ge(state_ready, d * (NSUB - 1) + n + 1)
                    for hp in range(2):
                        at = j % (NSUB // 2) * HEAD
                        last = stt(state[:, d, hp, n + 1, :], state[:, d, hp, n, :], decay[:, d, hp, j:j + 1],
                                   update_bank(d, hp, j // (NSUB // 2))[:, at:at + HEAD], ALU.mult, ALU.add)
                    last.then_inc(state_ready, 1)

                dve.wait_ge(in_proj, len(PARTS))
                dve.wait_ge(keys_turned, 5)
                nc.vector.tensor_copy(state[:, :, :, 0, :], b[5][:, 0:4 * HEAD].rearrange("p (d h v) -> p d h v", d=2, h=2)
                                      ).then_inc(state_ready, 1)
                dve.wait_ge(state_ready, 1)
                for q in range(2 * SUB):
                    d, i = divmod(q, SUB)
                    dve.wait_ge(prod_exp, q + 1)
                    pr = prod_of(q)
                    tt(pr, pr, qh.rearrange("p b (j t) -> p (b j) t", t=SUB)[:, :, seen_by(d, i)],
                       ALU.mult).then_inc(prod_ready, 1)
                    if i < NSUB - 1:
                        advance(d, i)
                dve.wait_ge(sc_ready, 1)
                for w, (hp, d) in enumerate(UNITS):
                    if w >= 1:
                        dve.wait_ge(dm_ps, w)
                    own = sc.rearrange("p a b -> p (a b)")[:, (d * 2 + hp) * 64:(d * 2 + hp + 1) * 64]
                    own = own.rearrange("p (n s) -> p n s", n=4).unsqueeze(2).broadcast_to([P, 4, P // SUB, SUB])
                    mask = K(C_DIAG + P * d).rearrange("p (j s) -> p j s", s=SUB).unsqueeze(1).broadcast_to([P, 4, P // SUB, SUB])
                    tt(dm.rearrange("p n (j s) -> p n j s", s=SUB), own, mask, ALU.mult).then_inc(dm_ready, 1)
                dve.wait_ge(out_ps, 3)
                then(tt(o2, o2, b[3].rearrange("p (j t) -> p j t", j=2), ALU.add))
                tt(o2, o2, b[7].rearrange("p (j t) -> p j t", j=2), ALU.add).then_inc(o2_ready, 1)
                head_norms(32)
                dve.wait_ge(bc_ps, turn(bc_ps))
                then(stt(o2, o2, vec[:, GAIN_O2:GAIN_O2 + 1], b[5].rearrange("p (j t) -> p j t", j=2), ALU.mult, ALU.mult))
                tt(ymix[:, 6:8, :], o2, gs, ALU.mult).then_inc(ymix_ready, 1)

            nc.vector.memset(csil[:, :, :], 0.0)
            nc.vector.memset(eps[:, :], EPS).then_inc(eps_ready, 1)
            dve.wait_ge(const_in, 16 * len(const_loads))
            lam4 = lamrow.rearrange("p (n two d) -> p n two d", n=2, two=2)
            then(tt(lamtmp[:, 0:2 * HEAD].rearrange("p (n d) -> p n d", n=2), lam4[:, :, 0, :], lam4[:, :, 1, :], ALU.mult))
            nc.vector.tensor_reduce(lamtmp[:, 128:130], lamtmp[:, 0:2 * HEAD].rearrange("p (n d) -> p n d", n=2),
                                    AX.X, ALU.add).then_inc(lam_step, 1)
            dve.wait_ge(vec_ps, 1)
            nc.vector.tensor_copy(vec[:, :], b[0][:, 0:N_VEC]).then_inc(vec_ready, 1)
            dve.wait_ge(lam_exp, 1)
            tt(lamtmp[:, 132:133], lamtmp[:, 131:132], lamtmp[:, 130:131], ALU.subtract).then_inc(lam_step, 1)
            dve.wait_ge(vec_ready, 1)
            for n, (g, f) in enumerate(((GAIN_AQ, HEAD ** -0.5), (GAIN_BQ, HEAD ** -0.5), (GAIN_Q2, HEAD ** -0.5),
                                        (GAIN_SUB, 1.0 - LAMBDA_INIT))):
                then(ts(qscale[:, n:n + 1], vec[:, g:g + 1], f, None, ALU.mult))
            dve.wait_ge(lam_bc, 1)
            ts(nlam[:, :], b[6][:, 0:1], -LAMBDA_INIT, None, ALU.add).then_inc(lam_step, 1)
            dve.wait_ge(lam_step, 3)
            dve.wait_ge(csil_ready, 1)
            for g in MOD_START:
                mod_add(g)
            for l in range(2):
                norm(xT[:, :, :], 0, gain1[:, l, :], mod[:, l, SH1:SH1 + KT])
                qkv(l)
                attention(l)
                add_out(l)
                norm(xT[:, :, :], 0, gain2[:, l, :], mod[:, l, SH2:SH2 + KT])
                route(l)
                experts(l)
            hybrid()
            add_out(2)
            norm(xT[:, :, :], 0, gain2[:, 2, :], mod[:, 2, SH2:SH2 + KT])
            route(2)
            experts(2)


_OUTS = [((1, S, D), "float32")]
_INS = ["x", "c", "ada_w", "ada_b", "norm_mix_g", "norm_ffn_g", "t5_bias", "a_w_qkv", "a_q_gain", "a_k_gain",
        "a_lambda", "a_subln_g", "a_w_o", "b_w_qkv", "b_q_gain", "b_k_gain", "b_rel_bias", "b_w_o", "router_w",
        "router_bias", "moe_w_gate", "moe_w_up", "moe_w_down", "c_2", "ctx_2", "c_ctx_2", "w_mod_2", "b_mod_2",
        "norm1_w_2", "w_in_2", "w_s_2", "b_s_2", "q_norm_w_2", "k_norm_w_2", "hgrn_lb_logits_2", "hgrn_norm_w_2",
        "w_out_2", "norm2_w_2", "w_grp_2", "b_grp_2", "w_exp_2", "b_exp_2", "w1_2", "w3_2", "w2_2"]


def kernel(**inputs):
    import concourse.bacc as bacc
    from concourse.bass_utils import run_bass_kernel_spmd

    nc = bacc.Bacc("TRN2", target_bir_lowering=False, num_devices=1)
    arrays, args = {}, []
    named = [(n, np.ascontiguousarray(inputs[n])) for n in _INS]
    named += list(zip(("const", "const2", "bucket"), constants()))
    for name, a in named:
        arrays[f"in_{name}_dram"] = a
        args.append(nc.dram_tensor(f"in_{name}_dram", a.shape, mybir.dt.from_np(a.dtype), kind="ExternalInput").ap())
    for i, (shape, dtype) in enumerate(_OUTS):
        args.append(nc.dram_tensor(f"out_{i}_dram", shape, mybir.dt.from_np(np.dtype(dtype)), kind="ExternalOutput").ap())
    program(nc, *args)
    r = run_bass_kernel_spmd(nc, [arrays], core_ids=[0])
    return r.results[0]["out_0_dram"]
```
